# Optimizing a Trainium2 kernel written in Bass

```python
import jax, jax.numpy as jnp
from jax import lax
import numpy as np

D_MODEL = 2048
BATCH = 1
SEQ = 256
DEPTH = 2

GRID_W = 64
CTX_LEN = 256

D_MLSTM = D_MODEL // 2
N_MLSTM_HEADS = 4
MLSTM_HEAD_DIM = D_MLSTM // N_MLSTM_HEADS
MLSTM_CHUNK = 64
QK_CONV = 3
N_DIR = 2
D_POOL = D_MODEL - D_MLSTM
POOL_WINDOWS = (2, 4, 8, 16)
N_POOL_GROUPS = len(POOL_WINDOWS)
POOL_GROUP_DIM = D_POOL // N_POOL_GROUPS
N_GATE = 2 * N_DIR * N_MLSTM_HEADS
N_IN_EVEN = 5 * D_MLSTM + N_GATE + 2 * D_POOL
EVEN_SPLITS = (D_MLSTM, 2 * D_MLSTM, 3 * D_MLSTM, 4 * D_MLSTM, 5 * D_MLSTM,
               5 * D_MLSTM + N_GATE, 5 * D_MLSTM + N_GATE + D_POOL)
D_SGU = D_MODEL
N_SGU_HEADS = 8
SGU_HEAD_DIM = D_SGU // N_SGU_HEADS
SGU_CHUNK = 128
N_IN_ODD = 3 * D_SGU

N_EVEN = (DEPTH + 1) // 2
N_ODD = DEPTH // 2
DEEPNORM_ALPHA = (2.0 * DEPTH) ** 0.25
DEEPNORM_BETA = (8.0 * DEPTH) ** -0.25
LN_EPS = 1e-5


def _normalize(x):
    xf = x.astype(jnp.float32)
    mu = xf.mean(-1, keepdims=True)
    var = jnp.square(xf - mu).mean(-1, keepdims=True)
    return (xf - mu) * lax.rsqrt(var + LN_EPS)

def layer_norm(x, g, b):
    return (_normalize(x) * g + b).astype(x.dtype)

def ada_params(cond, w, b):
    mod = jax.nn.silu(cond) @ w + b
    return jnp.split(mod, 3, axis=-1)

def dwconv_centered(x, w):
    k, ch = w.shape
    return lax.conv_general_dilated(x, w[:, None, :].astype(x.dtype), window_strides=(1,),
                                    padding=[(k // 2, k // 2)],
                                    dimension_numbers=('NWC', 'WIO', 'NWC'),
                                    feature_group_count=ch)

def mlstm_scan(q, k, v, log_i, log_f, state):
    bsz, nh, seqlen, dh = q.shape
    nc = seqlen // MLSTM_CHUNK

    def to_chunks(a):
        a = a.astype(jnp.float32).reshape(bsz, nh, nc, MLSTM_CHUNK, *a.shape[3:])
        return jnp.moveaxis(a, 2, 0)

    lower = jnp.tril(jnp.ones((MLSTM_CHUNK, MLSTM_CHUNK), bool))

    def step(carry, inp):
        cmat, nvec, m = carry
        qc, kc, vc, ic, fc = inp
        b = jnp.cumsum(fc, axis=-1)
        d = b[..., :, None] - b[..., None, :] + ic[..., None, :]
        d = jnp.where(lower, d, -jnp.inf)
        inter = b + m[..., None]
        m_t = jnp.maximum(d.max(-1), inter)
        w_intra = jnp.exp(d - m_t[..., None])
        w_inter = jnp.exp(inter - m_t)
        s = jnp.einsum('bhtd,bhsd->bhts', qc, kc) * w_intra
        num = (jnp.einsum('bhts,bhsd->bhtd', s, vc)
               + w_inter[..., None] * jnp.einsum('bhvk,bhtk->bhtv', cmat, qc))
        den = s.sum(-1) + w_inter * jnp.einsum('bhk,bhtk->bht', nvec, qc)
        h = num / jnp.maximum(jnp.abs(den), jnp.exp(-m_t))[..., None]
        b_last = b[..., -1]
        g = b_last[..., None] - b + ic
        m_new = jnp.maximum(b_last + m, g.max(-1))
        w_s = jnp.exp(g - m_new[..., None])
        decay = jnp.exp(b_last + m - m_new)
        c_new = decay[..., None, None] * cmat + jnp.einsum('bhs,bhsv,bhsk->bhvk', w_s, vc, kc)
        n_new = decay[..., None] * nvec + jnp.einsum('bhs,bhsk->bhk', w_s, kc)
        return (c_new, n_new, m_new), h

    xs = tuple(to_chunks(a) for a in (q, k, v, log_i, log_f))
    state, h = lax.scan(step, state, xs)
    h = jnp.moveaxis(h, 0, 2).reshape(bsz, nh, seqlen, dh)
    return h, state

def zero_mlstm_state(bsz):
    return (jnp.zeros((bsz, N_MLSTM_HEADS, MLSTM_HEAD_DIM, MLSTM_HEAD_DIM), jnp.float32),
            jnp.zeros((bsz, N_MLSTM_HEADS, MLSTM_HEAD_DIM), jnp.float32),
            jnp.zeros((bsz, N_MLSTM_HEADS), jnp.float32))

def even_proj(xm, w_in, conv_qk, b_igate, b_fgate):
    bsz, seqlen, _ = xm.shape
    proj = xm @ w_in
    q, k, v, o, z_m, gates, u_p, z_p = jnp.split(proj, EVEN_SPLITS, axis=-1)
    qk = jax.nn.silu(dwconv_centered(jnp.concatenate([q, k], -1), conv_qk))
    q, k = jnp.split(qk, 2, axis=-1)

    def heads(a):
        return a.reshape(bsz, seqlen, N_MLSTM_HEADS, MLSTM_HEAD_DIM).transpose(0, 2, 1, 3)

    q, k, v = heads(q), heads(k) * (MLSTM_HEAD_DIM ** -0.5), heads(v)
    gates = gates.astype(jnp.float32).reshape(bsz, seqlen, 2, N_DIR, N_MLSTM_HEADS)
    log_i = (gates[:, :, 0] + b_igate).transpose(2, 0, 3, 1)
    log_f = jax.nn.log_sigmoid(gates[:, :, 1] + b_fgate).transpose(2, 0, 3, 1)
    return q, k, v, o, z_m, log_i, log_f, u_p, z_p

def multiscale_pool(u, row_len):
    bsz, seqlen, _ = u.shape
    rows = seqlen // row_len
    ug = u.astype(jnp.float32).reshape(bsz, rows, row_len, N_POOL_GROUPS, POOL_GROUP_DIM)
    cs = jnp.pad(jnp.cumsum(ug, axis=2), ((0, 0), (0, 0), (1, 0), (0, 0), (0, 0)))
    pos = jnp.arange(row_len)
    outs = []
    for g, w in enumerate(POOL_WINDOWS):
        lo = jnp.maximum(pos - w // 2, 0)
        hi = jnp.minimum(pos + (w - 1 - w // 2), row_len - 1)
        csg = cs[:, :, :, g, :]
        s = jnp.take(csg, hi + 1, axis=2) - jnp.take(csg, lo, axis=2)
        outs.append(s / (hi - lo + 1).astype(jnp.float32)[:, None])
    pooled = jnp.stack(outs, axis=3)
    return (pooled - ug).reshape(bsz, seqlen, N_POOL_GROUPS, POOL_GROUP_DIM)

def even_out(h, o, z_m, u_p, z_p, row_len, mh_norm_g, pool_w, pool_scale):
    bsz, nh, seqlen, dh = h.shape
    h = jnp.moveaxis(h, 1, 2) * jax.nn.sigmoid(o.astype(jnp.float32)).reshape(bsz, seqlen, nh, dh)
    h = _normalize(h).reshape(bsz, seqlen, D_MLSTM) * mh_norm_g
    y_m = h * jax.nn.silu(z_m.astype(jnp.float32))
    r = multiscale_pool(u_p, row_len)
    y_p = jnp.einsum('blgc,gcd->blgd', r, pool_w.astype(jnp.float32)).reshape(bsz, seqlen, D_POOL)
    y_p = y_p * pool_scale * jax.nn.silu(z_p.astype(jnp.float32))
    return jnp.concatenate([y_m, y_p], axis=-1).astype(u_p.dtype)

def sgu_mixer(xm, w_in, ln_g, ln_b, w_sp, b_sp):
    bsz, seqlen, _ = xm.shape
    u, v, z = jnp.split(xm @ w_in, 3, axis=-1)
    v = layer_norm(v, ln_g, ln_b)
    nc = seqlen // SGU_CHUNK
    vh = v.reshape(bsz, nc, SGU_CHUNK, N_SGU_HEADS, SGU_HEAD_DIM)
    s = jnp.einsum('hts,bnshc->bnthc', w_sp, vh) + b_sp.T[None, None, :, :, None]
    return u * s.reshape(bsz, seqlen, D_SGU) * jax.nn.silu(z)

def first_inputs(seed: int = 0) -> dict:
    key = jax.random.key(seed)
    ks = jax.random.split(key, 24)

    def nrm(k, shape, s):
        return jax.random.normal(k, shape, jnp.float32) * s

    d = D_MODEL
    fgate_base = jnp.linspace(3.0, 6.0, N_MLSTM_HEADS, dtype=jnp.float32)
    return {
        "x": nrm(ks[0], (BATCH, SEQ, d), 1.0),
        "c": nrm(ks[1], (BATCH, d), 1.0),
        "ctx": nrm(ks[2], (BATCH, CTX_LEN, d), 1.0),
        "c_ctx": nrm(ks[3], (d,), 1.0),
        "ada_w": nrm(ks[4], (DEPTH, d, 3 * d), 0.5 * d ** -0.5),
        "ada_b": nrm(ks[5], (DEPTH, 3 * d), 0.02),
        "post_ln_g": 1.0 + nrm(ks[6], (DEPTH, d), 0.05),
        "post_ln_b": nrm(ks[7], (DEPTH, d), 0.02),
        "w_in_even": nrm(ks[8], (N_EVEN, d, N_IN_EVEN), d ** -0.5),
        "conv_qk": nrm(ks[9], (N_EVEN, QK_CONV, 2 * D_MLSTM), QK_CONV ** -0.5),
        "b_igate": nrm(ks[10], (N_EVEN, N_DIR, N_MLSTM_HEADS), 0.1),
        "b_fgate": fgate_base + nrm(ks[11], (N_EVEN, N_DIR, N_MLSTM_HEADS), 0.1),
        "mh_norm_g": 1.0 + nrm(ks[12], (N_EVEN, D_MLSTM), 0.05),
        "pool_w": nrm(ks[13], (N_EVEN, N_POOL_GROUPS, POOL_GROUP_DIM, POOL_GROUP_DIM), POOL_GROUP_DIM ** -0.5),
        "pool_scale": 1.0 + nrm(ks[14], (N_EVEN, D_POOL), 0.1),
        "w_out_even": nrm(ks[15], (N_EVEN, D_MLSTM + D_POOL, d), DEEPNORM_BETA * (D_MLSTM + D_POOL) ** -0.5),
        "w_in_odd": nrm(ks[16], (N_ODD, d, N_IN_ODD), d ** -0.5),
        "sgu_ln_g": 1.0 + nrm(ks[17], (N_ODD, D_SGU), 0.05),
        "sgu_ln_b": nrm(ks[18], (N_ODD, D_SGU), 0.02),
        "w_sp": nrm(ks[19], (N_ODD, N_SGU_HEADS, SGU_CHUNK, SGU_CHUNK), SGU_CHUNK ** -0.5),
        "b_sp": 1.0 + nrm(ks[20], (N_ODD, N_SGU_HEADS, SGU_CHUNK), 0.1),
        "w_out_odd": nrm(ks[21], (N_ODD, D_SGU, d), DEEPNORM_BETA * D_SGU ** -0.5),
    }

def first_block(x, c, ctx, c_ctx, ada_w, ada_b, post_ln_g, post_ln_b, w_in_even, conv_qk, b_igate,
              b_fgate, mh_norm_g, pool_w, pool_scale, w_out_even, w_in_odd, sgu_ln_g, sgu_ln_b,
              w_sp, b_sp, w_out_odd):
    x_lat, x_ctx = x, ctx
    bsz = x.shape[0]
    for layer in range(DEPTH):
        last = layer == DEPTH - 1
        j = layer // 2
        sh_l, sc_l, g_l = ada_params(c, ada_w[layer], ada_b[layer])
        sh_l, sc_l, g_l = sh_l[:, None], sc_l[:, None], g_l[:, None]
        sh_c, sc_c, g_c = ada_params(c_ctx, ada_w[layer], ada_b[layer])
        xm_l = x_lat * (1.0 + sc_l) + sh_l
        xm_c = x_ctx * (1.0 + sc_c) + sh_c
        if layer % 2 == 0:
            ql, kl, vl, ol, zml, lil, lfl, upl, zpl = even_proj(xm_l, w_in_even[j], conv_qk[j], b_igate[j], b_fgate[j])
            qc, kc, vc, oc, zmc, lic, lfc, upc, zpc = even_proj(xm_c, w_in_even[j], conv_qk[j], b_igate[j], b_fgate[j])
            flip = lambda a: jnp.flip(a, axis=2)
            zero = zero_mlstm_state(bsz)
            hc_f, st_f = mlstm_scan(qc, kc, vc, lic[0], lfc[0], zero)
            hl_f, _ = mlstm_scan(ql, kl, vl, lil[0], lfl[0], st_f)
            hc_b, st_b = mlstm_scan(flip(qc), flip(kc), flip(vc), flip(lic[1]), flip(lfc[1]), zero)
            hl_b, _ = mlstm_scan(flip(ql), flip(kl), flip(vl), flip(lil[1]), flip(lfl[1]), st_b)
            y_l = even_out(hl_f + flip(hl_b), ol, zml, upl, zpl, GRID_W, mh_norm_g[j], pool_w[j], pool_scale[j])
            x_lat_new = layer_norm(DEEPNORM_ALPHA * x_lat + g_l * (y_l @ w_out_even[j]), post_ln_g[layer], post_ln_b[layer])
            if not last:
                y_c = even_out(hc_f + flip(hc_b), oc, zmc, upc, zpc, x_ctx.shape[1], mh_norm_g[j], pool_w[j], pool_scale[j])
                x_ctx = layer_norm(DEEPNORM_ALPHA * x_ctx + g_c * (y_c @ w_out_even[j]), post_ln_g[layer], post_ln_b[layer])
            x_lat = x_lat_new
        else:
            y_l = sgu_mixer(xm_l, w_in_odd[j], sgu_ln_g[j], sgu_ln_b[j], w_sp[j], b_sp[j])
            x_lat = layer_norm(DEEPNORM_ALPHA * x_lat + g_l * (y_l @ w_out_odd[j]), post_ln_g[layer], post_ln_b[layer])
            if not last:
                y_c = sgu_mixer(xm_c, w_in_odd[j], sgu_ln_g[j], sgu_ln_b[j], w_sp[j], b_sp[j])
                x_ctx = layer_norm(DEEPNORM_ALPHA * x_ctx + g_c * (y_c @ w_out_odd[j]), post_ln_g[layer], post_ln_b[layer])
    return x_lat


DEPTH_2 = 1

N_MEM = 256
RET_HEADS = 8
RET_QK_DIM = 128
RET_V_DIM = 256
D_RET_QK = RET_HEADS * RET_QK_DIM
D_RET_V = RET_HEADS * RET_V_DIM
RET_CHUNK = 128
RNN_WIDTH = D_MODEL
RNN_BLOCKS = 16
RNN_BLOCK = RNN_WIDTH // RNN_BLOCKS
RNN_CONV = 4
RG_C = 8.0
XA_HEADS = 4
XA_HEAD_DIM = D_MODEL // XA_HEADS
D_FF = 5632
FFN_CONV = 3
ROPE_BASE = 10000.0
NORM_EPS = 1e-6
GN_EPS = 1e-5
MAX_POS_OFFSET = 1024


def rmsnorm(x, w):
    xf = x.astype(jnp.float32)
    y = xf * lax.rsqrt(jnp.mean(xf * xf, axis=-1, keepdims=True) + NORM_EPS)
    return (y * w.astype(jnp.float32)).astype(x.dtype)

def rotary(x, positions):
    d = x.shape[-1]
    half = d // 2
    inv_freq = ROPE_BASE ** (-jnp.arange(0, half, dtype=jnp.float32) * 2.0 / d)
    ang = positions.astype(jnp.float32)[..., None] * inv_freq
    cos = jnp.cos(ang)[:, :, None, :].astype(x.dtype)
    sin = jnp.sin(ang)[:, :, None, :].astype(x.dtype)
    x1, x2 = x[..., :half], x[..., half:]
    return jnp.concatenate([x1 * cos - x2 * sin, x2 * cos + x1 * sin], axis=-1)

def causal_dwconv(x, w, bias):
    k, c = w.shape
    y = lax.conv_general_dilated(
        x, w[:, None, :].astype(x.dtype), window_strides=(1,), padding=((k - 1, 0),),
        dimension_numbers=("NWC", "WIO", "NWC"), feature_group_count=c)
    return y + bias.astype(x.dtype)

def chunkwise_retention(q, k, v):
    dtype = v.dtype
    q = q.astype(jnp.float32)
    k = k.astype(jnp.float32)
    v = v.astype(jnp.float32)
    b, s, h, dk = q.shape
    dv = v.shape[-1]
    n = RET_CHUNK
    c = s // n
    log_gamma = jnp.log1p(-(2.0 ** (-5.0 - jnp.arange(h, dtype=jnp.float32))))
    idx = jnp.arange(n, dtype=jnp.float32)
    rel = idx[:, None] - idx[None, :]
    causal = rel >= 0
    d_intra = jnp.where(causal[None], jnp.exp(log_gamma[:, None, None] * jnp.where(causal, rel, 0.0)[None]), 0.0)
    q_decay = jnp.exp(log_gamma[None, :] * (idx[:, None] + 1.0))
    k_decay = jnp.exp(log_gamma[None, :] * (n - 1.0 - idx[:, None]))
    chunk_decay = jnp.exp(log_gamma * n)

    qc = q.reshape(b, c, n, h, dk)
    kc = k.reshape(b, c, n, h, dk)
    vc = v.reshape(b, c, n, h, dv)
    scores = jnp.einsum("bcnhd,bcmhd->bchnm", qc, kc) * d_intra
    inner = jnp.einsum("bchnm,bcmhe->bcnhe", scores, vc)
    kv = jnp.einsum("bcmhd,bcmhe->bchde", kc * k_decay[None, None, :, :, None], vc)

    def step(state, kv_c):
        return state * chunk_decay[None, :, None, None] + kv_c, state

    init = jnp.zeros((b, h, dk, dv), jnp.float32)
    _, prev = lax.scan(step, init, jnp.moveaxis(kv, 1, 0))
    prev = jnp.moveaxis(prev, 0, 1)
    cross = jnp.einsum("bcnhd,bchde->bcnhe", qc * q_decay[None, None, :, :, None], prev)
    return (inner + cross).reshape(b, s, h, dv).astype(dtype)

def head_groupnorm(x, w):
    xf = x.astype(jnp.float32)
    mu = jnp.mean(xf, axis=-1, keepdims=True)
    xc = xf - mu
    var = jnp.mean(xc * xc, axis=-1, keepdims=True)
    y = xc * lax.rsqrt(var + GN_EPS) * w.astype(jnp.float32).reshape(x.shape[2], x.shape[3])
    return y.astype(x.dtype)

def rg_lru(xr, w_a, b_a, w_x, b_x, lam):
    b, s, w = xr.shape
    xb = xr.reshape(b, s, RNN_BLOCKS, RNN_BLOCK)
    gate_r = jax.nn.sigmoid(jnp.einsum("bsgi,gij->bsgj", xb, w_a).reshape(b, s, w) + b_a)
    gate_i = jax.nn.sigmoid(jnp.einsum("bsgi,gij->bsgj", xb, w_x).reshape(b, s, w) + b_x)
    log_a = -RG_C * gate_r.astype(jnp.float32) * jax.nn.softplus(-lam.astype(jnp.float32))
    a = jnp.exp(log_a)
    u = jnp.sqrt(-jnp.expm1(2.0 * log_a)) * (gate_i * xr).astype(jnp.float32)

    def combine(left, right):
        a_l, b_l = left
        a_r, b_r = right
        return a_l * a_r, a_r * b_l + b_r

    _, hseq = lax.associative_scan(combine, (a, u), axis=1)
    return hseq.astype(xr.dtype)

def memory_cross_attention(hn, mem_n, w_q, w_k, w_v, w_o):
    b, s, _ = hn.shape
    m = mem_n.shape[1]
    q = (hn @ w_q).reshape(b, s, XA_HEADS, XA_HEAD_DIM)
    k = (mem_n @ w_k).reshape(b, m, XA_HEADS, XA_HEAD_DIM)
    v = (mem_n @ w_v).reshape(b, m, XA_HEADS, XA_HEAD_DIM)
    logits = jnp.einsum("bshd,bmhd->bhsm", q, k).astype(jnp.float32) * (XA_HEAD_DIM ** -0.5)
    p = jax.nn.softmax(logits, axis=-1).astype(v.dtype)
    o = jnp.einsum("bhsm,bmhd->bshd", p, v).reshape(b, s, D_MODEL)
    return o @ w_o

def conv_gated_ffn(hn, w_up, conv_w, conv_b, w_down):
    up = causal_dwconv(hn @ w_up, conv_w, conv_b)
    gate, val = jnp.split(up, 2, axis=-1)
    return (jax.nn.silu(gate) * val) @ w_down

def second_inputs(seed: int = 0) -> dict:
    key = jax.random.key(seed)
    ks = jax.random.split(key, 32)
    f32 = jnp.float32
    d_in = 2 * D_RET_QK + 2 * D_RET_V + 2 * RNN_WIDTH + 2 * D_MODEL

    def dense(k, shape, fan_in, scale=1.0):
        return jax.random.normal(k, shape, f32) * (scale * fan_in ** -0.5)

    def gain(k, shape):
        return 1.0 + 0.02 * jax.random.normal(k, shape, f32)

    def bias(k, shape):
        return 0.01 * jax.random.normal(k, shape, f32)

    u = jax.random.uniform(ks[10], (DEPTH_2, RNN_WIDTH), f32, 0.9, 0.999)
    start = jax.random.randint(ks[2], (BATCH, 1), 0, MAX_POS_OFFSET, dtype=jnp.int32)
    return {
        "x": jax.random.normal(ks[0], (BATCH, SEQ, D_MODEL), f32),
        "mem": jax.random.normal(ks[1], (BATCH, N_MEM, D_MODEL), f32),
        "positions": start + jnp.arange(SEQ, dtype=jnp.int32)[None, :],
        "norm_mix_w": gain(ks[3], (DEPTH_2, D_MODEL)),
        "w_in": dense(ks[4], (DEPTH_2, D_MODEL, d_in), D_MODEL),
        "ret_gn_w": gain(ks[5], (DEPTH_2, D_RET_V)),
        "rnn_conv_w": dense(ks[6], (DEPTH_2, RNN_CONV, RNN_WIDTH), RNN_CONV),
        "rnn_conv_b": bias(ks[7], (DEPTH_2, RNN_WIDTH)),
        "rg_w_a": dense(ks[8], (DEPTH_2, RNN_BLOCKS, RNN_BLOCK, RNN_BLOCK), RNN_BLOCK),
        "rg_b_a": bias(ks[9], (DEPTH_2, RNN_WIDTH)),
        "rg_w_x": dense(ks[11], (DEPTH_2, RNN_BLOCKS, RNN_BLOCK, RNN_BLOCK), RNN_BLOCK),
        "rg_b_x": bias(ks[12], (DEPTH_2, RNN_WIDTH)),
        "rg_lambda": jnp.log(u) - jnp.log1p(-u),
        "w_proj_ret": dense(ks[13], (DEPTH_2, D_RET_V, D_MODEL), D_RET_V),
        "w_proj_rnn": dense(ks[14], (DEPTH_2, RNN_WIDTH, D_MODEL), RNN_WIDTH),
        "w_mix_out": dense(ks[15], (DEPTH_2, D_MODEL, D_MODEL), D_MODEL, 0.5),
        "norm_xa_w": gain(ks[16], (DEPTH_2, D_MODEL)),
        "norm_mem_w": gain(ks[17], (DEPTH_2, D_MODEL)),
        "xa_w_q": dense(ks[18], (DEPTH_2, D_MODEL, D_MODEL), D_MODEL),
        "xa_w_k": dense(ks[19], (DEPTH_2, D_MODEL, D_MODEL), D_MODEL),
        "xa_w_v": dense(ks[20], (DEPTH_2, D_MODEL, D_MODEL), D_MODEL),
        "xa_w_o": dense(ks[21], (DEPTH_2, D_MODEL, D_MODEL), D_MODEL, 0.5),
        "norm_ffn_w": gain(ks[22], (DEPTH_2, D_MODEL)),
        "ffn_w_up": dense(ks[23], (DEPTH_2, D_MODEL, 2 * D_FF), D_MODEL),
        "ffn_conv_w": dense(ks[24], (DEPTH_2, FFN_CONV, 2 * D_FF), FFN_CONV),
        "ffn_conv_b": bias(ks[25], (DEPTH_2, 2 * D_FF)),
        "ffn_w_down": dense(ks[26], (DEPTH_2, D_FF, D_MODEL), D_FF, 0.5),
        "final_norm_w": gain(ks[27], (D_MODEL,)),
    }

def second_block(x, mem, positions, norm_mix_w, w_in, ret_gn_w, rnn_conv_w, rnn_conv_b,
              rg_w_a, rg_b_a, rg_w_x, rg_b_x, rg_lambda, w_proj_ret, w_proj_rnn, w_mix_out,
              norm_xa_w, norm_mem_w, xa_w_q, xa_w_k, xa_w_v, xa_w_o,
              norm_ffn_w, ffn_w_up, ffn_conv_w, ffn_conv_b, ffn_w_down, final_norm_w):
    b, s, _ = x.shape
    sizes = [D_RET_QK, D_RET_QK, D_RET_V, D_RET_V, RNN_WIDTH, RNN_WIDTH, D_MODEL, D_MODEL]
    offsets = [int(o) for o in np.cumsum(sizes)[:-1]]
    h = x
    for l in range(DEPTH_2):
        hn = rmsnorm(h, norm_mix_w[l])
        q, k, v, g_ret, xr, yr, g_a, g_b = jnp.split(hn @ w_in[l], offsets, axis=-1)
        q = rotary(q.reshape(b, s, RET_HEADS, RET_QK_DIM), positions)
        k = rotary(k.reshape(b, s, RET_HEADS, RET_QK_DIM), positions) * (RET_QK_DIM ** -0.5)
        v = v.reshape(b, s, RET_HEADS, RET_V_DIM)
        ret = head_groupnorm(chunkwise_retention(q, k, v), ret_gn_w[l]).reshape(b, s, D_RET_V)
        ret_out = jax.nn.silu(g_ret) * ret
        xr = causal_dwconv(xr, rnn_conv_w[l], rnn_conv_b[l])
        hr = rg_lru(xr, rg_w_a[l], rg_b_a[l], rg_w_x[l], rg_b_x[l], rg_lambda[l])
        rnn_out = jax.nn.gelu(yr) * hr
        merged = (jax.nn.sigmoid(g_a) * (ret_out @ w_proj_ret[l])
                  + jax.nn.sigmoid(g_b) * (rnn_out @ w_proj_rnn[l]))
        h = h + merged @ w_mix_out[l]
        hn = rmsnorm(h, norm_xa_w[l])
        mem_n = rmsnorm(mem, norm_mem_w[l])
        h = h + memory_cross_attention(hn, mem_n, xa_w_q[l], xa_w_k[l], xa_w_v[l], xa_w_o[l])
        hn = rmsnorm(h, norm_ffn_w[l])
        h = h + conv_gated_ffn(hn, ffn_w_up[l], ffn_conv_w[l], ffn_conv_b[l], ffn_w_down[l])
    return rmsnorm(h, final_norm_w)


def setup_inputs(seed=0):
    out = dict(first_inputs(seed))
    for name, value in second_inputs(seed + 1).items():
        if name != "x":
            out[name + "_2"] = value
    return out


def reference(
    x, c, ctx, c_ctx, ada_w, ada_b, post_ln_g, post_ln_b, w_in_even, conv_qk, b_igate, b_fgate,
    mh_norm_g, pool_w, pool_scale, w_out_even, w_in_odd, sgu_ln_g, sgu_ln_b, w_sp, b_sp,
    w_out_odd, mem_2, positions_2, norm_mix_w_2, w_in_2, ret_gn_w_2, rnn_conv_w_2, rnn_conv_b_2,
    rg_w_a_2, rg_b_a_2, rg_w_x_2, rg_b_x_2, rg_lambda_2, w_proj_ret_2, w_proj_rnn_2,
    w_mix_out_2, norm_xa_w_2, norm_mem_w_2, xa_w_q_2, xa_w_k_2, xa_w_v_2, xa_w_o_2,
    norm_ffn_w_2, ffn_w_up_2, ffn_conv_w_2, ffn_conv_b_2, ffn_w_down_2, final_norm_w_2,
):
    x = first_block(
        x, c, ctx, c_ctx, ada_w, ada_b, post_ln_g, post_ln_b, w_in_even, conv_qk, b_igate,
        b_fgate, mh_norm_g, pool_w, pool_scale, w_out_even, w_in_odd, sgu_ln_g, sgu_ln_b, w_sp,
        b_sp, w_out_odd,
    )
    return second_block(
        x, mem_2, positions_2, norm_mix_w_2, w_in_2, ret_gn_w_2, rnn_conv_w_2, rnn_conv_b_2,
        rg_w_a_2, rg_b_a_2, rg_w_x_2, rg_b_x_2, rg_lambda_2, w_proj_ret_2, w_proj_rnn_2,
        w_mix_out_2, norm_xa_w_2, norm_mem_w_2, xa_w_q_2, xa_w_k_2, xa_w_v_2, xa_w_o_2,
        norm_ffn_w_2, ffn_w_up_2, ffn_conv_w_2, ffn_conv_b_2, ffn_w_down_2, final_norm_w_2,
    )


_drawn_inputs = setup_inputs


def setup_inputs(seed=0):
    import zlib

    import numpy as np

    out = dict(_drawn_inputs(seed))
    spreads = {}
    factors = {'ctx': 5.785,
     'c_ctx': 3.019,
     'ada_b': 4.972,
     'conv_qk': 4.685,
     'b_igate': 200.0,
     'b_fgate': 2.854,
     'mh_norm_g': 8.0,
     'pool_scale': 8.0,
     'sgu_ln_g': 8.0,
     'sgu_ln_b': 8.0,
     'b_sp': 7.042,
     'norm_mix_w_2': 7.474,
     'ret_gn_w_2': 8.0,
     'rnn_conv_b_2': 8.0,
     'rg_b_a_2': 38.954,
     'rg_b_x_2': 29.124,
     'norm_xa_w_2': 8.0,
     'norm_mem_w_2': 8.0,
     'norm_ffn_w_2': 19.94,
     'ffn_conv_b_2': 39.084,
     'final_norm_w_2': 20.14}
    for name, (base, spread) in spreads.items():
        noise = np.random.default_rng([zlib.crc32(name.encode()), seed]).standard_normal(out[name].shape)
        drawn = base * np.exp(spread * noise) if base else spread * noise
        out[name] = __import__('jax').numpy.asarray(drawn.astype(out[name].dtype))
    for name, factor in factors.items():
        out[name] = (out[name] * factor).astype(out[name].dtype)
    return out
```

```python
from contextlib import ExitStack

import numpy as np

import concourse.bass as bass
import concourse.mybir as mybir

F32 = mybir.dt.float32
F32R = mybir.dt.float32r
I32 = mybir.dt.int32
ALU = mybir.AluOpType
ACT = mybir.ActivationFunctionType
AX = mybir.AxisListType.X

P = 128
T = 256
D = 2048
DC = D // P
NCOL = 512
KU = 2
UNIT = KU * NCOL
RING = 4
MLSTM_H, MLSTM_D = 4, 256
POOL_G = 4
POOL_WINDOWS = (2, 4, 8, 16)
GRID_W = 64
SGU_H, SGU_CHUNK = 8, 128
RET_H, RET_QK, RET_V = 8, 128, 256
XA_H, XA_D = 4, 512
FF = 5632
FC = FF // P
ALPHA = float((2.0 * 2) ** 0.25)
LN_EPS, GN_EPS, RMS_EPS = 1e-5, 1e-5, 1e-6
VA = MLSTM_D + 1
ROUND = 1.5 * 2 ** 23
TWO_PI_PARTS = [6.28125, 0.0019350051879882812, 3.0199159795074593e-07]
PI_BELOW = 3.1415925

PARAM_COLUMNS = [
    ("ada_b", 96), ("post_ln_g", 32), ("post_ln_b", 32), ("conv_qk", 48), ("mh_norm_g", 8), ("pool_scale", 8),
    ("sgu_ln_g", 16), ("sgu_ln_b", 16), ("norm_mix", 16), ("ret_gn", 16), ("rnn_conv_w", 64), ("rnn_conv_b", 16),
    ("rg_b_a", 16), ("rg_b_x", 16), ("rg_lambda", 16), ("norm_xa", 16), ("norm_mem", 16), ("norm_ffn", 16),
    ("ffn_conv_w", 3 * 2 * FC), ("ffn_conv_b", 2 * FC), ("final_norm", 16), ("gate_bias", 4), ("inv_freq", 1), ("rot_sign", 1),
]
COL = {}
_at = 0
for _name, _n in PARAM_COLUMNS:
    COL[_name] = _at
    _at += _n
N_PARAM = _at



class Stage:
    def __init__(self, name, weights, mode, iters, group_units=DC // KU, first=0, ada=None, act=1, dve=0, ready=0):
        self.name, self.weights, self.mode, self.iters, self.first = name, weights, mode, iters, first
        self.group_units, self.ada = group_units, ada
        self.act, self.dve, self.ready = act * 2, dve * 2, ready * 2
        if ada is None:
            self.kinds = [("w", g, k) for g in range(2) for k in range(group_units)]
        else:
            self.kinds = []
            w = a = 0
            for u in range(4 * 2 * group_units):
                if u % 4 == 0:
                    self.kinds.append(("w", w // group_units, w % group_units))
                    w += 1
                else:
                    self.kinds.append(("a", a // group_units, a % group_units))
                    a += 1
        self.n = len(self.kinds)
        self.total = self.n * iters


STAGES = [
    Stage("mem_k", "w_mem", "F", 2, ada=0, act=1),
    Stage("mem_v", "w_mem", "T", 2, ada=12, act=1, first=128),
    Stage("ctx_k", "w_k", "F", 1, act=2, dve=1),
    Stage("ctx_v", "w_v", "T", 1, act=1),
    Stage("lat_k", "w_k", "F", 1, act=2, dve=1),
    Stage("lat_v", "w_v", "T", 1, act=1),
    Stage("lat_q", "w_q", "F", 1, act=2, dve=1),
    Stage("lat_o", "w_o", "T", 1, act=1, dve=1),
    Stage("pool_u", "w_pool_u", "T", 1, act=1),
    Stage("mlstm_z", "w_mlstm_z", "F", 1, act=2, dve=1, ready=1),
    Stage("pool_z", "w_pool_z", "F", 1, act=2, dve=1, ready=1),
    Stage("even_out", "w_even_out", "F", 2, act=1, dve=1),
    Stage("sgu_v", "w_sgu_v", "T", 2, act=1),
    Stage("sgu_u", "w_sgu_u", "F", 2, act=1, dve=1),
    Stage("sgu_z", "w_sgu_z", "F", 2, act=2, dve=1, ready=1),
    Stage("odd_out", "w_odd_out", "F", 2, act=1, dve=1),
    Stage("ret_q", "w_ret_q", "F", 1, act=1, dve=1),
    Stage("ret_k", "w_ret_k", "F", 1, act=1, dve=1),
    Stage("ret_v", "w_ret_v", "T", 2, act=1),
    Stage("ret_g", "w_ret_g", "F", 2, act=2, dve=1, ready=1),
    Stage("ret_proj", "w_ret_proj", "F", 2, act=1),
    Stage("merge_a", "w_merge_a", "F", 2, act=1, dve=1),
    Stage("rnn_x", "w_rnn_x", "F", 2, act=1, dve=1),
    Stage("rnn_y", "w_rnn_y", "F", 2, act=2, dve=1, ready=1),
    Stage("merge_b", "w_merge_b", "F", 2, act=1),
    Stage("rnn_proj", "w_rnn_proj", "F", 2, act=2, dve=1, ready=1),
    Stage("mix_out", "w_mix_out", "F", 2, act=1, dve=1),
    Stage("xa_q", "w_xa_q", "F", 2, act=1),
    Stage("xa_o", "w_xa_o", "F", 2, act=1, dve=1),
    Stage("ffn_up", "w_ffn_up", "F", 11, act=2, dve=1, ready=0.5),
    Stage("ffn_down", "w_ffn_down", "F", 2, group_units=FC // KU, act=1, dve=1),
]
_u = _g = 0
ACT_DONE, DVE_DONE = {}, {}
_a = _d = 0
for _s in STAGES:
    _s.u0, _s.g0 = _u, _g
    _s.ready = int(_s.ready)
    _u += _s.total
    _g += 2 * _s.iters
    _a += _s.act * _s.iters
    _d += _s.dve * _s.iters
    ACT_DONE[_s.name], DVE_DONE[_s.name] = _a, _d
STAGE = {_s.name: _s for _s in STAGES}
LAST = STAGES[-1]


SECTIONS = [
    ("mem_norm", 1, 5, 4), ("cond", 0, 2, 2), ("lam", 0, 1, 1), ("mem_pair", 0, 8, 8), ("mod", 1, 0, 1),
    ("ctx_pair", 0, 8, 8), ("ctx_gates", 13, 13, 12), ("lat_pair", 0, 8, 8), ("lat_gates", 3, 2, 4),
    ("mlstm", 16, 8, 24), ("mh_norm", 2, 3, 2), ("pool", 4, 4, 0), ("ln0", 1, 5, 5), ("sgu_pair", 0, 8, 8),
    ("sgu_mix", 5, 2, 6), ("ln1", 1, 5, 5), ("mix_norm", 1, 5, 4), ("mix_pair", 0, 8, 8), ("retention", 20, 14, 12),
    ("rglru", 16, 36, 16), ("xa_norm", 1, 5, 4), ("xa_pair", 0, 8, 8), ("attention", 12, 12, 8),
    ("ffn_norm", 1, 5, 4), ("ffn_pair", 0, 8, 8), ("final", 1, 5, 5),
]
BEFORE, AFTER = {}, {}
_c = dict(pe=0, act=0, dve=0)
for _name, *_n in SECTIONS:
    BEFORE[_name] = dict(_c)
    _c = {k: _c[k] + n for k, n in zip(("pe", "act", "dve"), _n)}
    AFTER[_name] = dict(_c)
PAIR = dict(mem=8, ctx=16, lat=24, even_out=28, sgu=36, odd_out=40, mix=48, ret_proj=52, rnn_proj=56, mix_out=60,
            xa=68, xa_o=72, ffn=80, ffn_down=91)


class Steps:

    def __init__(self, eng, own, sems):
        self.eng, self.own, self.sems, self.at, self.n = eng, own, sems, 0, 0

    def wait(self, **need):
        for k, n in need.items():
            self.eng.wait_ge(self.sems[k], BEFORE[SECTIONS[self.at][0]][k] + n)

    def done(self, instruction):
        instruction.then_inc(self.sems[self.own], 1)
        self.n += 1

    def end(self, name):
        assert SECTIONS[self.at][0] == name, (name, SECTIONS[self.at])
        before, after = BEFORE[name][self.own], AFTER[name][self.own]
        assert self.n == after - before, (name, self.own, self.n, after - before)
        self.n = 0
        self.at += 1


class Count:

    def __init__(self):
        self.v, self.i, self.step = 0, None, 0

    def add(self, n=1):
        self.v += n
        return self.at()

    def at(self):
        return self.v if self.i is None else self.i * self.step + self.v


def rounds(eng, n, *counts):
    before = [c.v for c, _ in counts]
    if n == 1:
        yield 0
    else:
        with eng.Fori(0, n) as i:
            for c, step in counts:
                c.i, c.step = i, step
            yield i
    for (c, step), b in zip(counts, before):
        assert c.v - b == step, (c.v - b, step)
        c.v, c.i = b + step * n, None


def build(nc, t):
    ctx = ExitStack()
    with ctx:
        at = [-(-nc.sbuf_base // 64) * 64]

        def place(name, shape, dt, offset):
            return nc.alloc_sbuf_tensor_at(name, shape, dt, offset=offset)

        def sb(name, shape, dt=F32):
            size = -(-int(np.prod(shape[1:])) * 4 // 32) * 32
            at[0] += size
            return place(name, shape, dt, at[0] - size)

        SLAB = DC * T * 4
        raw = sb("raw", [P, RING, KU, NCOL])
        w_hi = sb("w_hi", [P, RING, KU, NCOL], F32R)
        w_lo = sb("w_lo", [P, RING, KU, NCOL], F32R)
        a_hi = sb("a_hi", [P, DC, T], F32R)
        a_lo = sb("a_lo", [P, DC, T], F32R)
        x = sb("x", [P, DC, T])
        work = at[0]
        at[0] += 88 * 1024

        def wk(name, shape, offset, dt=F32):
            assert offset + int(np.prod(shape[1:])) * 4 <= 88 * 1024, name
            return place(name, shape, dt, work + offset)

        K = 1024
        mem = wk("mem", [P, DC, T], 0)
        mod_rows = wk("mod_rows", [4, 96 * P], 16 * K)
        cond_pair = wk("cond_pair", [P, DC, P], 64 * K, F32R)
        kv_stage = wk("kv_stage", [P, 2, 2 * NCOL], 72 * K)
        cond = wk("cond", [P, DC, 2], 80 * K)
        cond_silu = wk("cond_silu", [P, DC, 2], 80 * K + 128)
        square = wk("square", [P, DC, T], 32 * K)
        ctx_x = wk("ctx_x", [P, DC, T], 0)
        rows = wk("rows", [4, 16, T], 0)
        gate_w = wk("gate_w", [P, DC, 16], 16 * K)
        gate_hi = wk("gate_hi", [P, DC, 16], 17 * K, F32R)
        gate_lo = wk("gate_lo", [P, DC, 16], 18 * K, F32R)
        gates = wk("gates", [P, 2, 16], 19 * K)
        columns = wk("columns", [P, 16, 4], 19 * K + 128)
        small = wk("small", [4, 4], 19 * K + 512)
        scratch_rows = wk("scratch_rows", [4, 3, 2 * T], 20 * K)
        b_hi = wk("b_hi", [P, DC, T], 0, F32R)
        b_lo = wk("b_lo", [P, DC, T], 16 * K, F32R)
        kf = wk("kf", [P, 8, T], 32 * K)
        qf = wk("qf", [P, 8, T], 40 * K)
        va = wk("va", [P, 2, MLSTM_H, VA], 48 * K)
        h_feat = wk("h_feat", [P, 8, T], 48 * K)
        state_at = 48 * K + 2 * MLSTM_H * VA * 4
        state = wk("state", [P, 8, 2, VA], state_at)
        h_tok_at = state_at + 16 * VA * 4
        h_tok = wk("h_tok", [P, 2, 4 * MLSTM_D], h_tok_at)
        k_tok = wk("k_tok", [P, 2, 4 * MLSTM_D], h_tok_at)
        mask_at = h_tok_at + 8 * K
        mask = wk("mask", [P, 2, 2, T], mask_at)
        pool_mat = wk("pool_mat", [P, POOL_G, P], mask_at + 4 * K)
        pool_tok = wk("pool_tok", [P, 2, 1024], 32 * K)
        pool_feat = wk("pool_feat", [P, 8, T], 40 * K)
        pool_y = wk("pool_y", [P, 8, T], 32 * K)
        pool_w = wk("pool_w", [P, 8, T], state_at)
        sgu_tok = wk("sgu_tok", [P, 2, D], 32 * K)
        sgu_s = wk("sgu_s", [P, DC, T], 48 * K)
        w_sp = wk("w_sp", [P, SGU_H, P], 64 * K)
        b_sp = wk("b_sp", [P, SGU_H, P], 68 * K)
        row_sum = wk("row_sum", [P, SGU_H, P], 72 * K)
        swap_q = wk("swap_q", [P, 8, T], 64 * K)
        swap_k = wk("swap_k", [P, 8, T], 72 * K)
        v_ret = wk("v_ret", [P, 2, D], 48 * K)
        ret_feat = wk("ret_feat", [P, DC, T], 64 * K)
        decay = wk("decay", [P, RET_H, T], 80 * K)
        angle = wk("angle", [P, 5, T], 0)
        ang_i = wk("ang_i", [P, T], 5 * K, I32)
        merged = wk("merged", [P, DC, T], 64 * K)
        xr = wk("xr", [P, DC, T], 32 * K)
        rec_a = wk("rec_a", [P, DC, T], 48 * K)
        rg_w = wk("rg_w", [P, 2, DC, P], 0)
        ratio = wk("ratio", [P, DC, T], 16 * K)
        sig_b = wk("sig_b", [P, DC, T], 32 * K)
        xa_qf = wk("xa_qf", [P, DC, T], 32 * K)
        xa_kf = wk("xa_kf", [P, DC, T], 48 * K)
        xa_vt = wk("xa_vt", [P, 2, D], 64 * K)
        prob = wk("prob", [P, 2, T], 80 * K)
        prob_t = wk("prob_t", [P, 2, T], 82 * K)
        soft = wk("soft", [P, 16], 84 * K)
        h_hi = wk("h_hi", [P, FC, T], 0, F32R)
        h_lo = wk("h_lo", [P, FC, T], 44 * K, F32R)
        y_out = wk("y_out", [P, DC, T], 0)

        prm = sb("prm", [P, N_PARAM])
        ident = sb("ident", [P, P])
        ones = sb("ones", [P, P])
        pick = sb("pick", [4, 4, P])
        mod = sb("mod", [P, 96, 2])
        buf_a = sb("buf_a", [P, 4, T])
        buf_b = sb("buf_b", [P, 4, T])
        buf_c = sb("buf_c", [P, 4, T])
        mean = sb("mean", [P, T])
        rstd = sb("rstd", [P, T])
        spare = sb("spare", [P, T])
        stats = sb("stats", [P, 16, 6])
        moments = sb("moments", [P, 16, 2])
        tiny = sb("tiny", [P, 24])
        lam = sb("lam", [P, 4, 16])
        lam_tmp = sb("lam_tmp", [P, 16])
        assert at[0] <= nc.sbuf_usable_end, (at[0], nc.sbuf_usable_end)

        acc = ctx.enter_context(nc.psum_tensor("acc", [P, 4, NCOL], F32))
        msc = ctx.enter_context(nc.psum_tensor("msc", [P, 4, NCOL], F32))

        def flat(tile):
            return tile[:].rearrange("p a b -> p (a b)")

        def col(name, c):
            return prm[:, bass.ds(COL[name] + c, 1)]

        def acc_f(g):
            return acc[:, 2 * g:2 * g + 2, :].rearrange("p a b -> p (a b)")

        def sem(name):
            return ctx.enter_context(nc.semaphore(name))

        raw_landed = [sem(f"raw_landed{i}") for i in range(RING)]
        hi_done, lo_done, unit_used = sem("hi_done"), sem("lo_done"), sem("unit_used")
        acc_free, ada_free = sem("acc_free"), sem("ada_free")
        act_done, dve_done, pair_ready = sem("act_done"), sem("dve_done"), sem("pair_ready")
        consts_in, mem_in, x_in, cond_in = sem("consts_in"), sem("mem_in"), sem("x_in"), sem("cond_in")
        ctx_in, gate_in, pool_in, sgu_in = sem("ctx_in"), sem("gate_in"), sem("pool_in"), sem("sgu_in")
        ret_in, rg_in, xa_in, mask_in = sem("ret_in"), sem("rg_in"), sem("xa_in"), sem("mask_in")
        kv_stored = [sem("kv_stored0"), sem("kv_stored1")]
        y_stored = sem("y_stored")
        pe_step, act_step, dve_step = sem("pe_step"), sem("act_step"), sem("dve_step")
        step_sems = dict(pe=pe_step, act=act_step, dve=dve_step)
        eps_set, x_normed = sem("eps_set"), sem("x_normed")

        block = ctx.enter_context(nc.Block())

        def used(stage):
            return RING + stage.u0 + stage.total

        @block.sync
        def _(sp):
            nc.sync.dma_start(mem[:], t["mem"]).then_inc(mem_in, 16)
            nc.sync.dma_start(prm[:], t["params"]).then_inc(consts_in, 16)
            nc.sync.dma_start(ident[:], t["ident"]).then_inc(consts_in, 16)
            nc.sync.dma_start(ones[:], t["ones"]).then_inc(consts_in, 16)
            nc.sync.dma_start(pick[:], t["pick"]).then_inc(consts_in, 16)
            nc.sync.dma_start(cond[:], t["cond"]).then_inc(cond_in, 16)
            nc.sync.dma_start(x[:], t["x"]).then_inc(x_in, 16)

            def load(stage):
                src = t[stage.weights]
                for i in rounds(sp, stage.iters):
                    for j in range(stage.n):
                        u = stage.u0 + j
                        sp.wait_ge(lo_done, i * stage.n + (u + 1))
                        at_ = i * stage.n + (stage.first + j)
                        nc.sync.dma_start(raw[:, u % RING].rearrange("p a b -> p (a b)"),
                                          src[bass.ds(at_, 1), :, :].rearrange("a p n -> p (a n)")
                                          ).then_inc(raw_landed[u % RING], 16)

            for stage in STAGES:
                if stage.name == "mem_v":
                    sp.wait_ge(pair_ready, PAIR["mem"])
                    nc.sync.dma_start(ctx_x[:], t["ctx"]).then_inc(ctx_in, 16)
                if stage.name == "ctx_v":
                    sp.wait_ge(pair_ready, PAIR["ctx"])
                    nc.sync.dma_start(gate_w[:], t["gate_w"]).then_inc(gate_in, 16)
                    nc.sync.dma_start(mask[:], t["mask"]).then_inc(mask_in, 16)
                    nc.sync.dma_start(pool_mat[:], t["pool_mat"]).then_inc(mask_in, 16)
                if stage.name == "pool_u":
                    sp.wait_ge(pe_step, AFTER["mlstm"]["pe"])
                    nc.sync.dma_start(pool_w[:], t["pool_w"]).then_inc(pool_in, 16)
                if stage.name == "sgu_v":
                    sp.wait_ge(pe_step, AFTER["pool"]["pe"])
                    nc.sync.dma_start(w_sp[:], t["w_sp"]).then_inc(sgu_in, 16)
                    nc.sync.dma_start(b_sp[:], t["b_sp"]).then_inc(sgu_in, 16)
                if stage.name == "ret_k":
                    sp.wait_ge(pair_ready, PAIR["mix"])
                    nc.sync.dma_start(ang_i[:], t["positions"].partition_broadcast(P)).then_inc(ret_in, 16)
                    nc.sync.dma_start(decay[:], t["decay"]).then_inc(ret_in, 16)
                if stage.name == "rnn_x":
                    sp.wait_ge(unit_used, used(STAGE["ret_proj"]))
                    nc.sync.dma_start(rg_w[:], t["rg_w"]).then_inc(rg_in, 16)
                if stage.name == "xa_q":
                    sp.wait_ge(pair_ready, PAIR["mix_out"])
                    sp.wait_ge(kv_stored[0], 16 * 5)
                    sp.wait_ge(kv_stored[1], 16 * 5)
                    nc.sync.dma_start(flat(xa_kf), t["mem_k"]).then_inc(xa_in, 16)
                    nc.sync.dma_start(flat(xa_vt), t["mem_v"]).then_inc(xa_in, 16)
                load(stage)
            sp.wait_ge(dve_step, AFTER["final"]["dve"])
            nc.sync.dma_start(t["out"], y_out[:]).then_inc(y_stored, 16)
            sp.wait_ge(y_stored, 16)

        @block.tensor
        def _(pe):
            steps = Steps(pe, "pe", step_sems)
            pe.sem_inc(unit_used, RING)
            pe.sem_inc(acc_free, 2)
            pe.sem_inc(ada_free, 3)

            def run(name, hi, lo, ready, as_made=False):
                stage = STAGE[name]
                for i in rounds(pe, stage.iters):
                    if not as_made:
                        pe.wait_ge(pair_ready, ready)
                    for j, (kind, g, k) in enumerate(stage.kinds):
                        u = stage.u0 + j
                        slot = u % RING
                        first, last = k == 0, k == stage.group_units - 1
                        if kind == "a":
                            if first:
                                pe.wait_ge(ada_free, i * 6 + (stage.ada + g + 1))
                            pe.wait_ge(lo_done, i * stage.n + (u + 1 + RING))
                            for c in range(KU):
                                kc = KU * k + c
                                pe.matmul(msc[:, g % 3, :], cond_pair[:, kc, :], w_hi[:, slot, c, :],
                                          start=(first and c == 0), stop=False)
                                mm = pe.matmul(msc[:, g % 3, :], cond_pair[:, kc, :], w_lo[:, slot, c, :],
                                               start=False, stop=(last and c == KU - 1))
                            mm.then_inc(unit_used, 1)
                            continue
                        if first:
                            pe.wait_ge(acc_free, i * 2 + (stage.g0 + g + 1))
                        if as_made and g == 0:
                            pe.wait_ge(pair_ready, ready + k + 1)
                        pe.wait_ge(lo_done, i * stage.n + (u + 1 + RING))
                        for c in range(KU):
                            kc = KU * k + c
                            begin, end = first and c == 0, last and c == KU - 1
                            if stage.mode == "F":
                                for m in range(4):
                                    out = acc[:, 2 * g + m // 2, (m % 2) * T:(m % 2 + 1) * T]
                                    wh = w_hi[:, slot, c, m * P:(m + 1) * P]
                                    wl = w_lo[:, slot, c, m * P:(m + 1) * P]
                                    pe.matmul(out, wh, hi[:, kc, :], start=(begin and m % 2 == 0), stop=False,
                                              skip_group_check=True)
                                    pe.matmul(out, wh, lo[:, kc, :], start=False, stop=False,
                                              skip_group_check=True)
                                    mm = pe.matmul(out, wl, hi[:, kc, :], start=False, stop=end,
                                                   skip_group_check=True)
                            else:
                                for tt in range(2):
                                    out = acc[:, 2 * g + tt, :]
                                    xh = hi[:, kc, tt * P:(tt + 1) * P]
                                    xl = lo[:, kc, tt * P:(tt + 1) * P]
                                    pe.matmul(out, xh, w_hi[:, slot, c, :], start=begin, stop=False)
                                    pe.matmul(out, xl, w_hi[:, slot, c, :], start=False, stop=False)
                                    mm = pe.matmul(out, xh, w_lo[:, slot, c, :], start=False, stop=end)
                        mm.then_inc(unit_used, 1)

            def column_sums(with_mean=False):
                if with_mean:
                    for c in range(DC):
                        pe.matmul(msc[:, 1, 0:T], ones[:], x[:, c, :], start=(c == 0), stop=(c == DC - 1))
                for q in range(4):
                    steps.wait(dve=q + 1)
                    mm = pe.matmul(msc[:, 0, 0:T], ones[:], buf_b[:, q, :], start=(q == 0), stop=(q == 3))
                steps.done(mm)

            def two_chunks(bank, c, tt):
                return msc[:, bank + c // 2, (c % 2) * T + tt * P:(c % 2) * T + (tt + 1) * P]

            pe.wait_ge(consts_in, 64)
            column_sums()
            steps.end("mem_norm")
            steps.wait(dve=2)
            steps.end("cond")
            steps.end("lam")
            steps.end("mem_pair")
            run("mem_k", a_hi, a_lo, 0, as_made=True)
            run("mem_v", a_hi, a_lo, PAIR["mem"])
            pe.wait_ge(ada_free, 3 + 24)
            for c in range(96):
                mm = pe.transpose(msc[:, 3, 4 * c:4 * c + 4], mod_rows[:, c * P:(c + 1) * P], ident[0:4, 0:4])
            steps.done(mm)
            steps.end("mod")
            steps.end("ctx_pair")

            def gate_logits():
                for tt in range(2):
                    for kc in range(DC):
                        for n, (a, w) in enumerate(((a_hi, gate_hi), (a_lo, gate_hi), (a_hi, gate_lo))):
                            mm = pe.matmul(msc[:, 0, 16 * tt:16 * tt + 16], a[:, kc, tt * P:(tt + 1) * P],
                                           w[:, kc, :], start=(kc == 0 and n == 0 and tt == 0),
                                           stop=(kc == DC - 1 and n == 2), skip_group_check=True)
                steps.done(mm)

            def gate_rows():
                for kind in range(4):
                    for tt in range(2):
                        at_ = (kind % 2) * T + tt * P
                        mm = pe.transpose(msc[0:4, 1 + kind // 2, at_:at_ + P],
                                          gates[:, tt, 4 * kind:4 * kind + 4], ident[:])
                steps.done(mm)

            def row_columns(first, n):
                for r in range(n):
                    for tt in range(2):
                        mm = pe.transpose(msc[:, 0, 8 * r + 4 * tt:8 * r + 4 * tt + 4],
                                          rows[:, first + r, tt * P:(tt + 1) * P], ident[0:4, 0:4])
                steps.done(mm)

            run("ctx_k", a_hi, a_lo, PAIR["mem"], as_made=True)
            run("ctx_v", a_hi, a_lo, PAIR["ctx"])
            steps.wait(dve=1)
            gate_logits()
            steps.wait(dve=2)
            gate_rows()
            pe.wait_ge(act_done, ACT_DONE["ctx_v"])
            for tt in range(2):
                for c in range(8):
                    mm = pe.transpose(acc[:, 2 * tt + c // 4, (c % 4) * P:(c % 4 + 1) * P],
                                      kf[:, c, tt * P:(tt + 1) * P], ident[:])
                steps.done(mm)
            steps.wait(act=5)
            row_columns(8, 2)
            for r in range(8):
                h = r % 4
                buf = flat(buf_b) if r % 2 == 0 else flat(buf_c)
                steps.wait(dve=5 + r)
                if r >= 2:
                    steps.wait(act=6 + r - 2)
                for kc in range(2):
                    for tt in range(2):
                        mm = pe.matmul(acc[:, 2 * (r % 2) + kc, 0:VA],
                                       k_tok[:, tt, h * MLSTM_D + kc * P:h * MLSTM_D + (kc + 1) * P],
                                       buf[:, tt * VA:(tt + 1) * VA], start=(tt == 0), stop=(tt == 1))
                steps.done(mm)
            steps.wait(act=13)
            steps.end("ctx_gates")
            steps.end("lat_pair")

            run("lat_k", a_hi, a_lo, PAIR["ctx"], as_made=True)
            run("lat_v", a_hi, a_lo, PAIR["lat"])
            gate_logits()
            steps.wait(dve=1)
            gate_rows()
            run("lat_q", a_hi, a_lo, PAIR["lat"])
            steps.wait(act=2, dve=3)
            row_columns(8, 6)
            steps.wait(dve=4)
            steps.end("lat_gates")
            pe.wait_ge(act_done, ACT_DONE["lat_q"])
            for r in range(8):
                d, h = divmod(r, 4)
                for j in range(2):
                    for kc in range(2):
                        pe.matmul(msc[:, 0, j * T:(j + 1) * T], kf[:, 2 * h + kc, j * P:(j + 1) * P],
                                  qf[:, 2 * h + kc, :], start=(j == 0 and kc == 0), stop=(kc == 1),
                                  skip_group_check=True)
                mm = pe.matmul(msc[:, 1, 0:T], pick[:, h, :], rows[:, 14 + d, :], start=True, stop=True)
                steps.done(mm)
                if r >= 1:
                    steps.wait(dve=3 * r)
                for tt in range(2):
                    for kc in range(2):
                        pe.matmul(acc[:, 2 + tt, 0:VA], qf[:, 2 * h + kc, tt * P:(tt + 1) * P],
                                  state[:, r, kc, :], start=(kc == 0), stop=(kc == 1))
                steps.wait(dve=3 * r + 2)
                for tt in range(2):
                    for j in range(2):
                        mm = pe.matmul(acc[:, tt, 0:VA], buf_c[:, j, tt * P:(tt + 1) * P], va[:, j, h, :],
                                       start=(j == 0), stop=(j == 1))
                steps.done(mm)
            steps.wait(dve=24)
            steps.end("mlstm")
            run("lat_o", a_hi, a_lo, PAIR["lat"])
            run("pool_u", a_hi, a_lo, PAIR["lat"])
            steps.wait(dve=2)
            for half in range(2):
                if half == 1:
                    steps.wait(act=2)
                for c in range(4):
                    for tt in range(2):
                        mm = pe.transpose(two_chunks(2, c, tt),
                                          h_tok[:, tt, (4 * half + c) * P:(4 * half + c + 1) * P], ident[:])
                steps.done(mm)
            steps.end("mh_norm")
            pe.wait_ge(act_done, ACT_DONE["pool_u"])
            pe.wait_ge(mask_in, 32)
            pe.wait_ge(pool_in, 16)
            for half in range(2):
                if half == 1:
                    steps.wait(act=1)
                for c in range(4):
                    for tt in range(2):
                        mm = pe.matmul(two_chunks(0, c, tt),
                                       pool_tok[:, tt, (4 * half + c) * P:(4 * half + c + 1) * P],
                                       pool_mat[:, (4 * half + c) // 2, :], start=(c % 2 == 0 and tt == 0),
                                       stop=True, skip_group_check=True)
                steps.done(mm)
            for half in range(2):
                steps.wait(act=2 + half)
                for c in range(4):
                    g = (4 * half + c) // 2
                    for kc in range(2):
                        mm = pe.matmul(msc[:, c // 2, (c % 2) * T:(c % 2 + 1) * T],
                                       pool_w[:, 2 * g + kc, (c % 2) * P:(c % 2 + 1) * P],
                                       pool_feat[:, 2 * g + kc, :], start=(c % 2 == 0 and kc == 0),
                                       stop=(kc == 1), skip_group_check=True)
                steps.done(mm)
            steps.end("pool")
            run("mlstm_z", a_hi, a_lo, PAIR["lat"])
            run("pool_z", a_hi, a_lo, PAIR["lat"])
            run("even_out", b_hi, b_lo, PAIR["even_out"])
            pe.wait_ge(dve_done, DVE_DONE["even_out"])
            column_sums(with_mean=True)
            steps.end("ln0")
            steps.end("sgu_pair")

            run("sgu_v", a_hi, a_lo, PAIR["even_out"], as_made=True)
            pe.wait_ge(sgu_in, 32)
            for h in range(SGU_H):
                mm = pe.matmul(msc[:, h // 4, (h % 4) * P:(h % 4 + 1) * P], ones[:], w_sp[:, h, :],
                               start=(h % 4 == 0), stop=True, skip_group_check=True)
            steps.done(mm)
            steps.wait(dve=2)
            for q in range(4):
                if q >= 1:
                    steps.wait(dve=2 + q)
                for c in range(4):
                    for n in range(2):
                        mm = pe.matmul(two_chunks(2, c, n), sgu_tok[:, n, (4 * q + c) * P:(4 * q + c + 1) * P],
                                       w_sp[:, (4 * q + c) // 2, :], start=(c % 2 == 0 and n == 0), stop=True,
                                       skip_group_check=True)
                steps.done(mm)
            steps.end("sgu_mix")
            run("sgu_u", a_hi, a_lo, PAIR["sgu"])
            run("sgu_z", a_hi, a_lo, PAIR["sgu"])
            run("odd_out", b_hi, b_lo, PAIR["odd_out"])
            pe.wait_ge(dve_done, DVE_DONE["odd_out"])
            column_sums(with_mean=True)
            steps.end("ln1")

            column_sums()
            steps.end("mix_norm")
            steps.end("mix_pair")
            run("ret_q", a_hi, a_lo, PAIR["odd_out"], as_made=True)
            run("ret_k", a_hi, a_lo, PAIR["mix"])
            run("ret_v", a_hi, a_lo, PAIR["mix"])

            def inner(h):
                buf = buf_b if h % 2 == 0 else buf_c
                steps.wait(dve=3 + h)
                if h >= 2:
                    steps.wait(act=2 + h - 2)
                cols = slice(h * RET_V, (h + 1) * RET_V)
                pe.matmul(acc[:, 2 * (h % 2), 0:RET_V], buf[:, 0, 0:P], v_ret[:, 0, cols], start=True, stop=True)
                pe.matmul(acc[:, 2 * (h % 2) + 1, 0:RET_V], buf[:, 0, P:T], v_ret[:, 0, cols], start=True,
                          stop=False)
                steps.done(pe.matmul(acc[:, 2 * (h % 2) + 1, 0:RET_V], buf[:, 1, P:T], v_ret[:, 1, cols],
                                     start=False, stop=True))

            pe.wait_ge(act_done, ACT_DONE["ret_v"])
            steps.wait(dve=2)
            for h in range(RET_H):
                if h >= 2:
                    steps.wait(dve=3 + h - 2)
                for j in range(2):
                    mm = pe.matmul(msc[:, h % 2, j * T:(j + 1) * T], kf[:, h, j * P:(j + 1) * P], qf[:, h, :],
                                   start=(j == 0), stop=True, skip_group_check=True)
                steps.done(mm)
                if h >= 1:
                    inner(h - 1)
            inner(RET_H - 1)
            steps.wait(dve=12)
            for q in range(4):
                if q >= 2:
                    steps.wait(act=11 + q - 2)
                for c in range(4):
                    for tt in range(2):
                        mm = pe.transpose(two_chunks(2 * (q % 2), c, tt),
                                          v_ret[:, tt, (4 * q + c) * P:(4 * q + c + 1) * P], ident[:])
                steps.done(mm)
            steps.end("retention")
            run("ret_g", a_hi, a_lo, PAIR["mix"])
            run("ret_proj", b_hi, b_lo, PAIR["ret_proj"])
            run("merge_a", a_hi, a_lo, PAIR["mix"])
            run("rnn_x", a_hi, a_lo, PAIR["mix"])
            pe.wait_ge(rg_in, 16)
            pe.wait_ge(dve_done, DVE_DONE["rnn_x"])
            pe.wait_ge(act_step, AFTER["retention"]["act"])
            for c in range(DC):
                if c >= 2:
                    steps.wait(act=2 * (c - 2) + 1)
                for a in range(2):
                    mm = pe.matmul(msc[:, c % 2, a * T:(a + 1) * T], rg_w[:, a, c, :], xr[:, c, :],
                                   start=(a == 0), stop=True, skip_group_check=True)
                steps.done(mm)
            steps.end("rglru")
            run("rnn_y", a_hi, a_lo, PAIR["mix"])
            run("merge_b", a_hi, a_lo, PAIR["mix"])
            run("rnn_proj", b_hi, b_lo, PAIR["rnn_proj"])
            run("mix_out", a_hi, a_lo, PAIR["mix_out"])
            pe.wait_ge(dve_done, DVE_DONE["mix_out"])
            column_sums()
            steps.end("xa_norm")
            steps.end("xa_pair")

            run("xa_q", a_hi, a_lo, PAIR["mix_out"], as_made=True)
            pe.wait_ge(act_done, ACT_DONE["xa_q"])
            pe.wait_ge(xa_in, 32)
            for h in range(XA_H):
                for tt in range(2):
                    for kc in range(4):
                        mm = pe.matmul(msc[:, 0, tt * T:(tt + 1) * T], xa_qf[:, 4 * h + kc, tt * P:(tt + 1) * P],
                                       xa_kf[:, 4 * h + kc, :], start=(tt == 0 and kc == 0), stop=(kc == 3),
                                       skip_group_check=True)
                steps.done(mm)
                steps.wait(dve=2 * h + 2)
                for j in range(2):
                    for tt in range(2):
                        mm = pe.transpose(msc[:, 1, j * T + tt * P:j * T + (tt + 1) * P],
                                          prob[:, tt, j * P:(j + 1) * P], ident[:])
                steps.done(mm)
                steps.wait(act=3 * h + 2)
                if h >= 1:
                    pe.wait_ge(pair_ready, PAIR["xa"] + h)
                for c in range(4):
                    for j in range(2):
                        mm = pe.matmul(msc[:, 2 + c // 2, (c % 2) * T:(c % 2 + 1) * T],
                                       xa_vt[:, j, h * XA_D + c * P:h * XA_D + (c + 1) * P], prob_t[:, j, :],
                                       start=(c % 2 == 0 and j == 0), stop=(j == 1), skip_group_check=True)
                steps.done(mm)
            steps.end("attention")
            run("xa_o", b_hi, b_lo, PAIR["xa_o"])
            pe.wait_ge(dve_done, DVE_DONE["xa_o"])
            column_sums()
            steps.end("ffn_norm")
            steps.end("ffn_pair")

            run("ffn_up", a_hi, a_lo, PAIR["xa_o"], as_made=True)
            run("ffn_down", h_hi, h_lo, PAIR["ffn_down"])
            pe.wait_ge(dve_done, DVE_DONE["ffn_down"])
            column_sums()
            steps.end("final")

        def walk(stage, i, split, epilogues, last=False):
            for j in range(stage.n):
                if not (last and j + RING >= stage.n):
                    split(stage, i, j + RING)
                kind, g, k = stage.kinds[j]
                if k == stage.group_units - 1:
                    epilogues[kind](i, g, i * stage.n + (stage.u0 + j + 1 + RING))

        def stage_rounds(eng, stage, *counts):
            if stage is LAST:
                for i in range(stage.iters):
                    yield i, i == stage.iters - 1
            else:
                for i in rounds(eng, stage.iters, *counts):
                    yield i, False

        @block.scalar
        def _(act):
            steps = Steps(act, "act", step_sems)
            done, dve = Count(), Count()

            def split(stage, i, j):
                u = stage.u0 + j
                slot = u % RING
                act.wait_ge(raw_landed[slot], i * (stage.n // RING * 16) + 16 * (u // RING + 1))
                act.wait_ge(unit_used, i * stage.n + (u + 1))
                nc.scalar.copy(w_hi[:, slot], raw[:, slot]).then_inc(hi_done, 1)

            def ran(instruction):
                instruction.then_inc(act_done, 1)
                done.add()

            def run(name, group):
                stage = STAGE[name]

                def rows_out(i, g, n_used):
                    act.wait_ge(unit_used, n_used)
                    at_ = i * (6 * NCOL) + (stage.ada + g) * NCOL
                    nc.scalar.copy(mod_rows[:, bass.ds(at_, NCOL)], msc[0:4, g % 3, :]).then_inc(ada_free, 1)

                def finish(i, g, n_used):
                    act.wait_ge(unit_used, n_used)
                    if dve.v:
                        act.wait_ge(dve_done, dve.at())
                    group(i, g)

                for i, last in stage_rounds(act, stage, (done, stage.act), (dve, stage.dve)):
                    walk(stage, i, split, {"w": finish, "a": rows_out}, last)

            def out_and_free(out, g, func=ACT.Copy, scale=1.0, width=None):
                src = acc_f(g) if width is None else acc[:, 2 * g:2 * g + 2, :]
                return nc.scalar.activation(out, src, func, scale=scale)

            both = flat(buf_a)

            def to_buffer(func, scale=1.0):
                def group(i, g):
                    nc.scalar.activation(both, acc_f(g), func, scale=scale).then_inc(acc_free, 1)
                    act.drain()
                    ran(act.nop())
                return group

            def to_slab(slab, func=ACT.Copy, scale=1.0):
                def group(i, g):
                    nc.scalar.activation(flat(slab)[:, bass.ds(i * (8 * T) + g * (4 * T), 4 * T)], acc_f(g), func,
                                         scale=scale).then_inc(acc_free, 1)
                    act.drain()
                    ran(act.nop())
                return group

            def to_tokens(slab):
                def group(i, g):
                    nc.scalar.copy(slab[:, :, bass.ds(i * (2 * NCOL) + g * NCOL, NCOL)],
                                   acc[:, 2 * g:2 * g + 2, :]).then_inc(acc_free, 1)
                    act.drain()
                    ran(act.nop())
                return group

            def gate_to_pair(func, hi, chunk=0, scale=1.0):
                def group(i, g):
                    to_buffer(func)(i, g)
                    act.wait_ge(dve_done, dve.add())
                    ran(nc.scalar.activation(flat(hi)[:, bass.ds(chunk * T + i * (8 * T) + g * (4 * T), 4 * T)],
                                             flat(buf_b), ACT.Copy, scale=scale))
                return group

            def with_dve(group, n=1):
                def wrapped(i, g):
                    group(i, g)
                    dve.add(n)
                return wrapped

            def squares(slab):
                for q in range(4):
                    steps.done(nc.scalar.activation(square[:, 4 * q:4 * q + 4, :].rearrange("p a b -> p (a b)"),
                                                    slab[:, 4 * q:4 * q + 4, :].rearrange("p a b -> p (a b)"),
                                                    ACT.Square))

            def rms(slab, name):
                squares(slab)
                steps.wait(pe=1)
                steps.done(nc.scalar.activation(spare[:], msc[:, 0, 0:T], ACT.Sqrt, bias=tiny[:, 21:22],
                                                scale=1.0 / D))
                steps.end(name)

            def layer_norm(name):
                squares(x)
                steps.wait(dve=5)
                steps.done(nc.scalar.activation(rstd[:], spare[:], ACT.Sqrt, bias=tiny[:, 20:21]))
                steps.end(name)

            def pair(hi, name):
                for q in range(8):
                    steps.wait(dve=q + 1)
                    steps.done(nc.scalar.copy(hi[:, 2 * q:2 * q + 2, :], buf_a[:, 2 * (q % 2):2 * (q % 2) + 2, :]))
                steps.end(name)

            act.sem_inc(kv_stored[0], 16)
            act.sem_inc(kv_stored[1], 16)
            act.wait_ge(mem_in, 16)
            act.wait_ge(eps_set, 1)
            squares(mem)
            steps.wait(pe=1)
            steps.done(nc.scalar.activation(spare[:], msc[:, 0, 0:T], ACT.Sqrt, bias=tiny[:, 21:22], scale=1.0 / D))
            steps.end("mem_norm")
            act.wait_ge(cond_in, 16)
            steps.done(nc.scalar.activation(cond_silu[:], cond[:], ACT.Silu))
            act.drain()
            steps.wait(dve=1)
            steps.done(nc.scalar.copy(cond_pair[:, :, 0:4:2], cond_silu[:]))
            steps.end("cond")
            act.wait_ge(consts_in, 64)
            steps.wait(dve=1)
            steps.done(nc.scalar.activation(lam[:, 1, :], lam[:, 0, :], ACT.Exp, scale=-1.0))
            steps.end("lam")
            pair(a_hi, "mem_pair")

            for j in range(RING):
                split(STAGES[0], 0, j)

            stored = [Count(), Count()]
            for c in stored:
                c.v = 16

            def store(dst, tokens):
                def group(i, g):
                    act.wait_ge(kv_stored[g], i * 16 + stored[g].v)
                    nc.scalar.copy(kv_stage[:, g, :], acc_f(g)).then_inc(acc_free, 1)
                    act.drain()
                    if tokens:
                        out = dst.rearrange("p (t n) -> p t n", t=2)[:, :, bass.ds(i * (2 * NCOL) + g * NCOL, NCOL)]
                        src = kv_stage[:, g, :].rearrange("p (t n) -> p t n", t=2)
                    else:
                        out, src = dst[:, bass.ds(i * (8 * T) + g * (4 * T), 4 * T)], kv_stage[:, g, :]
                    nc.scalar.dma_start(out, src).then_inc(kv_stored[g], 16)
                    ran(act.nop())
                return group

            run("mem_k", store(t["mem_k"], False))
            for c in stored:
                c.v += 32
            run("mem_v", store(t["mem_v"], True))
            steps.end("mod")

            pair(a_hi, "ctx_pair")

            def conv_silu(dst):
                def group(i, g):
                    to_buffer(ACT.Copy)(i, g)
                    act.wait_ge(dve_done, dve.add())
                    ran(nc.scalar.activation(dst[:, 4 * g:4 * g + 4, :].rearrange("p a b -> p (a b)"), flat(buf_b),
                                             ACT.Silu))
                return group

            def values(i, g):
                for tt in range(2):
                    mm = nc.scalar.copy(va[:, tt, 2 * g:2 * g + 2, 0:MLSTM_D],
                                        acc[:, 2 * g + tt, :].rearrange("p (h n) -> p h n", h=2))
                mm.then_inc(acc_free, 1)
                act.drain()
                ran(act.nop())

            run("ctx_k", conv_silu(kf))
            run("ctx_v", values)
            act.wait_ge(gate_in, 16)
            steps.done(nc.scalar.copy(gate_hi[:], gate_w[:]))
            act.wait_ge(kv_stored[0], 16 * 5)
            act.wait_ge(kv_stored[1], 16 * 5)
            for tt in range(2):
                steps.wait(pe=3 + tt)
                steps.done(nc.scalar.copy(k_tok[:, tt, :], acc_f(tt)))
            steps.wait(dve=3)
            steps.done(nc.scalar.activation(scratch_rows[:, 2, :], scratch_rows[:, 1, :], ACT.Exp, scale=-1.0))
            steps.wait(dve=4)
            steps.done(nc.scalar.activation(rows[:, 8:10, :], rows[:, 6:8, :], ACT.Exp))
            for r in range(8):
                steps.wait(pe=6 + r)
                steps.done(nc.scalar.activation(state[:, r, :, :], acc[:, 2 * (r % 2):2 * (r % 2) + 2, 0:VA], ACT.Copy,
                                                scale=MLSTM_D ** -0.5))
            steps.end("ctx_gates")
            pair(a_hi, "lat_pair")

            run("lat_k", conv_silu(kf))
            run("lat_v", values)
            steps.wait(dve=2)
            steps.done(nc.scalar.activation(scratch_rows[:, 2, :], scratch_rows[:, 1, :], ACT.Exp, scale=-1.0))
            steps.wait(dve=3)
            nc.scalar.activation(rows[:, 8:10, :], rows[:, 6:8, :], ACT.Exp)
            steps.done(nc.scalar.activation(rows[:, 10:12, :], rows[:, 0:2, :], ACT.Exp))
            run("lat_q", conv_silu(qf))
            steps.end("lat_gates")
            for r in range(8):
                d, h = divmod(r, 4)
                steps.wait(dve=3 * r + 1)
                for j in range(2):
                    mm = nc.scalar.activation(buf_b[:, j, :], buf_a[:, j, :], ACT.Exp,
                                              bias=columns[:, (4 + d) * 2 + j, h:h + 1])
                steps.done(mm)
            steps.end("mlstm")
            act.wait_ge(dve_step, AFTER["mlstm"]["dve"])
            run("lat_o", with_dve(to_buffer(ACT.Tanh, 0.5)))
            run("pool_u", to_tokens(pool_tok))
            steps.wait(dve=1)
            steps.done(nc.scalar.activation(tiny[:, 0:8], moments[:, 0:8, 1], ACT.Sqrt, bias=tiny[:, 20:21]))
            for half in range(2):
                steps.wait(pe=1 + half)
                for c in range(4):
                    mm = nc.scalar.activation(h_feat[:, 4 * half + c, :],
                                              msc[:, 2 + c // 2, (c % 2) * T:(c % 2 + 1) * T], ACT.Copy,
                                              scale=col("mh_norm_g", 4 * half + c))
                steps.done(mm)
            steps.end("mh_norm")
            for half in range(2):
                steps.wait(pe=1 + half)
                steps.done(nc.scalar.copy(pool_feat[:, 4 * half:4 * half + 4, :].rearrange("p a b -> p (a b)"),
                                          msc[:, 0:2, :].rearrange("p a b -> p (a b)")))
            for half in range(2):
                steps.wait(pe=3 + half)
                for c in range(4):
                    mm = nc.scalar.activation(pool_y[:, 4 * half + c, :],
                                              msc[:, c // 2, (c % 2) * T:(c % 2 + 1) * T], ACT.Copy,
                                              scale=col("pool_scale", 4 * half + c))
                steps.done(mm)
            steps.end("pool")
            run("mlstm_z", gate_to_pair(ACT.Silu, b_hi))
            run("pool_z", gate_to_pair(ACT.Silu, b_hi, chunk=8))

            def modulated(layer):
                def group(i, g):
                    for m in range(4):
                        mm = nc.scalar.activation(buf_a[:, m, :], acc[:, 2 * g + m // 2, (m % 2) * T:(m % 2 + 1) * T],
                                                  ACT.Copy,
                                                  scale=mod[:, bass.ds(i * 8 + (48 * layer + 32 + 4 * g + m), 1), 0])
                    mm.then_inc(acc_free, 1)
                    act.drain()
                    ran(act.nop())
                    dve.add()
                return group

            run("even_out", modulated(0))
            act.wait_ge(dve_done, DVE_DONE["even_out"])
            layer_norm("ln0")
            pair(a_hi, "sgu_pair")

            run("sgu_v", to_tokens(sgu_tok))
            steps.wait(pe=1)
            steps.done(nc.scalar.copy(row_sum[:].rearrange("p a b -> p (a b)"),
                                      msc[:, 0:2, :].rearrange("p a b -> p (a b)")))
            steps.wait(dve=1)
            steps.done(nc.scalar.activation(tiny[:, 0:2], moments[:, 0:2, 1], ACT.Sqrt, bias=tiny[:, 20:21]))
            steps.end("sgu_mix")
            act.wait_ge(dve_step, AFTER["sgu_mix"]["dve"])
            run("sgu_u", with_dve(to_buffer(ACT.Copy)))
            run("sgu_z", gate_to_pair(ACT.Silu, b_hi))
            run("odd_out", modulated(1))
            act.wait_ge(dve_done, DVE_DONE["odd_out"])
            layer_norm("ln1")
            act.wait_ge(x_normed, 1)
            rms(x, "mix_norm")
            pair(a_hi, "mix_pair")

            def halves(swap):
                def group(i, g):
                    for a in range(2):
                        nc.scalar.copy(swap[64 * a:64 * a + 64, 4 * g:4 * g + 4, :].rearrange("p a b -> p (a b)"),
                                       acc_f(g)[64 - 64 * a:128 - 64 * a, :])
                    act.drain()
                    ran(act.nop())
                    dve.add()
                return group

            run("ret_q", halves(swap_q))
            run("ret_k", halves(swap_k))
            run("ret_v", to_tokens(v_ret))
            steps.wait(dve=1)
            nc.scalar.activation(angle[:, 2, :], angle[:, 1, :], ACT.Sin, scale=col("rot_sign", 0))
            steps.done(nc.scalar.activation(angle[:, 3, :], angle[:, 1, :], ACT.Sin, scale=0.5))
            for h in range(RET_H):
                steps.wait(pe=2 * h + 3 if h < RET_H - 1 else 2 * h + 2)
                steps.done(nc.scalar.copy(v_ret[:, :, h * RET_V:(h + 1) * RET_V],
                                          acc[:, 2 * (h % 2):2 * (h % 2) + 2, 0:RET_V]))
            steps.wait(dve=11)
            steps.done(nc.scalar.activation(tiny[:, 0:16], moments[:, 0:16, 1], ACT.Sqrt, bias=tiny[:, 20:21]))
            for q in range(4):
                steps.wait(pe=17 + q)
                for c in range(4):
                    mm = nc.scalar.activation(ret_feat[:, 4 * q + c, :],
                                              msc[:, 2 * (q % 2) + c // 2, (c % 2) * T:(c % 2 + 1) * T], ACT.Copy,
                                              scale=col("ret_gn", 4 * q + c))
                steps.done(mm)
            steps.end("retention")
            run("ret_g", gate_to_pair(ACT.Silu, b_hi))
            run("ret_proj", to_slab(merged))
            run("merge_a", with_dve(to_buffer(ACT.Tanh, 0.5)))
            run("rnn_x", with_dve(to_buffer(ACT.Copy)))
            act.wait_ge(dve_done, DVE_DONE["rnn_x"])
            for c in range(DC):
                steps.wait(pe=c + 1)
                if c >= 2:
                    steps.wait(dve=c - 1)
                nc.scalar.activation(buf_a[:, c % 2, :], msc[:, c % 2, 0:T], ACT.Tanh, bias=lam[:, 1, c:c + 1], scale=0.5)
                steps.done(nc.scalar.activation(buf_b[:, c % 2, :], msc[:, c % 2, T:2 * T], ACT.Tanh,
                                                bias=lam[:, 2, c:c + 1], scale=0.5))
                act.drain()
                nc.scalar.activation(buf_c[:, c % 2, :], buf_a[:, c % 2, :], ACT.Tanh, bias=lam[:, 0, c:c + 1],
                                     scale=lam[:, 0, c:c + 1])
                steps.done(nc.scalar.activation(rec_a[:, c, :], buf_a[:, c % 2, :], ACT.Exp, bias=lam[:, 3, c:c + 1],
                                                scale=lam[:, 3, c:c + 1]))
            steps.wait(dve=16)
            for q in range(4):
                part = ratio[:, 4 * q:4 * q + 4, :].rearrange("p a b -> p (a b)")
                steps.done(nc.scalar.activation(part, part, ACT.Sqrt, scale=2.0))
            steps.end("rglru")
            run("rnn_y", gate_to_pair(ACT.Gelu_apprx_tanh, b_hi))
            run("merge_b", to_slab(sig_b, ACT.Tanh, 0.5))
            run("rnn_proj", gate_to_pair(ACT.Copy, a_hi, scale=0.5))
            run("mix_out", with_dve(to_buffer(ACT.Copy)))
            act.wait_ge(dve_done, DVE_DONE["mix_out"])
            rms(x, "xa_norm")
            pair(a_hi, "xa_pair")

            run("xa_q", to_slab(xa_qf))
            for h in range(XA_H):
                steps.wait(dve=2 * h + 1)
                for tt in range(2):
                    mm = nc.scalar.activation(prob[:, tt, :], msc[:, 0, tt * T:(tt + 1) * T], ACT.Exp,
                                              bias=soft[:, 2 + tt:3 + tt], scale=XA_D ** -0.5,
                                              accum_out=soft[:, 4 + tt:5 + tt])
                steps.done(mm)
                steps.wait(pe=3 * h + 2)
                steps.done(nc.scalar.copy(flat(prob_t), msc[:, 1, :]))
                steps.wait(pe=3 * h + 3)
                steps.done(nc.scalar.copy(b_hi[:, 4 * h:4 * h + 4, :].rearrange("p a b -> p (a b)"),
                                          msc[:, 2:4, :].rearrange("p a b -> p (a b)")))
            steps.end("attention")
            run("xa_o", with_dve(to_buffer(ACT.Copy)))
            act.wait_ge(dve_done, DVE_DONE["xa_o"])
            rms(x, "ffn_norm")
            pair(a_hi, "ffn_pair")

            def gate_and_value(i, g):
                to_buffer(ACT.Copy)(i, g)
                act.wait_ge(dve_done, dve.add())
                if g == 0:
                    ran(nc.scalar.activation(flat(buf_b), flat(buf_b), ACT.Silu))
                else:
                    ran(nc.scalar.copy(flat(h_hi)[:, bass.ds(i * (4 * T), 4 * T)], flat(buf_c)))

            run("ffn_up", gate_and_value)
            run("ffn_down", with_dve(to_buffer(ACT.Copy)))
            act.wait_ge(dve_done, DVE_DONE["ffn_down"])
            rms(x, "final")

        @block.vector
        def _(dve):
            steps = Steps(dve, "dve", step_sems)
            done, act_at = Count(), Count()
            vec = nc.vector

            def split(stage, i, j):
                u = stage.u0 + j
                slot = u % RING
                dve.wait_ge(hi_done, i * stage.n + (u + 1))
                vec.tensor_tensor(w_lo[:, slot], raw[:, slot], w_hi[:, slot].bitcast(F32),
                                  ALU.subtract).then_inc(lo_done, 1)

            def ran(instruction):
                instruction.then_inc(dve_done, 1)
                done.add()

            def run(name, group):
                stage = STAGE[name]

                def finish(i, g, n_used):
                    group(i, g)

                for i, last in stage_rounds(dve, stage, (done, stage.dve), (act_at, stage.act)):
                    walk(stage, i, split, {"w": finish, "a": lambda i, g, n: None}, last)

            def wait_act(n=1):
                dve.wait_ge(act_done, act_at.add(n))

            def none(n=1):
                def group(i, g):
                    act_at.add(n)
                return group

            def bcast(tile, n):
                return tile[:].unsqueeze(1).to_broadcast([P, n, T])

            def squares_summed():
                for q in range(4):
                    steps.wait(act=q + 1)
                    steps.done(vec.tensor_reduce(buf_b[:, q, :], square[:, 4 * q:4 * q + 4, :].rearrange("p c t -> p t c"),
                                                 AX, ALU.add))

            def reciprocal_of_root():
                steps.wait(act=5)
                vec.reciprocal(rstd[:], spare[:])
                dve.drain()

            def pair(hi, lo, make, name):
                def low(q):
                    steps.wait(act=q + 1)
                    vec.tensor_tensor(lo[:, 2 * q:2 * q + 2, :], buf_a[:, 2 * (q % 2):2 * (q % 2) + 2, :],
                                      hi[:, 2 * q:2 * q + 2, :].bitcast(F32), ALU.subtract).then_inc(pair_ready, 1)

                for q in range(8):
                    dve.drain()
                    for c in range(2):
                        mm = make(buf_a[:, 2 * (q % 2) + c, :], 2 * q + c)
                    steps.done(mm)
                    if q:
                        low(q - 1)
                low(7)
                steps.end(name)

            def rms_of(slab, weight):
                def make(out, c):
                    return vec.scalar_tensor_tensor(out, slab[:, c, :], col(weight, c), rstd[:], ALU.mult, ALU.mult)
                return make

            def modulate(slab, layer, which):
                def make(out, c):
                    return vec.tensor_scalar(out, slab[:, c, :], mod[:, 48 * layer + 16 + c, which:which + 1],
                                             mod[:, 48 * layer + c, which:which + 1], ALU.mult, ALU.add)
                return make

            def log1p(out, e, t1, t2):
                vec.tensor_scalar(t1, e, 2.0, None, ALU.add)
                dve.drain()
                vec.reciprocal(t1, t1)
                dve.drain()
                vec.tensor_tensor(t1, t1, e, ALU.mult)
                dve.drain()
                vec.tensor_tensor(t2, t1, t1, ALU.mult)
                dve.drain()
                vec.tensor_scalar(out, t2, 1.0 / 17, None, ALU.mult)
                for n in (15, 13, 11, 9, 7, 5, 3):
                    dve.drain()
                    vec.scalar_tensor_tensor(out, out, 1.0 / n, t2, ALU.add, ALU.mult)
                dve.drain()
                vec.scalar_tensor_tensor(out, out, 1.0, t1, ALU.add, ALU.mult)
                dve.drain()
                vec.tensor_scalar(out, out, 2.0, None, ALU.mult)
                dve.drain()

            dve.sem_inc(lo_done, RING)
            vec.memset(tiny[:, 20:21], LN_EPS)
            vec.memset(tiny[:, 21:22], RMS_EPS)
            dve.drain().then_inc(eps_set, 1)
            squares_summed()
            reciprocal_of_root()
            steps.end("mem_norm")
            steps.done(vec.memset(cond_pair[:].bitcast(F32), 0.0))
            steps.wait(act=2)
            steps.done(vec.tensor_tensor(cond_pair[:, :, 1:4:2], cond_silu[:], cond_pair[:, :, 0:4:2].bitcast(F32),
                                         ALU.subtract))
            steps.end("cond")
            dve.wait_ge(consts_in, 64)
            lmb = prm[:, COL["rg_lambda"]:COL["rg_lambda"] + 16]
            steps.done(vec.scalar_tensor_tensor(lam[:, 0, :], lmb, -1.0, lmb, ALU.mult, ALU.max))
            steps.wait(act=1)
            log1p(lam[:, 2, :], lam[:, 1, :], lam[:, 0, :], lam[:, 3, :])
            vec.tensor_scalar(lam[:, 0, :], lmb, -1.0, 0.0, ALU.mult, ALU.max)
            dve.drain()
            vec.tensor_tensor(lam[:, 0, :], lam[:, 0, :], lam[:, 2, :], ALU.add)
            dve.drain()
            vec.tensor_scalar(lam[:, 3, :], lam[:, 0, :], -4.0, None, ALU.mult)
            dve.drain()
            vec.tensor_scalar(lam[:, 0, :], lam[:, 3, :], -1.0, None, ALU.mult)
            vec.tensor_scalar(lam[:, 1, :], prm[:, COL["rg_b_a"]:COL["rg_b_a"] + 16], 0.5, None, ALU.mult)
            vec.tensor_scalar(lam[:, 2, :], prm[:, COL["rg_b_x"]:COL["rg_b_x"] + 16], 0.5, None, ALU.mult)
            steps.end("lam")
            dve.wait_ge(mem_in, 16)
            pair(a_hi, a_lo, rms_of(mem, "norm_mem"), "mem_pair")

            for j in range(RING):
                split(STAGES[0], 0, j)
            run("mem_k", none())
            run("mem_v", none())
            steps.wait(pe=1)
            rows4 = msc[:, 3, 0:384].rearrange("p (c n) -> p c n", n=4)
            vec.tensor_copy(mod[:], rows4[:, :, 0:4:2])
            dve.drain()
            vec.tensor_tensor(mod[:], mod[:], rows4[:, :, 1:4:2], ALU.add)
            dve.drain()
            vec.tensor_tensor(mod[:], mod[:], prm[:, COL["ada_b"]:COL["ada_b"] + 96].unsqueeze(2).to_broadcast([P, 96, 2]),
                              ALU.add)
            dve.drain()
            for layer in range(2):
                scale = mod[:, 48 * layer + 16:48 * layer + 32, :]
                mm = vec.tensor_scalar(scale, scale, 1.0, None, ALU.add)
            dve.drain()
            steps.done(dve.drain())
            steps.end("mod")

            dve.wait_ge(ctx_in, 16)
            dve.wait_ge(unit_used, used(STAGE["mem_v"]))
            pair(a_hi, a_lo, modulate(ctx_x, 0, 1), "ctx_pair")

            def conv3(dst, src, weight, c, middle):
                name, n = weight
                taps = ((1, 0), (0, -1), (2, 1)) if middle else ((2, 0), (1, -1), (0, -2))
                for m in range(4):
                    if middle:
                        vec.tensor_scalar(dst[:, m, :], src[:, m, :], col(name, c + n + m), None, ALU.mult)
                    else:
                        vec.tensor_scalar(dst[:, m, :], src[:, m, :], col(name, c + 2 * n + m), col("ffn_conv_b", c + m),
                                          ALU.mult, ALU.add)
                for tap, shift in taps[1:]:
                    dve.drain()
                    for m in range(4):
                        a, b = (slice(-shift, T), slice(0, T + shift)) if shift < 0 else (slice(0, T - shift), slice(shift, T))
                        mm = vec.scalar_tensor_tensor(dst[:, m, a], src[:, m, b], col(name, c + tap * n + m), dst[:, m, a],
                                                      ALU.mult, ALU.add)
                return mm

            def conv_qk(first):
                def group(i, g):
                    wait_act()
                    ran(conv3(buf_b, buf_a, ("conv_qk", 16), first + 4 * g, True))
                    act_at.add()
                return group

            run("ctx_k", conv_qk(8))
            run("ctx_v", none())
            steps.wait(act=1)
            steps.done(vec.tensor_tensor(gate_lo[:], gate_w[:], gate_hi[:].bitcast(F32), ALU.subtract))

            def gates_out():
                steps.wait(pe=1)
                steps.done(vec.tensor_copy(gates[:].rearrange("p a b -> p (a b)"), msc[:, 0, 0:32]))

            def forget_logits():
                steps.wait(pe=2)
                for d in range(2):
                    vec.tensor_scalar(rows[:, d, :], msc[0:4, 1, d * T:(d + 1) * T],
                                      prm[0:4, COL["gate_bias"] + d:COL["gate_bias"] + d + 1], None, ALU.add)
                    vec.tensor_scalar(scratch_rows[:, 0, d * T:(d + 1) * T], msc[0:4, 2, d * T:(d + 1) * T],
                                      prm[0:4, COL["gate_bias"] + 2 + d:COL["gate_bias"] + 3 + d], None, ALU.add)
                dve.drain()
                z = scratch_rows[:, 0, :]
                steps.done(vec.scalar_tensor_tensor(scratch_rows[:, 1, :], z, -1.0, z, ALU.mult, ALU.max))

            def decays():
                log1p(log_f, scratch_rows[:, 2, :], scratch_rows[:, 1, :], log_t)
                vec.scalar_tensor_tensor(log_f, scratch_rows[:, 0, :], 0.0, log_f, ALU.min, ALU.subtract)
                dve.drain()
                vec.tensor_tensor_scan(rows[:, 2, :], log_f[:, 0:T], log_f[:, 0:T], 0.0, ALU.add, ALU.bypass)
                vec.tensor_tensor_scan(rows[:, 3, ::-1], log_f[:, T:2 * T][:, ::-1], log_f[:, T:2 * T][:, ::-1], 0.0,
                                       ALU.add, ALU.bypass)
                dve.drain()
                vec.tensor_tensor(rows[:, 4:6, :], rows[:, 0:2, :], rows[:, 2:4, :], ALU.subtract)
                dve.drain()

            log_f = rows[:, 12:14, :].rearrange("p a b -> p (a b)")
            log_t = rows[:, 14:16, :].rearrange("p a b -> p (a b)")

            gates_out()
            forget_logits()
            steps.wait(act=4)
            decays()
            vec.tensor_reduce(small[:, 0:2], rows[:, 4:6, :], AX, ALU.max)
            dve.drain()
            vec.tensor_scalar(small[:, 0:2], small[:, 0:2], 0.0, None, ALU.max)
            dve.drain()
            for d in range(2):
                end = T - 1 if d == 0 else 0
                vec.tensor_tensor(small[:, 2 + d:3 + d], rows[:, 2 + d, end:end + 1], small[:, d:d + 1], ALU.add)
                mm = vec.tensor_scalar(rows[:, 6 + d, :], rows[:, 4 + d, :], small[:, d:d + 1], None, ALU.subtract)
            steps.done(mm)
            steps.wait(pe=5)
            vec.tensor_copy(columns[:, 0:4, :].rearrange("p a b -> p (a b)"), msc[:, 0, 0:16])
            vec.memset(va[:, :, :, MLSTM_D:VA], 1.0)
            dve.drain()
            dve.wait_ge(act_done, ACT_DONE["ctx_v"])
            for r in range(8):
                d, h = divmod(r, 4)
                buf = flat(buf_b) if r % 2 == 0 else flat(buf_c)
                if r >= 2:
                    steps.wait(pe=6 + r - 2)
                for tt in range(2):
                    mm = vec.tensor_scalar(buf[:, tt * VA:(tt + 1) * VA], va[:, tt, h, :], columns[:, 2 * d + tt, h:h + 1],
                                           None, ALU.mult)
                steps.done(mm)
            steps.end("ctx_gates")
            dve.wait_ge(x_in, 16)
            dve.wait_ge(pe_step, BEFORE["ctx_gates"]["pe"] + 1)
            pair(a_hi, a_lo, modulate(x, 0, 0), "lat_pair")

            run("lat_k", conv_qk(8))
            run("lat_v", none())
            gates_out()
            forget_logits()
            steps.wait(act=1)
            decays()
            vec.tensor_tensor_scan(rows[:, 14, :], rows[:, 4, :], rows[:, 4, :], small[:, 2:3], ALU.max, ALU.bypass)
            vec.tensor_tensor_scan(rows[:, 15, ::-1], rows[:, 5, ::-1], rows[:, 5, ::-1], small[:, 3:4], ALU.max, ALU.bypass)
            vec.tensor_copy(rows[:, 12:14, :], rows[:, 4:6, :])
            dve.drain()
            for d in range(2):
                vec.tensor_scalar(rows[:, 6 + d, :], rows[:, 14 + d, :], small[:, 2 + d:3 + d], -1.0, ALU.subtract, ALU.mult)
            steps.done(vec.scalar_tensor_tensor(rows[:, 0:2, :], rows[:, 2:4, :], -1.0, rows[:, 14:16, :], ALU.mult,
                                                ALU.subtract))
            run("lat_q", conv_qk(0))
            steps.wait(pe=3)
            steps.done(vec.tensor_copy(columns[:, 0:12, :].rearrange("p a b -> p (a b)"), msc[:, 0, 0:48]))
            steps.end("lat_gates")
            dve.wait_ge(mask_in, 32)
            num = flat(buf_a)
            for r in range(8):
                d, h = divmod(r, 4)
                steps.wait(pe=2 * r + 1)
                dve.drain()
                steps.done(vec.tensor_tensor(buf_a[:, 0:2, :], mask[:, d, :, :],
                                             msc[:, 1, 0:T].unsqueeze(1).to_broadcast([P, 2, T]), ALU.subtract))
                steps.wait(act=r + 1)
                steps.done(vec.scalar_tensor_tensor(buf_c[:, 0:2, :].rearrange("p a b -> p (a b)"), msc[:, 0, :],
                                                    MLSTM_D ** -0.5, buf_b[:, 0:2, :].rearrange("p a b -> p (a b)"),
                                                    ALU.mult, ALU.mult))
                steps.wait(pe=2 * r + 2)
                for tt in range(2):
                    vec.tensor_scalar(num[:, tt * VA:(tt + 1) * VA], acc[:, 2 + tt, 0:VA],
                                      columns[:, 2 * d + tt, h:h + 1], None, ALU.mult)
                dve.drain()
                for tt in range(2):
                    vec.tensor_tensor(num[:, tt * VA:(tt + 1) * VA], num[:, tt * VA:(tt + 1) * VA], acc[:, tt, 0:VA],
                                      ALU.add)
                dve.drain()
                den = num[:, 0:2 * VA].rearrange("p (a b) -> p a b", a=2)[:, :, MLSTM_D]
                vec.scalar_tensor_tensor(tiny[:, 0:2], den, -1.0, den, ALU.mult, ALU.max)
                dve.drain()
                vec.tensor_tensor(tiny[:, 0:2], tiny[:, 0:2], columns[:, 4 + 2 * d:6 + 2 * d, h], ALU.max)
                dve.drain()
                vec.reciprocal(tiny[:, 2:4], tiny[:, 0:2])
                dve.drain()
                vec.tensor_scalar(tiny[:, 2:4], tiny[:, 2:4], 0.5, None, ALU.mult)
                dve.drain()
                for tt in range(2):
                    out = h_tok[:, tt, h * MLSTM_D:(h + 1) * MLSTM_D]
                    n = num[:, tt * VA:tt * VA + MLSTM_D]
                    if d == 0:
                        mm = vec.tensor_scalar(out, n, tiny[:, 2 + tt:3 + tt], None, ALU.mult)
                    else:
                        mm = vec.scalar_tensor_tensor(out, n, tiny[:, 2 + tt:3 + tt], out, ALU.mult, ALU.add)
                steps.done(mm)
            steps.end("mlstm")

            def output_gate(i, g):
                wait_act()
                part = h_tok[:, :, g * NCOL:(g + 1) * NCOL]
                ran(vec.scalar_tensor_tensor(part, buf_a[:].rearrange("p (a b) t -> p a (b t)", a=2), 1.0, part,
                                             ALU.add, ALU.mult))

            run("lat_o", output_gate)
            dve.drain()
            run("pool_u", none())
            for n in range(8):
                vec.bn_stats(stats[:, n, :], h_tok[:, n // 4, (n % 4) * MLSTM_D:(n % 4 + 1) * MLSTM_D])
            dve.drain()
            for n in range(8):
                mm = vec.bn_aggr(moments[:, n, :], stats[:, n, :])
            steps.done(mm)
            steps.wait(act=1)
            vec.reciprocal(tiny[:, 8:16], tiny[:, 0:8])
            dve.drain()
            for n in range(8):
                part = h_tok[:, n // 4, (n % 4) * MLSTM_D:(n % 4 + 1) * MLSTM_D]
                mm = vec.tensor_scalar(part, part, moments[:, n, 0:1], tiny[:, 8 + n:9 + n], ALU.subtract, ALU.mult)
            steps.done(mm)
            steps.end("mh_norm")
            steps.end("pool")

            def gate_to_pair(factor, hi, lo, chunk=0):
                def group(i, g):
                    wait_act()
                    at_ = i * (8 * T) + g * (4 * T)
                    ran(vec.tensor_tensor(flat(buf_b), flat(buf_a), flat(factor)[:, bass.ds(at_, 4 * T)], ALU.mult))
                    wait_act()
                    at_ = chunk * T + i * (8 * T) + g * (4 * T)
                    vec.tensor_tensor(flat(lo)[:, bass.ds(at_, 4 * T)], flat(buf_b),
                                      flat(hi)[:, bass.ds(at_, 4 * T)].bitcast(F32), ALU.subtract).then_inc(pair_ready, 1)
                return group

            dve.wait_ge(act_step, AFTER["pool"]["act"])
            run("mlstm_z", gate_to_pair(h_feat, b_hi, b_lo))
            run("pool_z", gate_to_pair(pool_y, b_hi, b_lo, chunk=8))

            def residual(scale):
                def group(i, g):
                    wait_act()
                    part = flat(x)[:, bass.ds(i * (8 * T) + g * (4 * T), 4 * T)]
                    ran(vec.scalar_tensor_tensor(part, part, scale, flat(buf_a), ALU.mult, ALU.add))
                return group

            def layer_norm(layer, name):
                squares_summed()
                steps.wait(pe=1)
                vec.tensor_scalar(mean[:], msc[:, 1, 0:T], 1.0 / D, None, ALU.mult)
                dve.drain()
                vec.tensor_tensor(rstd[:], mean[:], mean[:], ALU.mult)
                dve.drain()
                steps.done(vec.scalar_tensor_tensor(spare[:], msc[:, 0, 0:T], 1.0 / D, rstd[:], ALU.mult, ALU.subtract))
                steps.wait(act=5)
                vec.reciprocal(rstd[:], rstd[:])
                for q in range(4):
                    part = x[:, 4 * q:4 * q + 4, :]
                    vec.tensor_tensor(part, part, bcast(mean, 4), ALU.subtract)
                dve.drain()
                for q in range(4):
                    part = x[:, 4 * q:4 * q + 4, :]
                    vec.tensor_tensor(part, part, bcast(rstd, 4), ALU.mult)
                dve.drain()
                for c in range(DC):
                    vec.tensor_scalar(x[:, c, :], x[:, c, :], col("post_ln_g", 16 * layer + c),
                                      col("post_ln_b", 16 * layer + c), ALU.mult, ALU.add)
                dve.drain()
                steps.end(name)

            run("even_out", residual(ALPHA))
            layer_norm(0, "ln0")
            pair(a_hi, a_lo, modulate(x, 1, 0), "sgu_pair")

            run("sgu_v", none())
            dve.wait_ge(act_done, ACT_DONE["sgu_v"])
            for n in range(8):
                vec.bn_stats(stats[:, n, :], sgu_tok[:, n // 4, (n % 4) * NCOL:(n % 4 + 1) * NCOL])
            dve.drain()
            for tt in range(2):
                mm = vec.bn_aggr(moments[:, tt, :], stats[:, 4 * tt:4 * tt + 4, :].rearrange("p a b -> p (a b)"))
            steps.done(mm)
            steps.wait(act=2)
            vec.reciprocal(tiny[:, 2:4], tiny[:, 0:2])
            dve.drain()
            for tt in range(2):
                mm = vec.tensor_scalar(sgu_tok[:, tt, :], sgu_tok[:, tt, :], moments[:, tt, 0:1], tiny[:, 2 + tt:3 + tt],
                                       ALU.subtract, ALU.mult)
            steps.done(mm)
            for q in range(4):
                dve.drain()
                for c in range(4):
                    h = (4 * q + c) // 2
                    vec.scalar_tensor_tensor(buf_a[:, c, 0:P], row_sum[:, h, :], col("sgu_ln_b", 4 * q + c), b_sp[:, h, :],
                                             ALU.mult, ALU.add)
                dve.drain()
                steps.wait(pe=2 + q)
                for c in range(4):
                    mm = vec.scalar_tensor_tensor(
                        sgu_s[:, 4 * q + c, :].rearrange("p (n t) -> p n t", n=2),
                        msc[:, 2 + c // 2, (c % 2) * T:(c % 2 + 1) * T].rearrange("p (n t) -> p n t", n=2),
                        col("sgu_ln_g", 4 * q + c), buf_a[:, c, 0:P].unsqueeze(1).to_broadcast([P, 2, P]),
                        ALU.mult, ALU.add)
                steps.done(mm)
            steps.end("sgu_mix")
            dve.drain()

            def times_slab(i, g):
                wait_act()
                part = flat(sgu_s)[:, bass.ds(i * (8 * T) + g * (4 * T), 4 * T)]
                ran(vec.tensor_tensor(part, part, flat(buf_a), ALU.mult))

            run("sgu_u", times_slab)
            dve.drain()
            run("sgu_z", gate_to_pair(sgu_s, b_hi, b_lo))
            run("odd_out", residual(ALPHA))
            layer_norm(1, "ln1")
            dve.drain().then_inc(x_normed, 1)
            squares_summed()
            reciprocal_of_root()
            steps.end("mix_norm")
            pair(a_hi, a_lo, rms_of(x, "norm_mix"), "mix_pair")

            def copy_to(slab):
                def group(i, g):
                    wait_act()
                    vec.tensor_copy(slab[:, 4 * g:4 * g + 4, :].rearrange("p a b -> p (a b)"), acc_f(g)).then_inc(acc_free, 1)
                    dve.drain()
                    ran(dve.drain())
                return group

            run("ret_q", copy_to(qf))
            run("ret_k", copy_to(kf))
            run("ret_v", none())
            dve.wait_ge(ret_in, 32)
            pos, ang = angle[:, 0, :], angle[:, 1, :]
            vec.tensor_copy(pos, ang_i[:])
            dve.drain()
            vec.tensor_scalar(ang, pos, col("inv_freq", 0), None, ALU.mult)
            dve.drain()
            vec.tensor_scalar(pos, ang, 1.0 / (2 * np.pi), None, ALU.mult)
            dve.drain()
            for magic in (ROUND, -ROUND):
                vec.tensor_scalar(pos, pos, magic, None, ALU.add)
                dve.drain()
            for part in TWO_PI_PARTS:
                vec.scalar_tensor_tensor(ang, pos, -part, ang, ALU.mult, ALU.add)
                dve.drain()
            steps.done(vec.tensor_scalar(ang, ang, PI_BELOW, -PI_BELOW, ALU.min, ALU.max))
            steps.wait(act=1)
            cos, sin = angle[:, 4, :], angle[:, 2, :]
            vec.tensor_tensor(cos, angle[:, 3, :], angle[:, 3, :], ALU.mult)
            dve.drain()
            vec.tensor_scalar(cos, cos, -2.0, 1.0, ALU.mult, ALU.add)
            dve.drain()
            for slab, swap in ((qf, swap_q), (kf, swap_k)):
                vec.tensor_tensor(slab[:], slab[:], cos.unsqueeze(1).to_broadcast([P, 8, T]), ALU.mult)
                vec.tensor_tensor(swap[:], swap[:], sin.unsqueeze(1).to_broadcast([P, 8, T]), ALU.mult)
            dve.drain()
            vec.tensor_tensor(qf[:], qf[:], swap_q[:], ALU.add)
            vec.tensor_tensor(kf[:], kf[:], swap_k[:], ALU.add)
            steps.done(dve.drain())
            for h in range(RET_H):
                buf = buf_b if h % 2 == 0 else buf_c
                steps.wait(pe=1 if h == 0 else 2 * h)
                if h >= 2:
                    steps.wait(pe=2 * (h - 2) + 3)
                vec.scalar_tensor_tensor(buf[:, 0, :], msc[:, h % 2, 0:T], RET_QK ** -0.5, decay[:, h, :], ALU.mult, ALU.mult)
                steps.done(vec.scalar_tensor_tensor(buf[:, 1, P:T], msc[:, h % 2, T + P:2 * T], RET_QK ** -0.5,
                                                    decay[:, h, 0:P], ALU.mult, ALU.mult))
            for n in range(16):
                h, tt = divmod(n, 2)
                steps.wait(act=2 + h)
                vec.bn_stats(stats[:, n, :], v_ret[:, tt, h * RET_V:(h + 1) * RET_V])
            dve.drain()
            for n in range(16):
                mm = vec.bn_aggr(moments[:, n, :], stats[:, n, :])
            steps.done(mm)
            steps.wait(act=10)
            vec.reciprocal(lam_tmp[:], tiny[:, 0:16])
            dve.drain()
            for n in range(16):
                h, tt = divmod(n, 2)
                part = v_ret[:, tt, h * RET_V:(h + 1) * RET_V]
                mm = vec.tensor_scalar(part, part, moments[:, n, 0:1], lam_tmp[:, n:n + 1], ALU.subtract, ALU.mult)
            steps.done(mm)
            steps.end("retention")
            dve.wait_ge(act_step, AFTER["retention"]["act"])
            run("ret_g", gate_to_pair(ret_feat, b_hi, b_lo))
            run("ret_proj", none())

            def merge_first(i, g):
                wait_act()
                part = flat(merged)[:, bass.ds(i * (8 * T) + g * (4 * T), 4 * T)]
                ran(vec.scalar_tensor_tensor(part, flat(buf_a), 1.0, part, ALU.add, ALU.mult))

            run("merge_a", merge_first)
            dve.drain()

            def conv4(i, g):
                wait_act()

                def weight(tap, m):
                    return prm[:, bass.ds(i * 8 + (COL["rnn_conv_w"] + 16 * tap + 4 * g + m), 1)]

                def part(m, start):
                    return flat(xr)[:, bass.ds(i * (8 * T) + ((4 * g + m) * T + start), T - start)]

                for m in range(4):
                    vec.tensor_scalar(part(m, 0), buf_a[:, m, :], weight(3, m),
                                      prm[:, bass.ds(i * 8 + (COL["rnn_conv_b"] + 4 * g + m), 1)], ALU.mult, ALU.add)
                for shift in (1, 2, 3):
                    dve.drain()
                    for m in range(4):
                        mm = vec.scalar_tensor_tensor(part(m, shift), buf_a[:, m, 0:T - shift], weight(3 - shift, m),
                                                      part(m, shift), ALU.mult, ALU.add)
                ran(mm)

            run("rnn_x", conv4)
            dve.drain()
            for c in range(DC):
                steps.wait(act=2 * c + 2)
                vec.scalar_tensor_tensor(xr[:, c, :], buf_b[:, c % 2, :], 1.0, xr[:, c, :], ALU.add, ALU.mult)
                vec.tensor_scalar(mean[:], buf_c[:, c % 2, :], 1.0, None, ALU.add)
                dve.drain()
                vec.reciprocal(spare[:], mean[:])
                dve.drain()
                steps.done(vec.tensor_tensor(ratio[:, c, :], buf_c[:, c % 2, :], spare[:], ALU.mult))
            dve.drain()
            for q in range(4):
                steps.wait(act=33 + q)
                for c in range(4 * q, 4 * q + 4):
                    vec.scalar_tensor_tensor(xr[:, c, :], xr[:, c, :], 0.5, ratio[:, c, :], ALU.mult, ALU.mult)
                dve.drain()
                for c in range(4 * q, 4 * q + 4):
                    vec.tensor_tensor_scan(xr[:, c, :], rec_a[:, c, :], xr[:, c, :], 0.0, ALU.mult, ALU.add)
            dve.drain()
            steps.end("rglru")
            run("rnn_y", gate_to_pair(xr, b_hi, b_lo))
            run("merge_b", none())

            def merge_second(i, g):
                wait_act()
                at_ = i * (8 * T) + g * (4 * T)
                vec.scalar_tensor_tensor(flat(buf_b), flat(sig_b)[:, bass.ds(at_, 4 * T)], 1.0, flat(buf_a), ALU.add, ALU.mult)
                dve.drain()
                ran(vec.tensor_tensor(flat(buf_b), flat(buf_b), flat(merged)[:, bass.ds(at_, 4 * T)], ALU.add))
                wait_act()
                vec.scalar_tensor_tensor(flat(a_lo)[:, bass.ds(at_, 4 * T)], flat(buf_b), 0.5,
                                         flat(a_hi)[:, bass.ds(at_, 4 * T)].bitcast(F32), ALU.mult,
                                         ALU.subtract).then_inc(pair_ready, 1)

            run("rnn_proj", merge_second)
            run("mix_out", residual(1.0))
            squares_summed()
            reciprocal_of_root()
            steps.end("xa_norm")
            pair(a_hi, a_lo, rms_of(x, "norm_xa"), "xa_pair")

            run("xa_q", none())
            for h in range(XA_H):
                steps.wait(pe=3 * h + 1)
                vec.tensor_reduce(soft[:, 0:2], msc[:, 0, :].rearrange("p (a b) -> p a b", a=2), AX, ALU.max)
                dve.drain()
                steps.done(vec.tensor_scalar(soft[:, 2:4], soft[:, 0:2], -(XA_D ** -0.5), None, ALU.mult))
                steps.wait(act=3 * h + 1)
                vec.reciprocal(soft[:, 6:8], soft[:, 4:6])
                dve.drain()
                for tt in range(2):
                    mm = vec.tensor_scalar(prob[:, tt, :], prob[:, tt, :], soft[:, 6 + tt:7 + tt], None, ALU.mult)
                steps.done(mm)
                steps.wait(act=3 * h + 3)
                vec.tensor_tensor(b_lo[:, 4 * h:4 * h + 4, :].rearrange("p a b -> p (a b)"),
                                  msc[:, 2:4, :].rearrange("p a b -> p (a b)"),
                                  b_hi[:, 4 * h:4 * h + 4, :].bitcast(F32).rearrange("p a b -> p (a b)"),
                                  ALU.subtract).then_inc(pair_ready, 1)
            steps.end("attention")
            run("xa_o", residual(1.0))
            squares_summed()
            reciprocal_of_root()
            steps.end("ffn_norm")
            pair(a_hi, a_lo, rms_of(x, "norm_ffn"), "ffn_pair")

            def gate_and_value(i, g):
                wait_act()
                dst = buf_b if g == 0 else buf_c

                def weight(name, at_):
                    return prm[:, bass.ds(i * 4 + (COL[name] + FC * g + at_), 1)]

                for m in range(4):
                    vec.tensor_scalar(dst[:, m, :], buf_a[:, m, :], weight("ffn_conv_w", 4 * FC + m),
                                      weight("ffn_conv_b", m), ALU.mult, ALU.add)
                for shift in (1, 2):
                    dve.drain()
                    for m in range(4):
                        mm = vec.scalar_tensor_tensor(dst[:, m, shift:T], buf_a[:, m, 0:T - shift],
                                                      weight("ffn_conv_w", 2 * FC * (2 - shift) + m), dst[:, m, shift:T],
                                                      ALU.mult, ALU.add)
                if g == 0:
                    ran(mm)
                    wait_act()
                    return
                dve.drain()
                ran(vec.tensor_tensor(flat(buf_c), flat(buf_c), flat(buf_b), ALU.mult))
                wait_act()
                vec.tensor_tensor(flat(h_lo)[:, bass.ds(i * (4 * T), 4 * T)], flat(buf_c),
                                  flat(h_hi)[:, bass.ds(i * (4 * T), 4 * T)].bitcast(F32),
                                  ALU.subtract).then_inc(pair_ready, 1)

            run("ffn_up", gate_and_value)
            run("ffn_down", residual(1.0))
            squares_summed()
            reciprocal_of_root()
            for c in range(DC):
                mm = vec.scalar_tensor_tensor(y_out[:, c, :], x[:, c, :], col("final_norm", c), rstd[:], ALU.mult, ALU.mult)
            steps.done(mm)
            steps.end("final")


def units(w):
    k, n = w.shape
    w = w.reshape(k // (KU * P), KU, P, n // NCOL, NCOL).transpose(3, 0, 2, 1, 4)
    return np.ascontiguousarray(w).reshape(-1, P, UNIT)


def chunks(a):
    return np.ascontiguousarray(a.reshape(a.shape[0], -1, P).transpose(2, 1, 0))


def columns_of(v):
    return v.reshape(-1, P).T


def constants():
    s, q = np.arange(T)[:, None], np.arange(T)[None, :]
    seen = np.stack([s <= q, s >= q])
    mask = np.where(seen, 0.0, -1e30).astype(np.float32)
    mask = mask.reshape(2, 2, P, T).transpose(2, 0, 1, 3)
    pool = np.zeros((P, POOL_G, P))
    for g, w in enumerate(POOL_WINDOWS):
        for row in range(P // GRID_W):
            for pos in range(GRID_W):
                lo, hi = max(pos - w // 2, 0), min(pos + (w - 1 - w // 2), GRID_W - 1)
                pool[row * GRID_W + lo:row * GRID_W + hi + 1, g, row * GRID_W + pos] = 1.0 / (hi - lo + 1)
                pool[row * GRID_W + pos, g, row * GRID_W + pos] -= 1.0
    log_gamma = np.log1p(-(2.0 ** (-5.0 - np.arange(RET_H))))
    rel = np.arange(T)[None, None, :] - np.arange(P)[:, None, None]
    decay = np.where(rel >= 0, np.exp(log_gamma[None, :, None] * np.maximum(rel, 0)), 0.0)
    pick = np.zeros((4, 4, P), np.float32)
    for h in range(4):
        pick[h, h] = 1.0
    half = RET_QK // 2
    freq = np.float32(10000.0) ** (-np.arange(half, dtype=np.float32) * np.float32(2.0) / np.float32(RET_QK))
    return {
        "ident": np.eye(P, dtype=np.float32), "ones": np.ones((P, P), np.float32), "pick": pick,
        "mask": np.ascontiguousarray(mask), "pool_mat": pool.astype(np.float32), "decay": decay.astype(np.float32),
        "inv_freq": np.tile(freq.astype(np.float32), 2),
        "rot_sign": np.repeat(np.float32([-1.0, 1.0]), half),
    }


def lay_out(i):
    const = constants()
    bias = np.zeros((P, 4), np.float32)
    bias[0:4, 0:2] = i["b_igate"][0].T
    bias[0:4, 2:4] = i["b_fgate"][0].T
    parts = {
        "ada_b": i["ada_b"], "post_ln_g": i["post_ln_g"], "post_ln_b": i["post_ln_b"], "conv_qk": i["conv_qk"],
        "mh_norm_g": i["mh_norm_g"], "pool_scale": i["pool_scale"], "sgu_ln_g": i["sgu_ln_g"],
        "sgu_ln_b": i["sgu_ln_b"], "norm_mix": i["norm_mix_w_2"], "ret_gn": i["ret_gn_w_2"],
        "rnn_conv_w": i["rnn_conv_w_2"], "rnn_conv_b": i["rnn_conv_b_2"], "rg_b_a": i["rg_b_a_2"],
        "rg_b_x": i["rg_b_x_2"], "rg_lambda": i["rg_lambda_2"], "norm_xa": i["norm_xa_w_2"],
        "norm_mem": i["norm_mem_w_2"], "norm_ffn": i["norm_ffn_w_2"], "ffn_conv_w": i["ffn_conv_w_2"],
        "ffn_conv_b": i["ffn_conv_b_2"], "final_norm": i["final_norm_w_2"], "inv_freq": const.pop("inv_freq"),
        "rot_sign": const.pop("rot_sign"),
    }
    params = [bias if name == "gate_bias" else columns_of(parts[name]) for name, _ in PARAM_COLUMNS]
    out = dict(const)
    out["params"] = np.ascontiguousarray(np.concatenate(params, axis=1))
    assert out["params"].shape == (P, N_PARAM)
    out["x"], out["ctx"], out["mem"] = chunks(i["x"][0]), chunks(i["ctx"][0]), chunks(i["mem_2"][0])
    out["cond"] = np.ascontiguousarray(np.stack([i["c"][0].reshape(DC, P).T, i["c_ctx"].reshape(DC, P).T], axis=2))
    out["positions"] = np.ascontiguousarray(i["positions_2"].reshape(T))

    kv = np.concatenate([units(i["xa_w_k_2"][0]), units(i["xa_w_v_2"][0])])
    ada = np.concatenate([units(i["ada_w"][0]), units(i["ada_w"][1])])
    n = len(kv)
    out["w_mem"] = np.concatenate([kv[:, None], ada.reshape(n, 3, P, UNIT)], axis=1).reshape(4 * n, P, UNIT)

    w = i["w_in_even"][0]
    n_m = MLSTM_H * MLSTM_D
    for k, name in enumerate(("w_q", "w_k", "w_v", "w_o", "w_mlstm_z")):
        out[name] = units(w[:, k * n_m:(k + 1) * n_m])
    gate = w[:, 5 * n_m:5 * n_m + 16]
    out["gate_w"] = np.ascontiguousarray(gate.reshape(DC, P, 16).transpose(1, 0, 2))
    out["w_pool_u"] = units(w[:, 5 * n_m + 16:6 * n_m + 16])
    out["w_pool_z"] = units(w[:, 6 * n_m + 16:])
    out["pool_w"] = np.ascontiguousarray(i["pool_w"][0].reshape(POOL_G, 2, P, 256).transpose(2, 0, 1, 3)).reshape(P, 8, 256)
    out["w_even_out"] = units(i["w_out_even"][0])
    w = i["w_in_odd"][0]
    out["w_sgu_u"], out["w_sgu_v"], out["w_sgu_z"] = units(w[:, :D]), units(w[:, D:2 * D]), units(w[:, 2 * D:])
    out["w_sp"] = np.ascontiguousarray(i["w_sp"][0].transpose(2, 0, 1))
    out["b_sp"] = np.ascontiguousarray(np.broadcast_to(i["b_sp"][0][None], (P, SGU_H, SGU_CHUNK)))
    out["w_odd_out"] = units(i["w_out_odd"][0])
    w = i["w_in_2"][0]
    first = 0
    for name, width in (("w_ret_q", 1024), ("w_ret_k", 1024), ("w_ret_v", D), ("w_ret_g", D), ("w_rnn_x", D),
                        ("w_rnn_y", D), ("w_merge_a", D), ("w_merge_b", D)):
        out[name] = units(w[:, first:first + width])
        first += width
    out["rg_w"] = np.ascontiguousarray(np.stack([i["rg_w_a_2"][0], i["rg_w_x_2"][0]]).transpose(2, 0, 1, 3))
    out["w_ret_proj"], out["w_rnn_proj"] = units(i["w_proj_ret_2"][0]), units(i["w_proj_rnn_2"][0])
    out["w_mix_out"] = units(i["w_mix_out_2"][0])
    out["w_xa_q"], out["w_xa_o"] = units(i["xa_w_q_2"][0]), units(i["xa_w_o_2"][0])
    up = i["ffn_w_up_2"][0].reshape(D, 2, FF // NCOL, NCOL).transpose(0, 2, 1, 3).reshape(D, 2 * FF)
    out["w_ffn_up"] = units(up)
    out["w_ffn_down"] = units(i["ffn_w_down_2"][0])
    return out


def kernel(**inputs):
    import concourse.bacc as bacc
    from concourse.bass_utils import run_bass_kernel_spmd

    laid = lay_out({k: np.asarray(v) for k, v in inputs.items()})
    nc = bacc.Bacc("TRN2", target_bir_lowering=False, num_devices=1)
    t = {}
    for name, a in laid.items():
        t[name] = nc.dram_tensor(f"in_{name}", a.shape, mybir.dt.from_np(a.dtype), kind="ExternalInput").ap()
    t["out"] = nc.dram_tensor("out_y", (P, DC, T), F32, kind="ExternalOutput").ap()
    t["mem_k"] = nc.dram_tensor("mem_k", (P, DC * T), F32).ap()
    t["mem_v"] = nc.dram_tensor("mem_v", (P, 2 * D), F32).ap()
    build(nc, t)
    r = run_bass_kernel_spmd(nc, [{f"in_{k}": v for k, v in laid.items()}], core_ids=[0])
    y = r.results[0]["out_y"]
    return np.ascontiguousarray(y.transpose(2, 1, 0)).reshape(1, T, D)
```

```python
from contextlib import ExitStack

import numpy as np

import concourse.bass as bass
import concourse.mybir as mybir

F32 = mybir.dt.float32
F32R = mybir.dt.float32r
I32 = mybir.dt.int32
ALU = mybir.AluOpType
ACT = mybir.ActivationFunctionType
AX = mybir.AxisListType.X

P = 128
T = 256
D = 2048
DC = D // P
NCOL = 512
KU = 2
UNIT = KU * NCOL
RING = 4
MLSTM_H, MLSTM_D = 4, 256
POOL_G = 4
POOL_WINDOWS = (2, 4, 8, 16)
GRID_W = 64
SGU_H, SGU_CHUNK = 8, 128
RET_H, RET_QK, RET_V = 8, 128, 256
XA_H, XA_D = 4, 512
FF = 5632
FC = FF // P
ALPHA = float((2.0 * 2) ** 0.25)
LN_EPS, GN_EPS, RMS_EPS = 1e-5, 1e-5, 1e-6
GATE_UNITS = DC * P // UNIT
VA = MLSTM_D + 1
ROUND = 1.5 * 2 ** 23
TWO_PI_PARTS = [6.28125, 0.0019350051879882812, 3.0199159795074593e-07]
PI_BELOW = 3.1415925

PARAM_COLUMNS = [
    ("ada_b", 96), ("post_ln_g", 32), ("post_ln_b", 32), ("conv_qk", 48), ("mh_norm_g", 8), ("pool_scale", 8),
    ("sgu_ln_g", 16), ("sgu_ln_b", 16), ("norm_mix", 16), ("ret_gn", 16), ("rnn_conv_w", 64), ("rnn_conv_b", 16),
    ("rg_b_a", 16), ("rg_b_x", 16), ("rg_lambda", 16), ("norm_xa", 16), ("norm_mem", 16), ("norm_ffn", 16),
    ("ffn_conv_w", 3 * 2 * FC), ("ffn_conv_b", 2 * FC), ("final_norm", 16), ("gate_bias", 1), ("inv_freq", 1), ("rot_sign", 1),
]
COL = {}
_at = 0
for _name, _n in PARAM_COLUMNS:
    COL[_name] = _at
    _at += _n
N_PARAM = _at



class Stage:
    def __init__(self, name, weights, mode, iters, group_units=DC // KU, ada=None, gate=False, act=1, dve=0, ready=0):
        self.name, self.weights, self.mode, self.iters = name, weights, mode, iters
        self.group_units, self.ada, self.gate = group_units, ada, gate
        self.act, self.dve, self.ready = act * 2, dve * 2, ready * 2
        self.n_w = 2 * group_units
        self.kinds = [("w", *divmod(n, group_units), (n + 1) % group_units == 0) for n in range(self.n_w)]
        if ada is not None:
            mixed = []
            for n in range(self.n_w // 2):
                a = [("a", *divmod(3 * n + m, DC // KU), (3 * n + m + 1) % (DC // KU) == 0) for m in range(3)]
                mixed += [self.kinds[2 * n], a[0], self.kinds[2 * n + 1], a[1], a[2]]
            self.kinds = mixed
        if gate:
            self.kinds += [("x", 0, k, k == GATE_UNITS - 1) for k in range(GATE_UNITS)]
        self.n = len(self.kinds)
        self.total = self.n * iters
        assert iters == 1 or self.n % RING == 0


STAGES = [
    Stage("mem_k", "w_xa_k", "F", 2, ada=0),
    Stage("mem_v", "w_xa_v", "T", 2, ada=6),
    Stage("ctx_k", "w_k", "F", 1, ada=12, gate=True, act=2, dve=1),
    Stage("ctx_v", "w_v", "T", 1, ada=15),
    Stage("lat_k", "w_k", "F", 1, ada=18, gate=True, act=2, dve=1),
    Stage("lat_v", "w_v", "T", 1, ada=21),
    Stage("lat_q", "w_q", "F", 1, act=2, dve=1),
    Stage("lat_o", "w_o", "T", 1, act=1, dve=1),
    Stage("pool_u", "w_pool_u", "T", 1, act=1),
    Stage("mlstm_z", "w_mlstm_z", "F", 1, act=2, dve=1, ready=1),
    Stage("pool_z", "w_pool_z", "F", 1, act=2, dve=1, ready=1),
    Stage("even_out", "w_even_out", "F", 2, act=2, dve=2),
    Stage("sgu_v", "w_sgu_v", "T", 2, act=1),
    Stage("sgu_u", "w_sgu_u", "F", 2, act=1, dve=1),
    Stage("sgu_z", "w_sgu_z", "F", 2, act=2, dve=1, ready=1),
    Stage("odd_out", "w_odd_out", "F", 2, act=2, dve=2),
    Stage("ret_q", "w_ret_q", "F", 1, act=1, dve=1),
    Stage("ret_k", "w_ret_k", "F", 1, act=1, dve=1),
    Stage("ret_v", "w_ret_v", "T", 2, act=1),
    Stage("ret_g", "w_ret_g", "F", 2, act=2, dve=1, ready=1),
    Stage("ret_proj", "w_ret_proj", "F", 2, act=1),
    Stage("merge_a", "w_merge_a", "F", 2, act=1, dve=1),
    Stage("rnn_x", "w_rnn_x", "F", 2, act=1, dve=1),
    Stage("rnn_y", "w_rnn_y", "F", 2, act=2, dve=1, ready=1),
    Stage("merge_b", "w_merge_b", "F", 2, act=1),
    Stage("rnn_proj", "w_rnn_proj", "F", 2, act=2, dve=1, ready=1),
    Stage("mix_out", "w_mix_out", "F", 2, act=2, dve=2),
    Stage("xa_q", "w_xa_q", "F", 2, act=1),
    Stage("xa_o", "w_xa_o", "F", 2, act=2, dve=2),
    Stage("ffn_up", "w_ffn_up", "F", 11, act=2, dve=1, ready=0.5),
    Stage("ffn_down", "w_ffn_down", "F", 2, group_units=FC // KU, act=2, dve=2),
]
_u = _g = 0
ACT_DONE, DVE_DONE = {}, {}
_a = _d = 0
for _s in STAGES:
    _s.u0, _s.g0 = _u, _g
    _s.ready = int(_s.ready)
    _u += _s.total
    _g += 2 * _s.iters
    _a += _s.act * _s.iters
    _d += _s.dve * _s.iters
    ACT_DONE[_s.name], DVE_DONE[_s.name] = _a, _d
STAGE = {_s.name: _s for _s in STAGES}
LAST = STAGES[-1]


SECTIONS = [
    ("mem_norm", 1, 5, 4), ("cond", 0, 2, 2), ("mem_pair", 0, 8, 8), ("lam", 0, 1, 1), ("mod", 1, 0, 1),
    ("ctx_pair", 0, 8, 8), ("ctx_gates", 11, 12, 10), ("lat_pair", 0, 8, 8), ("lat_gates", 1, 2, 3),
    ("mlstm", 16, 8, 24), ("mh_norm", 2, 3, 2), ("pool", 4, 4, 0), ("ln0", 1, 1, 1), ("sgu_pair", 0, 8, 8),
    ("sgu_mix", 5, 2, 6), ("ln1", 1, 1, 1), ("mix_norm", 1, 5, 8), ("mix_pair", 0, 8, 8), ("angles", 0, 1, 2), ("retention", 20, 13, 10),
    ("rglru", 16, 36, 16), ("xa_norm", 1, 1, 0), ("xa_pair", 0, 8, 8), ("attention", 12, 12, 8),
    ("ffn_norm", 1, 1, 0), ("ffn_pair", 0, 8, 8), ("final", 1, 1, 1),
]
BEFORE, AFTER = {}, {}
_c = dict(pe=0, act=0, dve=0)
for _name, *_n in SECTIONS:
    BEFORE[_name] = dict(_c)
    _c = {k: _c[k] + n for k, n in zip(("pe", "act", "dve"), _n)}
    AFTER[_name] = dict(_c)
PAIR = dict(mem=8, ctx=16, lat=24, even_out=28, sgu=36, odd_out=40, mix=48, ret_proj=52, rnn_proj=56, mix_out=60,
            xa=68, xa_o=72, ffn=80, ffn_down=91)


class Steps:

    def __init__(self, eng, own, sems):
        self.eng, self.own, self.sems, self.at, self.n = eng, own, sems, 0, 0

    def wait(self, **need):
        for k, n in need.items():
            self.eng.wait_ge(self.sems[k], BEFORE[SECTIONS[self.at][0]][k] + n)

    def done(self, instruction):
        instruction.then_inc(self.sems[self.own], 1)
        self.n += 1

    def end(self, name):
        assert SECTIONS[self.at][0] == name, (name, SECTIONS[self.at])
        before, after = BEFORE[name][self.own], AFTER[name][self.own]
        assert self.n == after - before, (name, self.own, self.n, after - before)
        self.n = 0
        self.at += 1


class Count:

    def __init__(self):
        self.v, self.i, self.step = 0, None, 0

    def add(self, n=1):
        self.v += n
        return self.at()

    def at(self):
        return self.v if self.i is None else self.i * self.step + self.v


def rounds(eng, n, *counts):
    before = [c.v for c, _ in counts]
    if n == 1:
        yield 0
    else:
        with eng.Fori(0, n) as i:
            for c, step in counts:
                c.i, c.step = i, step
            yield i
    for (c, step), b in zip(counts, before):
        assert c.v - b == step, (c.v - b, step)
        c.v, c.i = b + step * n, None


def build(nc, t):
    ctx = ExitStack()
    with ctx:
        at = [-(-nc.sbuf_base // 64) * 64]

        def place(name, shape, dt, offset):
            return nc.alloc_sbuf_tensor_at(name, shape, dt, offset=offset)

        def sb(name, shape, dt=F32):
            size = -(-int(np.prod(shape[1:])) * 4 // 32) * 32
            at[0] += size
            return place(name, shape, dt, at[0] - size)

        SLAB = DC * T * 4
        raw = sb("raw", [P, RING, KU, NCOL])
        w_hi = sb("w_hi", [P, RING, KU, NCOL], F32R)
        w_lo = sb("w_lo", [P, RING, KU, NCOL], F32R)
        a_hi = sb("a_hi", [P, DC, T], F32R)
        a_lo = sb("a_lo", [P, DC, T], F32R)
        x = sb("x", [P, DC, T])
        work = at[0]
        at[0] += 88 * 1024

        def wk(name, shape, offset, dt=F32):
            assert offset + int(np.prod(shape[1:])) * 4 <= 88 * 1024, name
            return place(name, shape, dt, work + offset)

        K = 1024
        mem = wk("mem", [P, DC, T], 0)
        mod_rows = wk("mod_rows", [4, 48 * P], 16 * K)
        cond_pair = wk("cond_pair", [P, DC, P], 80 * K, F32R)
        kv_stage = wk("kv_stage", [P, 2, 2 * NCOL], 72 * K)
        cond = wk("cond", [P, DC, 2], 30 * K)
        cond_silu = wk("cond_silu", [P, DC, 2], 30 * K + 128)
        square = wk("square", [P, DC, T], 32 * K)
        ctx_x = wk("ctx_x", [P, DC, T], 0)
        rows = wk("rows", [4, 16, T], 0)
        mod_rows2 = wk("mod_rows2", [4, 2, 3 * NCOL], 18 * K)
        gate_tmp = wk("gate_tmp", [P, 5, T], 40 * K - 128)
        columns = wk("columns", [P, 16, 4], 16 * K)
        small = wk("small", [4, 4], 17 * K)
        b_hi = wk("b_hi", [P, DC, T], 0, F32R)
        b_lo = wk("b_lo", [P, DC, T], 16 * K, F32R)
        kf = wk("kf", [P, 8, T], 32 * K - 128)
        qf = wk("qf", [P, 8, T], 40 * K - 128)
        va = wk("va", [P, 2, MLSTM_H, VA], 48 * K - 128)
        h_feat = wk("h_feat", [P, 8, T], 48 * K)
        state_at = 48 * K - 128 + 2 * MLSTM_H * VA * 4
        state = wk("state", [P, 8, 2, VA], state_at)
        h_tok_at = state_at + 16 * VA * 4
        h_tok = wk("h_tok", [P, 2, 4 * MLSTM_D], h_tok_at)
        k_tok = wk("k_tok", [P, 2, 4 * MLSTM_D], h_tok_at)
        mask_at = h_tok_at + 8 * K
        mask = wk("mask", [P, 2, 2, T], mask_at)
        pool_mat = wk("pool_mat", [P, POOL_G, P], mask_at + 4 * K)
        pool_tok = wk("pool_tok", [P, 2, 1024], 32 * K)
        pool_feat = wk("pool_feat", [P, 8, T], 40 * K)
        pool_y = wk("pool_y", [P, 8, T], 32 * K)
        pool_w = wk("pool_w", [P, 8, T], 57 * K)
        sgu_tok = wk("sgu_tok", [P, 2, D], 32 * K)
        sgu_s = wk("sgu_s", [P, DC, T], 48 * K)
        w_sp = wk("w_sp", [P, SGU_H, P], 64 * K)
        b_sp = wk("b_sp", [P, SGU_H, P], 68 * K)
        row_sum = wk("row_sum", [P, SGU_H, P], 72 * K)
        v_ret = wk("v_ret", [P, 2, D], 48 * K)
        ret_feat = wk("ret_feat", [P, DC, T], 64 * K)
        decay = wk("decay", [P, RET_H, T], 80 * K)
        angle = wk("angle", [P, 5, T], 0)
        ang_i = wk("ang_i", [P, T], 87 * K, I32)
        merged = wk("merged", [P, DC, T], 64 * K)
        xr = wk("xr", [P, DC, T], 32 * K)
        rec_a = wk("rec_a", [P, DC, T], 48 * K)
        rg_w = wk("rg_w", [P, 2, DC, P], 0)
        ratio = wk("ratio", [P, DC, T], 16 * K)
        sig_b = wk("sig_b", [P, DC, T], 32 * K)
        xa_qf = wk("xa_qf", [P, DC, T], 32 * K)
        xa_kf = wk("xa_kf", [P, DC, T], 48 * K)
        xa_vt = wk("xa_vt", [P, 2, D], 64 * K)
        prob = wk("prob", [P, 2, T], 80 * K)
        prob_t = wk("prob_t", [P, 2, T], 82 * K)
        soft = wk("soft", [P, 16], 84 * K)
        h_hi = wk("h_hi", [P, FC, T], 0, F32R)
        h_lo = wk("h_lo", [P, FC, T], 44 * K, F32R)
        y_out = wk("y_out", [P, DC, T], 0)

        prm = sb("prm", [P, N_PARAM])
        ident = sb("ident", [P, P])
        ones = sb("ones", [P, P])
        pick = sb("pick", [4, 4, P])
        mod = sb("mod", [P, 96, 2])
        buf_a = sb("buf_a", [P, 4, T])
        buf_b = sb("buf_b", [P, 4, T])
        buf_c = sb("buf_c", [P, 4, T])
        mean = sb("mean", [P, T])
        rstd = sb("rstd", [P, T])
        spare = sb("spare", [P, T])
        stats = sb("stats", [P, 16, 6])
        moments = sb("moments", [P, 16, 2])
        tiny = sb("tiny", [P, 24])
        lam = sb("lam", [P, 4, 16])
        lam_tmp = sb("lam_tmp", [P, 16])
        both_affine = sb("both_affine", [P, 2, 16])
        assert at[0] <= nc.sbuf_usable_end, (at[0], nc.sbuf_usable_end)

        acc = ctx.enter_context(nc.psum_tensor("acc", [P, 4, NCOL], F32))
        msc = ctx.enter_context(nc.psum_tensor("msc", [P, 4, NCOL], F32))

        def flat(tile):
            return tile[:].rearrange("p a b -> p (a b)")

        def col(name, c):
            return prm[:, bass.ds(COL[name] + c, 1)]

        def acc_f(g):
            return acc[:, 2 * g:2 * g + 2, :].rearrange("p a b -> p (a b)")

        def sem(name):
            return ctx.enter_context(nc.semaphore(name))

        raw_landed = [sem(f"raw_landed{i}") for i in range(RING)]
        hi_done, lo_done, unit_used = sem("hi_done"), sem("lo_done"), sem("unit_used")
        acc_free, ada_free = sem("acc_free"), sem("ada_free")
        act_done, dve_done, pair_ready = sem("act_done"), sem("dve_done"), sem("pair_ready")
        consts_in, x_in, cond_in = sem("consts_in"), sem("x_in"), sem("cond_in")
        mem_in = [sem(f"mem_in{q}") for q in range(4)]
        ctx_in, pool_in, sgu_in = sem("ctx_in"), sem("pool_in"), sem("sgu_in")
        ret_in, rg_in, xa_in, mask_in = sem("ret_in"), sem("rg_in"), sem("xa_in"), sem("mask_in")
        kv_stored = [sem("kv_stored0"), sem("kv_stored1")]
        y_stored = sem("y_stored")
        pe_step, act_step, dve_step = sem("pe_step"), sem("act_step"), sem("dve_step")
        step_sems = dict(pe=pe_step, act=act_step, dve=dve_step)
        eps_set = sem("eps_set")
        rows_turned = sem("rows_turned")

        block = ctx.enter_context(nc.Block())

        def used(stage):
            return RING + stage.u0 + stage.total

        @block.sync
        def _(sp):
            for q in range(4):
                nc.sync.dma_start(mem[:, 4 * q:4 * q + 4, :], t["mem"][:, 4 * q:4 * q + 4, :]).then_inc(mem_in[q], 16)
            nc.sync.dma_start(prm[:], t["params"]).then_inc(consts_in, 16)
            nc.sync.dma_start(ident[:], t["ident"]).then_inc(consts_in, 16)
            nc.sync.dma_start(ones[:], t["ones"]).then_inc(consts_in, 16)
            nc.sync.dma_start(pick[:], t["pick"]).then_inc(consts_in, 16)
            nc.sync.dma_start(cond[:], t["cond"]).then_inc(cond_in, 16)
            nc.sync.dma_start(x[:], t["x"]).then_inc(x_in, 16)

            def load(stage):
                for i in rounds(sp, stage.iters):
                    for j, (kind, g, k, _) in enumerate(stage.kinds):
                        u = stage.u0 + j
                        sp.wait_ge(lo_done, i * stage.n + (u + 1))
                        if kind == "w":
                            src, at_ = t[stage.weights], i * stage.n_w + (g * stage.group_units + k)
                        elif kind == "a":
                            src, at_ = t["w_ada"], i * (3 * DC // KU) + ((stage.ada + g) * (DC // KU) + k)
                        else:
                            src, at_ = t["w_gate"], k
                        nc.sync.dma_start(raw[:, u % RING].rearrange("p a b -> p (a b)"),
                                          src[bass.ds(at_, 1), :, :].rearrange("a p n -> p (a n)")
                                          ).then_inc(raw_landed[u % RING], 16)

            for stage in STAGES:
                if stage.name == "mem_v":
                    sp.wait_ge(pair_ready, PAIR["mem"])
                    nc.sync.dma_start(ctx_x[:], t["ctx"]).then_inc(ctx_in, 16)
                if stage.name == "lat_o":
                    sp.wait_ge(unit_used, used(STAGE["lat_v"]))
                    nc.sync.dma_start(mask[:], t["mask"]).then_inc(mask_in, 16)
                    nc.sync.dma_start(pool_mat[:], t["pool_mat"]).then_inc(mask_in, 16)
                    nc.sync.dma_start(ang_i[:], t["positions"].partition_broadcast(P)).then_inc(ret_in, 16)
                if stage.name == "pool_u":
                    sp.wait_ge(pe_step, AFTER["mlstm"]["pe"])
                    nc.sync.dma_start(pool_w[:], t["pool_w"]).then_inc(pool_in, 16)
                if stage.name == "sgu_v":
                    sp.wait_ge(pe_step, AFTER["pool"]["pe"])
                    nc.sync.dma_start(w_sp[:], t["w_sp"]).then_inc(sgu_in, 16)
                    nc.sync.dma_start(b_sp[:], t["b_sp"]).then_inc(sgu_in, 16)
                if stage.name == "ret_k":
                    sp.wait_ge(dve_step, AFTER["angles"]["dve"])
                    nc.sync.dma_start(decay[:], t["decay"]).then_inc(ret_in, 16)
                if stage.name == "rnn_x":
                    sp.wait_ge(unit_used, used(STAGE["ret_proj"]))
                    nc.sync.dma_start(rg_w[:], t["rg_w"]).then_inc(rg_in, 16)
                if stage.name == "xa_q":
                    sp.wait_ge(pair_ready, PAIR["mix_out"])
                    sp.wait_ge(kv_stored[0], 16 * 5)
                    sp.wait_ge(kv_stored[1], 16 * 5)
                    nc.sync.dma_start(flat(xa_kf), t["mem_k"]).then_inc(xa_in, 16)
                    nc.sync.dma_start(flat(xa_vt), t["mem_v"]).then_inc(xa_in, 16)
                load(stage)
            sp.wait_ge(dve_step, AFTER["final"]["dve"])
            nc.sync.dma_start(t["out"], y_out[:]).then_inc(y_stored, 16)
            sp.wait_ge(y_stored, 16)

        @block.tensor
        def _(pe):
            steps = Steps(pe, "pe", step_sems)
            pe.sem_inc(unit_used, RING)
            pe.sem_inc(acc_free, 2)
            pe.sem_inc(ada_free, 3)

            def run(name, hi, lo, ready, batch=0, between=None):
                stage = STAGE[name]
                for i in rounds(pe, stage.iters):
                    if not batch:
                        pe.wait_ge(pair_ready, ready)
                    for j, (kind, g, k, ends) in enumerate(stage.kinds):
                        u = stage.u0 + j
                        slot = u % RING
                        first, last = k == 0, ends
                        if kind == "a":
                            if first:
                                pe.wait_ge(ada_free, i * 3 + (stage.ada + g + 1))
                            pe.wait_ge(lo_done, i * stage.n + (u + 1 + RING))
                            for c in range(KU):
                                kc = KU * k + c
                                pe.matmul(msc[:, g, :], cond_pair[:, kc, :], w_hi[:, slot, c, :],
                                          start=(first and c == 0), stop=False)
                                mm = pe.matmul(msc[:, g, :], cond_pair[:, kc, :], w_lo[:, slot, c, :],
                                               start=False, stop=(last and c == KU - 1))
                            mm.then_inc(unit_used, 1)
                            continue
                        if kind == "x":
                            if first:
                                pe.wait_ge(ada_free, stage.ada + 3 + 3)
                            pe.wait_ge(lo_done, u + 1 + RING)
                            w_h = w_hi[:, slot].rearrange("p a b -> p (a b)")
                            w_l = w_lo[:, slot].rearrange("p a b -> p (a b)")
                            for c in range(UNIT // P):
                                kc = UNIT // P * k + c
                                cols = slice(c * P, (c + 1) * P)
                                pe.matmul(msc[:, 2, 0:T], w_h[:, cols], hi[:, kc, :], start=(kc == 0), stop=False)
                                pe.matmul(msc[:, 2, 0:T], w_h[:, cols], lo[:, kc, :], start=False, stop=False)
                                mm = pe.matmul(msc[:, 2, 0:T], w_l[:, cols], hi[:, kc, :], start=False, stop=(kc == DC - 1))
                            mm.then_inc(unit_used, 1)
                            continue
                        if first and g == 1 and between:
                            between()
                        if first:
                            pe.wait_ge(acc_free, i * 2 + (stage.g0 + g + 1))
                        if batch and g == 0 and KU * k % batch == 0:
                            pe.wait_ge(pair_ready, ready + KU * k // batch + 1)
                        pe.wait_ge(lo_done, i * stage.n + (u + 1 + RING))
                        for c in range(KU):
                            kc = KU * k + c
                            begin, end = first and c == 0, last and c == KU - 1
                            if stage.mode == "F":
                                for m in range(4):
                                    out = acc[:, 2 * g + m // 2, (m % 2) * T:(m % 2 + 1) * T]
                                    wh = w_hi[:, slot, c, m * P:(m + 1) * P]
                                    wl = w_lo[:, slot, c, m * P:(m + 1) * P]
                                    pe.matmul(out, wh, hi[:, kc, :], start=(begin and m % 2 == 0), stop=False,
                                              skip_group_check=True)
                                    pe.matmul(out, wh, lo[:, kc, :], start=False, stop=False,
                                              skip_group_check=True)
                                    mm = pe.matmul(out, wl, hi[:, kc, :], start=False, stop=end,
                                                   skip_group_check=True)
                            else:
                                for tt in range(2):
                                    out = acc[:, 2 * g + tt, :]
                                    xh = hi[:, kc, tt * P:(tt + 1) * P]
                                    xl = lo[:, kc, tt * P:(tt + 1) * P]
                                    pe.matmul(out, xh, w_hi[:, slot, c, :], start=begin, stop=False)
                                    pe.matmul(out, xl, w_hi[:, slot, c, :], start=False, stop=False)
                                    mm = pe.matmul(out, xh, w_lo[:, slot, c, :], start=False, stop=end)
                        mm.then_inc(unit_used, 1)

            def column_sums(steps_of=(1, 2, 3, 4)):
                for q in range(4):
                    steps.wait(dve=steps_of[q])
                    mm = pe.matmul(msc[:, 0, 0:T], ones[:], buf_b[:, q, :], start=(q == 0), stop=(q == 3))
                steps.done(mm)

            def sums_of(stage, with_mean=False):
                for q in range(4):
                    pe.wait_ge(dve_done, DVE_DONE[stage] - 2 * (3 - q))
                    if with_mean:
                        pe.matmul(msc[:, 1, 0:T], ones[:], buf_c[:, q, :], start=(q == 0), stop=(q == 3))
                    mm = pe.matmul(msc[:, 0, 0:T], ones[:], buf_b[:, q, :], start=(q == 0), stop=(q == 3))
                steps.done(mm)

            def two_chunks(bank, c, tt):
                return msc[:, bank + c // 2, (c % 2) * T + tt * P:(c % 2) * T + (tt + 1) * P]

            pe.wait_ge(consts_in, 64)
            column_sums()
            steps.end("mem_norm")
            steps.wait(dve=2)
            steps.end("cond")
            steps.end("mem_pair")
            steps.end("lam")
            run("mem_k", a_hi, a_lo, 0, batch=2)
            run("mem_v", a_hi, a_lo, PAIR["mem"])
            pe.wait_ge(ada_free, 3 + 12)
            for c in range(48):
                mm = pe.transpose(msc[:, 3, 4 * c:4 * c + 4], mod_rows[:, c * P:(c + 1) * P], ident[0:4, 0:4])
            steps.done(mm)
            steps.end("mod")
            steps.end("ctx_pair")

            def turn_rows(n):
                pe.wait_ge(ada_free, 3 + 12 + 3 * (n + 1))
                for c in range(12):
                    at_ = 4 * (48 + 12 * n + c)
                    mm = pe.transpose(msc[:, 3, at_:at_ + 4], mod_rows2[:, n % 2, c * P:(c + 1) * P], ident[0:4, 0:4])
                mm.then_inc(rows_turned, 1)

            def row_columns(first, n):
                for r in range(n):
                    for tt in range(2):
                        mm = pe.transpose(msc[:, 0, 8 * r + 4 * tt:8 * r + 4 * tt + 4],
                                          rows[:, first + r, tt * P:(tt + 1) * P], ident[0:4, 0:4])
                steps.done(mm)

            run("ctx_k", a_hi, a_lo, PAIR["mem"], batch=2)

            def in_ctx_v():
                steps.wait(dve=1)
                turn_rows(0)

            run("ctx_v", a_hi, a_lo, PAIR["ctx"], between=in_ctx_v)
            pe.wait_ge(act_done, ACT_DONE["ctx_v"])
            for tt in range(2):
                for c in range(8):
                    mm = pe.transpose(acc[:, 2 * tt + c // 4, (c % 4) * P:(c % 4 + 1) * P],
                                      kf[:, c, tt * P:(tt + 1) * P], ident[:])
                steps.done(mm)
            turn_rows(1)
            steps.wait(act=4)
            row_columns(8, 2)
            for r in range(8):
                h = r % 4
                buf = flat(buf_b) if r % 2 == 0 else flat(buf_c)
                steps.wait(dve=3 + r)
                if r >= 2:
                    steps.wait(act=5 + r - 2)
                for kc in range(2):
                    for tt in range(2):
                        mm = pe.matmul(acc[:, 2 * (r % 2) + kc, 0:VA],
                                       k_tok[:, tt, h * MLSTM_D + kc * P:h * MLSTM_D + (kc + 1) * P],
                                       buf[:, tt * VA:(tt + 1) * VA], start=(tt == 0), stop=(tt == 1))
                steps.done(mm)
            steps.wait(act=12)
            steps.end("ctx_gates")
            steps.end("lat_pair")

            run("lat_k", a_hi, a_lo, PAIR["ctx"], batch=2)

            def in_lat_v():
                steps.wait(dve=1)
                turn_rows(2)

            run("lat_v", a_hi, a_lo, PAIR["lat"], between=in_lat_v)
            run("lat_q", a_hi, a_lo, PAIR["lat"])
            turn_rows(3)
            steps.wait(act=2, dve=2)
            row_columns(8, 6)
            steps.wait(dve=3)
            steps.end("lat_gates")
            pe.wait_ge(act_done, ACT_DONE["lat_q"])
            for r in range(8):
                d, h = divmod(r, 4)
                for j in range(2):
                    for kc in range(2):
                        pe.matmul(msc[:, 0, j * T:(j + 1) * T], kf[:, 2 * h + kc, j * P:(j + 1) * P],
                                  qf[:, 2 * h + kc, :], start=(j == 0 and kc == 0), stop=(kc == 1),
                                  skip_group_check=True)
                mm = pe.matmul(msc[:, 1, 0:T], pick[:, h, :], rows[:, 14 + d, :], start=True, stop=True)
                steps.done(mm)
                if r >= 1:
                    steps.wait(dve=3 * r)
                for tt in range(2):
                    for kc in range(2):
                        pe.matmul(acc[:, 2 + tt, 0:VA], qf[:, 2 * h + kc, tt * P:(tt + 1) * P],
                                  state[:, r, kc, :], start=(kc == 0), stop=(kc == 1))
                steps.wait(dve=3 * r + 2)
                for tt in range(2):
                    for j in range(2):
                        mm = pe.matmul(acc[:, tt, 0:VA], buf_c[:, j, tt * P:(tt + 1) * P], va[:, j, h, :],
                                       start=(j == 0), stop=(j == 1))
                steps.done(mm)
            steps.wait(dve=24)
            steps.end("mlstm")
            run("lat_o", a_hi, a_lo, PAIR["lat"])
            run("pool_u", a_hi, a_lo, PAIR["lat"])
            steps.wait(dve=2)
            for half in range(2):
                if half == 1:
                    steps.wait(act=2)
                for c in range(4):
                    for tt in range(2):
                        mm = pe.transpose(two_chunks(2, c, tt),
                                          h_tok[:, tt, (4 * half + c) * P:(4 * half + c + 1) * P], ident[:])
                steps.done(mm)
            steps.end("mh_norm")
            pe.wait_ge(act_done, ACT_DONE["pool_u"])
            pe.wait_ge(mask_in, 32)
            pe.wait_ge(pool_in, 16)
            for half in range(2):
                if half == 1:
                    steps.wait(act=1)
                for c in range(4):
                    for tt in range(2):
                        mm = pe.matmul(two_chunks(0, c, tt),
                                       pool_tok[:, tt, (4 * half + c) * P:(4 * half + c + 1) * P],
                                       pool_mat[:, (4 * half + c) // 2, :], start=(c % 2 == 0 and tt == 0),
                                       stop=True, skip_group_check=True)
                steps.done(mm)
            for half in range(2):
                steps.wait(act=2 + half)
                for c in range(4):
                    g = (4 * half + c) // 2
                    for kc in range(2):
                        mm = pe.matmul(msc[:, c // 2, (c % 2) * T:(c % 2 + 1) * T],
                                       pool_w[:, 2 * g + kc, (c % 2) * P:(c % 2 + 1) * P],
                                       pool_feat[:, 2 * g + kc, :], start=(c % 2 == 0 and kc == 0),
                                       stop=(kc == 1), skip_group_check=True)
                steps.done(mm)
            steps.end("pool")
            run("mlstm_z", a_hi, a_lo, PAIR["lat"])
            run("pool_z", a_hi, a_lo, PAIR["lat"])
            run("even_out", b_hi, b_lo, PAIR["lat"], batch=4)
            sums_of("even_out", with_mean=True)
            steps.end("ln0")
            steps.end("sgu_pair")

            run("sgu_v", a_hi, a_lo, PAIR["even_out"], batch=2)
            pe.wait_ge(sgu_in, 32)
            for h in range(SGU_H):
                mm = pe.matmul(msc[:, h // 4, (h % 4) * P:(h % 4 + 1) * P], ones[:], w_sp[:, h, :],
                               start=(h % 4 == 0), stop=True, skip_group_check=True)
            steps.done(mm)
            steps.wait(dve=2)
            for q in range(4):
                if q >= 1:
                    steps.wait(dve=2 + q)
                for c in range(4):
                    for n in range(2):
                        mm = pe.matmul(two_chunks(2, c, n), sgu_tok[:, n, (4 * q + c) * P:(4 * q + c + 1) * P],
                                       w_sp[:, (4 * q + c) // 2, :], start=(c % 2 == 0 and n == 0), stop=True,
                                       skip_group_check=True)
                steps.done(mm)
            steps.end("sgu_mix")
            run("sgu_u", a_hi, a_lo, PAIR["sgu"])
            run("sgu_z", a_hi, a_lo, PAIR["sgu"])
            run("odd_out", b_hi, b_lo, PAIR["sgu"], batch=4)
            sums_of("odd_out", with_mean=True)
            steps.end("ln1")

            column_sums((3, 5, 7, 8))
            steps.end("mix_norm")
            steps.end("mix_pair")
            steps.end("angles")
            run("ret_q", a_hi, a_lo, PAIR["odd_out"], batch=2)
            run("ret_k", a_hi, a_lo, PAIR["mix"])
            run("ret_v", a_hi, a_lo, PAIR["mix"])

            def inner(h):
                buf = buf_b if h % 2 == 0 else buf_c
                steps.wait(dve=1 + h)
                if h >= 2:
                    steps.wait(act=1 + h - 2)
                cols = slice(h * RET_V, (h + 1) * RET_V)
                pe.matmul(acc[:, 2 * (h % 2), 0:RET_V], buf[:, 0, 0:P], v_ret[:, 0, cols], start=True, stop=True)
                pe.matmul(acc[:, 2 * (h % 2) + 1, 0:RET_V], buf[:, 0, P:T], v_ret[:, 0, cols], start=True,
                          stop=False)
                steps.done(pe.matmul(acc[:, 2 * (h % 2) + 1, 0:RET_V], buf[:, 1, P:T], v_ret[:, 1, cols],
                                     start=False, stop=True))

            pe.wait_ge(act_done, ACT_DONE["ret_v"])
            pe.wait_ge(dve_done, DVE_DONE["ret_k"])
            for h in range(RET_H):
                if h >= 2:
                    steps.wait(dve=1 + h - 2)
                for j in range(2):
                    mm = pe.matmul(msc[:, h % 2, j * T:(j + 1) * T], kf[:, h, j * P:(j + 1) * P], qf[:, h, :],
                                   start=(j == 0), stop=True, skip_group_check=True)
                steps.done(mm)
                if h >= 1:
                    inner(h - 1)
            inner(RET_H - 1)
            steps.wait(dve=10)
            for q in range(4):
                if q >= 2:
                    steps.wait(act=10 + q - 2)
                for c in range(4):
                    for tt in range(2):
                        mm = pe.transpose(two_chunks(2 * (q % 2), c, tt),
                                          v_ret[:, tt, (4 * q + c) * P:(4 * q + c + 1) * P], ident[:])
                steps.done(mm)
            steps.end("retention")
            run("ret_g", a_hi, a_lo, PAIR["mix"])
            run("ret_proj", b_hi, b_lo, PAIR["mix"], batch=4)
            run("merge_a", a_hi, a_lo, PAIR["mix"])
            run("rnn_x", a_hi, a_lo, PAIR["mix"])
            pe.wait_ge(rg_in, 16)
            pe.wait_ge(dve_done, DVE_DONE["rnn_x"])
            pe.wait_ge(act_step, AFTER["retention"]["act"])
            for c in range(DC):
                if c >= 2:
                    steps.wait(act=2 * (c - 2) + 1)
                for a in range(2):
                    mm = pe.matmul(msc[:, c % 2, a * T:(a + 1) * T], rg_w[:, a, c, :], xr[:, c, :],
                                   start=(a == 0), stop=True, skip_group_check=True)
                steps.done(mm)
            steps.end("rglru")
            run("rnn_y", a_hi, a_lo, PAIR["mix"])
            run("merge_b", a_hi, a_lo, PAIR["mix"])
            run("rnn_proj", b_hi, b_lo, PAIR["rnn_proj"])
            run("mix_out", a_hi, a_lo, PAIR["rnn_proj"], batch=4)
            sums_of("mix_out")
            steps.end("xa_norm")
            steps.end("xa_pair")

            run("xa_q", a_hi, a_lo, PAIR["mix_out"], batch=2)
            pe.wait_ge(act_done, ACT_DONE["xa_q"])
            pe.wait_ge(xa_in, 32)
            for h in range(XA_H):
                for tt in range(2):
                    for kc in range(4):
                        mm = pe.matmul(msc[:, 0, tt * T:(tt + 1) * T], xa_qf[:, 4 * h + kc, tt * P:(tt + 1) * P],
                                       xa_kf[:, 4 * h + kc, :], start=(tt == 0 and kc == 0), stop=(kc == 3),
                                       skip_group_check=True)
                steps.done(mm)
                steps.wait(dve=2 * h + 2)
                for j in range(2):
                    for tt in range(2):
                        mm = pe.transpose(msc[:, 1, j * T + tt * P:j * T + (tt + 1) * P],
                                          prob[:, tt, j * P:(j + 1) * P], ident[:])
                steps.done(mm)
                steps.wait(act=3 * h + 2)
                if h >= 1:
                    pe.wait_ge(pair_ready, PAIR["xa"] + h)
                for c in range(4):
                    for j in range(2):
                        mm = pe.matmul(msc[:, 2 + c // 2, (c % 2) * T:(c % 2 + 1) * T],
                                       xa_vt[:, j, h * XA_D + c * P:h * XA_D + (c + 1) * P], prob_t[:, j, :],
                                       start=(c % 2 == 0 and j == 0), stop=(j == 1), skip_group_check=True)
                steps.done(mm)
            steps.end("attention")
            run("xa_o", b_hi, b_lo, PAIR["xa"], batch=4)
            sums_of("xa_o")
            steps.end("ffn_norm")
            steps.end("ffn_pair")

            run("ffn_up", a_hi, a_lo, PAIR["xa_o"], batch=2)
            run("ffn_down", h_hi, h_lo, PAIR["ffn"], batch=4)
            sums_of("ffn_down")
            steps.end("final")

        def walk(stage, i, split, epilogues, last=False):
            for j in range(stage.n):
                if not (last and j + RING >= stage.n):
                    split(stage, i, j + RING)
                kind, g, _, ends = stage.kinds[j]
                if ends:
                    epilogues[kind](i, g, i * stage.n + (stage.u0 + j + 1 + RING))

        def stage_rounds(eng, stage, *counts):
            if stage is LAST:
                for i in range(stage.iters):
                    yield i, i == stage.iters - 1
            else:
                for i in rounds(eng, stage.iters, *counts):
                    yield i, False

        @block.scalar
        def _(act):
            steps = Steps(act, "act", step_sems)
            done, dve = Count(), Count()

            def split(stage, i, j):
                u = stage.u0 + j
                slot = u % RING
                act.wait_ge(raw_landed[slot], i * (stage.n // RING * 16) + 16 * (u // RING + 1))
                act.wait_ge(unit_used, i * stage.n + (u + 1))
                nc.scalar.copy(w_hi[:, slot], raw[:, slot]).then_inc(hi_done, 1)

            def ran(instruction):
                instruction.then_inc(act_done, 1)
                done.add()

            def forget_exp(i, g, n_used):
                steps.wait(dve=1)
                steps.done(nc.scalar.activation(gate_tmp[64:P, 2, :], gate_tmp[64:P, 1, :], ACT.Exp, scale=-1.0))

            def run(name, group):
                stage = STAGE[name]

                def rows_out(i, g, n_used):
                    if stage.ada >= 18 and g == 0:
                        act.wait_ge(rows_turned, stage.ada // 3 - 5)
                    act.wait_ge(unit_used, n_used)
                    if stage.ada < 12:
                        out = mod_rows[:, bass.ds(i * (3 * NCOL) + (stage.ada + g) * NCOL, NCOL)]
                    else:
                        out = mod_rows2[:, stage.ada // 3 % 2, g * NCOL:(g + 1) * NCOL]
                    nc.scalar.copy(out, msc[0:4, g, :]).then_inc(ada_free, 1)

                def finish(i, g, n_used):
                    act.wait_ge(unit_used, n_used)
                    if dve.v:
                        act.wait_ge(dve_done, dve.at())
                    group(i, g)

                for i, last in stage_rounds(act, stage, (done, stage.act), (dve, stage.dve)):
                    walk(stage, i, split, {"w": finish, "a": rows_out, "x": forget_exp}, last)

            def out_and_free(out, g, func=ACT.Copy, scale=1.0, width=None):
                src = acc_f(g) if width is None else acc[:, 2 * g:2 * g + 2, :]
                return nc.scalar.activation(out, src, func, scale=scale)

            both = flat(buf_a)

            def to_buffer(func, scale=1.0):
                def group(i, g):
                    nc.scalar.activation(both, acc_f(g), func, scale=scale).then_inc(acc_free, 1)
                    act.drain()
                    ran(act.nop())
                return group

            def to_slab(slab, func=ACT.Copy, scale=1.0):
                def group(i, g):
                    nc.scalar.activation(flat(slab)[:, bass.ds(i * (8 * T) + g * (4 * T), 4 * T)], acc_f(g), func,
                                         scale=scale).then_inc(acc_free, 1)
                    act.drain()
                    ran(act.nop())
                return group

            def to_tokens(slab):
                def group(i, g):
                    nc.scalar.copy(slab[:, :, bass.ds(i * (2 * NCOL) + g * NCOL, NCOL)],
                                   acc[:, 2 * g:2 * g + 2, :]).then_inc(acc_free, 1)
                    act.drain()
                    ran(act.nop())
                return group

            def gate_to_pair(func, hi, chunk=0, scale=1.0):
                def group(i, g):
                    to_buffer(func)(i, g)
                    act.wait_ge(dve_done, dve.add())
                    ran(nc.scalar.activation(flat(hi)[:, bass.ds(chunk * T + i * (8 * T) + g * (4 * T), 4 * T)],
                                             flat(buf_b), ACT.Copy, scale=scale))
                return group

            def with_dve(group, n=1):
                def wrapped(i, g):
                    group(i, g)
                    dve.add(n)
                return wrapped

            def rms(name):
                steps.wait(pe=1)
                steps.done(nc.scalar.activation(spare[:], msc[:, 0, 0:T], ACT.Sqrt, bias=tiny[:, 21:22],
                                                scale=1.0 / D))
                steps.end(name)

            def layer_norm(name):
                steps.wait(dve=1)
                steps.done(nc.scalar.activation(rstd[:], spare[:], ACT.Sqrt, bias=tiny[:, 20:21]))
                steps.end(name)

            def pair(hi, name, after=None):
                for q in range(8):
                    steps.wait(dve=q + 1)
                    steps.done(nc.scalar.copy(hi[:, 2 * q:2 * q + 2, :], buf_a[:, 2 * (q % 2):2 * (q % 2) + 2, :]))
                    if after:
                        after(2 * q)
                        after(2 * q + 1)
                steps.end(name)

            act.sem_inc(kv_stored[0], 16)
            act.sem_inc(kv_stored[1], 16)
            act.wait_ge(eps_set, 1)
            for q in range(4):
                act.wait_ge(mem_in[q], 16)
                steps.done(nc.scalar.activation(square[:, 4 * q:4 * q + 4, :].rearrange("p a b -> p (a b)"),
                                                mem[:, 4 * q:4 * q + 4, :].rearrange("p a b -> p (a b)"), ACT.Square))
            rms("mem_norm")
            act.wait_ge(cond_in, 16)
            steps.done(nc.scalar.activation(cond_silu[:], cond[:], ACT.Silu))
            act.drain()
            steps.wait(dve=1)
            steps.done(nc.scalar.copy(cond_pair[:, :, 0:4:2], cond_silu[:]))
            steps.end("cond")
            for j in range(RING):
                split(STAGES[0], 0, j)
            pair(a_hi, "mem_pair")
            act.wait_ge(consts_in, 64)
            steps.wait(dve=1)
            steps.done(nc.scalar.activation(lam[:, 1, :], lam[:, 0, :], ACT.Exp, scale=-1.0))
            steps.end("lam")

            stored = [Count(), Count()]
            for c in stored:
                c.v = 16

            def store(dst, tokens):
                def group(i, g):
                    act.wait_ge(kv_stored[g], i * 16 + stored[g].v)
                    nc.scalar.copy(kv_stage[:, g, :], acc_f(g)).then_inc(acc_free, 1)
                    act.drain()
                    if tokens:
                        out = dst.rearrange("p (t n) -> p t n", t=2)[:, :, bass.ds(i * (2 * NCOL) + g * NCOL, NCOL)]
                        src = kv_stage[:, g, :].rearrange("p (t n) -> p t n", t=2)
                    else:
                        out, src = dst[:, bass.ds(i * (8 * T) + g * (4 * T), 4 * T)], kv_stage[:, g, :]
                    nc.scalar.dma_start(out, src).then_inc(kv_stored[g], 16)
                    ran(act.nop())
                return group

            run("mem_k", store(t["mem_k"], False))
            for c in stored:
                c.v += 32
            run("mem_v", store(t["mem_v"], True))
            steps.end("mod")

            pair(a_hi, "ctx_pair")

            def conv_silu(dst):
                def group(i, g):
                    to_buffer(ACT.Copy)(i, g)
                    act.wait_ge(dve_done, dve.add())
                    ran(nc.scalar.activation(dst[:, 4 * g:4 * g + 4, :].rearrange("p a b -> p (a b)"), flat(buf_b),
                                             ACT.Silu))
                return group

            def values(i, g):
                for tt in range(2):
                    mm = nc.scalar.copy(va[:, tt, 2 * g:2 * g + 2, 0:MLSTM_D],
                                        acc[:, 2 * g + tt, :].rearrange("p (h n) -> p h n", h=2))
                mm.then_inc(acc_free, 1)
                act.drain()
                ran(act.nop())

            run("ctx_k", conv_silu(kf))
            run("ctx_v", values)
            act.wait_ge(kv_stored[0], 16 * 5)
            act.wait_ge(kv_stored[1], 16 * 5)
            for tt in range(2):
                steps.wait(pe=1 + tt)
                steps.done(nc.scalar.copy(k_tok[:, tt, :], acc_f(tt)))
            steps.wait(dve=2)
            steps.done(nc.scalar.activation(rows[:, 8:10, :], rows[:, 6:8, :], ACT.Exp))
            for r in range(8):
                steps.wait(pe=4 + r)
                steps.done(nc.scalar.activation(state[:, r, :, :], acc[:, 2 * (r % 2):2 * (r % 2) + 2, 0:VA], ACT.Copy,
                                                scale=MLSTM_D ** -0.5))
            steps.end("ctx_gates")
            pair(a_hi, "lat_pair")

            run("lat_k", conv_silu(kf))
            run("lat_v", values)
            steps.wait(dve=2)
            nc.scalar.activation(rows[:, 8:10, :], rows[:, 6:8, :], ACT.Exp)
            steps.done(nc.scalar.activation(rows[:, 10:12, :], rows[:, 0:2, :], ACT.Exp))
            run("lat_q", conv_silu(qf))
            steps.end("lat_gates")
            for r in range(8):
                d, h = divmod(r, 4)
                steps.wait(dve=3 * r + 1)
                for j in range(2):
                    mm = nc.scalar.activation(buf_b[:, j, :], buf_a[:, j, :], ACT.Exp,
                                              bias=columns[:, (4 + d) * 2 + j, h:h + 1])
                steps.done(mm)
            steps.end("mlstm")
            act.wait_ge(dve_step, AFTER["mlstm"]["dve"])
            run("lat_o", with_dve(to_buffer(ACT.Tanh, 0.5)))
            run("pool_u", to_tokens(pool_tok))
            steps.wait(dve=1)
            steps.done(nc.scalar.activation(tiny[:, 0:8], moments[:, 0:8, 1], ACT.Sqrt, bias=tiny[:, 20:21]))
            for half in range(2):
                steps.wait(pe=1 + half)
                for c in range(4):
                    mm = nc.scalar.activation(h_feat[:, 4 * half + c, :],
                                              msc[:, 2 + c // 2, (c % 2) * T:(c % 2 + 1) * T], ACT.Copy,
                                              scale=col("mh_norm_g", 4 * half + c))
                steps.done(mm)
            steps.end("mh_norm")
            for half in range(2):
                steps.wait(pe=1 + half)
                steps.done(nc.scalar.copy(pool_feat[:, 4 * half:4 * half + 4, :].rearrange("p a b -> p (a b)"),
                                          msc[:, 0:2, :].rearrange("p a b -> p (a b)")))
            for half in range(2):
                steps.wait(pe=3 + half)
                for c in range(4):
                    mm = nc.scalar.activation(pool_y[:, 4 * half + c, :],
                                              msc[:, c // 2, (c % 2) * T:(c % 2 + 1) * T], ACT.Copy,
                                              scale=col("pool_scale", 4 * half + c))
                steps.done(mm)
            steps.end("pool")
            run("mlstm_z", gate_to_pair(ACT.Silu, b_hi))
            run("pool_z", gate_to_pair(ACT.Silu, b_hi, chunk=8))

            def modulated(layer):
                def group(i, g):
                    for m in range(4):
                        mm = nc.scalar.activation(buf_a[:, m, :], acc[:, 2 * g + m // 2, (m % 2) * T:(m % 2 + 1) * T],
                                                  ACT.Copy,
                                                  scale=mod[:, bass.ds(i * 8 + (48 * layer + 32 + 4 * g + m), 1), 0])
                    mm.then_inc(acc_free, 1)
                    act.drain()
                    ran(act.nop())
                return group

            def with_squares(group):
                def wrapped(i, g):
                    group(i, g)
                    act.wait_ge(dve_done, dve.add())
                    ran(nc.scalar.activation(both, flat(x)[:, bass.ds(i * (8 * T) + g * (4 * T), 4 * T)], ACT.Square))
                    dve.add()
                return wrapped

            def affine(layer, c):
                return nc.scalar.activation(x[:, c, :], x[:, c, :], ACT.Identity, bias=col("post_ln_b", 16 * layer + c),
                                            scale=col("post_ln_g", 16 * layer + c))

            run("even_out", with_squares(modulated(0)))
            layer_norm("ln0")
            pair(a_hi, "sgu_pair", after=lambda c: affine(0, c))

            run("sgu_v", to_tokens(sgu_tok))
            steps.wait(pe=1)
            steps.done(nc.scalar.copy(row_sum[:].rearrange("p a b -> p (a b)"),
                                      msc[:, 0:2, :].rearrange("p a b -> p (a b)")))
            steps.wait(dve=1)
            steps.done(nc.scalar.activation(tiny[:, 0:2], moments[:, 0:2, 1], ACT.Sqrt, bias=tiny[:, 20:21]))
            steps.end("sgu_mix")
            act.wait_ge(dve_step, AFTER["sgu_mix"]["dve"])
            run("sgu_u", with_dve(to_buffer(ACT.Copy)))
            run("sgu_z", gate_to_pair(ACT.Silu, b_hi))
            run("odd_out", with_squares(modulated(1)))
            layer_norm("ln1")
            for q in range(4):
                steps.wait(dve=(1, 2, 4, 6)[q])
                buf = buf_a if q % 2 == 0 else buf_c
                for m in range(4):
                    c = 4 * q + m
                    mm = nc.scalar.activation(buf[:, m, :], x[:, c, :], ACT.Square, bias=col("post_ln_b", 16 + c),
                                              scale=col("post_ln_g", 16 + c))
                steps.done(mm)
                act.drain()
                for m in range(4):
                    affine(1, 4 * q + m)
            rms("mix_norm")
            pair(a_hi, "mix_pair")

            steps.wait(dve=1)
            nc.scalar.activation(angle[:, 2, :], angle[:, 1, :], ACT.Sin, scale=col("rot_sign", 0))
            steps.done(nc.scalar.activation(angle[:, 3, :], angle[:, 1, :], ACT.Sin, scale=0.5))
            steps.end("angles")

            def halves(i, g):
                for a in range(2):
                    nc.scalar.copy(both[64 * a:64 * a + 64, :], acc_f(g)[64 - 64 * a:128 - 64 * a, :])
                act.drain()
                ran(act.nop())
                dve.add()

            run("ret_q", halves)
            run("ret_k", halves)
            run("ret_v", to_tokens(v_ret))
            for h in range(RET_H):
                steps.wait(pe=2 * h + 3 if h < RET_H - 1 else 2 * h + 2)
                steps.done(nc.scalar.copy(v_ret[:, :, h * RET_V:(h + 1) * RET_V],
                                          acc[:, 2 * (h % 2):2 * (h % 2) + 2, 0:RET_V]))
            steps.wait(dve=9)
            steps.done(nc.scalar.activation(tiny[:, 0:16], moments[:, 0:16, 1], ACT.Sqrt, bias=tiny[:, 20:21]))
            for q in range(4):
                steps.wait(pe=17 + q)
                for c in range(4):
                    mm = nc.scalar.activation(ret_feat[:, 4 * q + c, :],
                                              msc[:, 2 * (q % 2) + c // 2, (c % 2) * T:(c % 2 + 1) * T], ACT.Copy,
                                              scale=col("ret_gn", 4 * q + c))
                steps.done(mm)
            steps.end("retention")
            run("ret_g", gate_to_pair(ACT.Silu, b_hi))
            run("ret_proj", to_slab(merged))
            run("merge_a", with_dve(to_buffer(ACT.Tanh, 0.5)))
            run("rnn_x", with_dve(to_buffer(ACT.Copy)))
            act.wait_ge(dve_done, DVE_DONE["rnn_x"])
            for c in range(DC):
                steps.wait(pe=c + 1)
                if c >= 2:
                    steps.wait(dve=c - 1)
                nc.scalar.activation(buf_a[:, c % 2, :], msc[:, c % 2, 0:T], ACT.Tanh, bias=lam[:, 1, c:c + 1], scale=0.5)
                steps.done(nc.scalar.activation(buf_b[:, c % 2, :], msc[:, c % 2, T:2 * T], ACT.Tanh,
                                                bias=lam[:, 2, c:c + 1], scale=0.5))
                act.drain()
                nc.scalar.activation(buf_c[:, c % 2, :], buf_a[:, c % 2, :], ACT.Tanh, bias=lam[:, 0, c:c + 1],
                                     scale=lam[:, 0, c:c + 1])
                steps.done(nc.scalar.activation(rec_a[:, c, :], buf_a[:, c % 2, :], ACT.Exp, bias=lam[:, 3, c:c + 1],
                                                scale=lam[:, 3, c:c + 1]))
            steps.wait(dve=16)
            for q in range(4):
                part = ratio[:, 4 * q:4 * q + 4, :].rearrange("p a b -> p (a b)")
                steps.done(nc.scalar.activation(part, part, ACT.Sqrt, scale=2.0))
            steps.end("rglru")
            run("rnn_y", gate_to_pair(ACT.Gelu_apprx_tanh, b_hi))
            run("merge_b", to_slab(sig_b, ACT.Tanh, 0.5))
            run("rnn_proj", gate_to_pair(ACT.Copy, a_hi, scale=0.5))
            run("mix_out", with_squares(to_buffer(ACT.Copy)))
            rms("xa_norm")
            pair(a_hi, "xa_pair")

            run("xa_q", to_slab(xa_qf))
            for h in range(XA_H):
                steps.wait(dve=2 * h + 1)
                for tt in range(2):
                    mm = nc.scalar.activation(prob[:, tt, :], msc[:, 0, tt * T:(tt + 1) * T], ACT.Exp,
                                              bias=soft[:, 2 + tt:3 + tt], scale=XA_D ** -0.5,
                                              accum_out=soft[:, 4 + tt:5 + tt])
                steps.done(mm)
                steps.wait(pe=3 * h + 2)
                steps.done(nc.scalar.copy(flat(prob_t), msc[:, 1, :]))
                steps.wait(pe=3 * h + 3)
                steps.done(nc.scalar.copy(b_hi[:, 4 * h:4 * h + 4, :].rearrange("p a b -> p (a b)"),
                                          msc[:, 2:4, :].rearrange("p a b -> p (a b)")))
            steps.end("attention")
            run("xa_o", with_squares(to_buffer(ACT.Copy)))
            rms("ffn_norm")
            pair(a_hi, "ffn_pair")

            def gate_and_value(i, g):
                dst = buf_b if g == 0 else buf_c
                for m in range(4):
                    at_ = FC * g + m
                    mm = nc.scalar.activation(dst[:, m, :], acc[:, 2 * g + m // 2, (m % 2) * T:(m % 2 + 1) * T],
                                              ACT.Identity, bias=prm[:, bass.ds(i * 4 + (COL["ffn_conv_b"] + at_), 1)],
                                              scale=prm[:, bass.ds(i * 4 + (COL["ffn_conv_w"] + 4 * FC + at_), 1)])
                ran(mm)
                act.wait_ge(dve_done, dve.add())
                if g == 0:
                    ran(nc.scalar.activation(flat(buf_b), flat(buf_b), ACT.Silu))
                else:
                    ran(nc.scalar.copy(flat(h_hi)[:, bass.ds(i * (4 * T), 4 * T)], flat(buf_c)))

            run("ffn_up", gate_and_value)
            run("ffn_down", with_squares(to_buffer(ACT.Copy)))
            rms("final")

        @block.vector
        def _(dve):
            steps = Steps(dve, "dve", step_sems)
            done, act_at = Count(), Count()
            vec = nc.vector

            def split(stage, i, j):
                u = stage.u0 + j
                slot = u % RING
                dve.wait_ge(hi_done, i * stage.n + (u + 1))
                vec.tensor_tensor(w_lo[:, slot], raw[:, slot], w_hi[:, slot].bitcast(F32),
                                  ALU.subtract).then_inc(lo_done, 1)

            def ran(instruction):
                instruction.then_inc(dve_done, 1)
                done.add()

            def gates_out(i, g, n_used):
                dve.wait_ge(unit_used, n_used)
                vec.tensor_scalar(gate_tmp[:, 0, :], msc[:, 2, 0:T], col("gate_bias", 0), None, ALU.add)
                dve.drain()
                z = gate_tmp[64:P, 0, :]
                steps.done(vec.scalar_tensor_tensor(gate_tmp[64:P, 1, :], z, -1.0, z, ALU.mult, ALU.max))
                steps.wait(act=1)
                log1p(gate_tmp[64:P, 3, :], gate_tmp[64:P, 2, :], gate_tmp[64:P, 1, :], gate_tmp[64:P, 4, :])
                vec.scalar_tensor_tensor(z, z, 0.0, gate_tmp[64:P, 3, :], ALU.min, ALU.subtract)
                dve.drain()

            def run(name, group, between=None):
                stage = STAGE[name]

                def finish(i, g, n_used):
                    group(i, g)
                    if g == 0 and between:
                        between()

                for i, last in stage_rounds(dve, stage, (done, stage.dve), (act_at, stage.act)):
                    walk(stage, i, split, {"w": finish, "a": lambda i, g, n: None, "x": gates_out}, last)

            def wait_act(n=1):
                dve.wait_ge(act_done, act_at.add(n))

            def none(n=1):
                def group(i, g):
                    act_at.add(n)
                return group

            def bcast(tile, n):
                return tile[:].unsqueeze(1).to_broadcast([P, n, T])

            def reciprocal_of_root(n):
                steps.wait(act=n)
                vec.reciprocal(rstd[:], spare[:])
                dve.drain()

            def pair(hi, lo, make, name, before=None):
                def low(q):
                    steps.wait(act=q + 1)
                    vec.tensor_tensor(lo[:, 2 * q:2 * q + 2, :], buf_a[:, 2 * (q % 2):2 * (q % 2) + 2, :],
                                      hi[:, 2 * q:2 * q + 2, :].bitcast(F32), ALU.subtract).then_inc(pair_ready, 1)

                for q in range(8):
                    dve.drain()
                    if before:
                        before(2 * q, 2)
                    for c in range(2):
                        mm = make(buf_a[:, 2 * (q % 2) + c, :], 2 * q + c)
                    steps.done(mm)
                    if q:
                        low(q - 1)
                low(7)
                steps.end(name)

            def rms_of(slab, weight):
                def make(out, c):
                    return vec.scalar_tensor_tensor(out, slab[:, c, :], col(weight, c), rstd[:], ALU.mult, ALU.mult)
                return make

            def modulate(slab, layer, which):
                def make(out, c):
                    return vec.tensor_scalar(out, slab[:, c, :], mod[:, 48 * layer + 16 + c, which:which + 1],
                                             mod[:, 48 * layer + c, which:which + 1], ALU.mult, ALU.add)
                return make

            def log1p(out, e, t1, t2):
                vec.tensor_scalar(t1, e, 2.0, None, ALU.add)
                dve.drain()
                vec.reciprocal(t1, t1)
                dve.drain()
                vec.tensor_tensor(t1, t1, e, ALU.mult)
                dve.drain()
                vec.tensor_tensor(t2, t1, t1, ALU.mult)
                dve.drain()
                vec.tensor_scalar(out, t2, 1.0 / 17, None, ALU.mult)
                for n in (15, 13, 11, 9, 7, 5, 3):
                    dve.drain()
                    vec.scalar_tensor_tensor(out, out, 1.0 / n, t2, ALU.add, ALU.mult)
                dve.drain()
                vec.scalar_tensor_tensor(out, out, 1.0, t1, ALU.add, ALU.mult)
                dve.drain()
                vec.tensor_scalar(out, out, 2.0, None, ALU.mult)
                dve.drain()

            dve.sem_inc(lo_done, RING)
            vec.memset(tiny[:, 20:21], LN_EPS)
            vec.memset(tiny[:, 21:22], RMS_EPS)
            dve.drain().then_inc(eps_set, 1)
            for q in range(4):
                steps.wait(act=q + 1)
                steps.done(vec.tensor_reduce(buf_b[:, q, :], square[:, 4 * q:4 * q + 4, :].rearrange("p c t -> p t c"),
                                             AX, ALU.add))
            for q in range(4):
                dve.wait_ge(mem_in[q], 16)
            reciprocal_of_root(5)
            steps.end("mem_norm")
            steps.done(vec.memset(cond_pair[:].bitcast(F32), 0.0))
            steps.wait(act=2)
            steps.done(vec.tensor_tensor(cond_pair[:, :, 1:4:2], cond_silu[:], cond_pair[:, :, 0:4:2].bitcast(F32),
                                         ALU.subtract))
            steps.end("cond")
            for j in range(RING):
                split(STAGES[0], 0, j)
            dve.wait_ge(consts_in, 64)
            pair(a_hi, a_lo, rms_of(mem, "norm_mem"), "mem_pair")
            lmb = prm[:, COL["rg_lambda"]:COL["rg_lambda"] + 16]
            steps.done(vec.scalar_tensor_tensor(lam[:, 0, :], lmb, -1.0, lmb, ALU.mult, ALU.max))
            steps.wait(act=1)
            log1p(lam[:, 2, :], lam[:, 1, :], lam[:, 0, :], lam[:, 3, :])
            vec.tensor_scalar(lam[:, 0, :], lmb, -1.0, 0.0, ALU.mult, ALU.max)
            dve.drain()
            vec.tensor_tensor(lam[:, 0, :], lam[:, 0, :], lam[:, 2, :], ALU.add)
            dve.drain()
            vec.tensor_scalar(lam[:, 3, :], lam[:, 0, :], -4.0, None, ALU.mult)
            dve.drain()
            vec.tensor_scalar(lam[:, 0, :], lam[:, 3, :], -1.0, None, ALU.mult)
            vec.tensor_scalar(lam[:, 1, :], prm[:, COL["rg_b_a"]:COL["rg_b_a"] + 16], 0.5, None, ALU.mult)
            vec.tensor_scalar(lam[:, 2, :], prm[:, COL["rg_b_x"]:COL["rg_b_x"] + 16], 0.5, None, ALU.mult)
            steps.end("lam")
            run("mem_k", none())
            run("mem_v", none())
            def make_mod(layer):
                part = mod[:, 48 * layer:48 * layer + 48, :]
                rows4 = msc[:, 3, 192 * layer:192 * layer + 192].rearrange("p (c n) -> p c n", n=4)
                vec.tensor_copy(part, rows4[:, :, 0:4:2])
                dve.drain()
                vec.tensor_tensor(part, part, rows4[:, :, 1:4:2], ALU.add)
                dve.drain()
                bias = prm[:, COL["ada_b"] + 48 * layer:COL["ada_b"] + 48 * layer + 48]
                vec.tensor_tensor(part, part, bias.unsqueeze(2).to_broadcast([P, 48, 2]), ALU.add)
                dve.drain()
                scale = mod[:, 48 * layer + 16:48 * layer + 32, :]
                vec.tensor_scalar(scale, scale, 1.0, None, ALU.add)
                dve.drain()

            steps.wait(pe=1)
            make_mod(0)
            steps.done(dve.drain())
            steps.end("mod")

            dve.wait_ge(ctx_in, 16)
            dve.wait_ge(unit_used, used(STAGE["mem_v"]))
            pair(a_hi, a_lo, modulate(ctx_x, 0, 1), "ctx_pair")

            def conv3(dst, src, weight, c, middle):
                name, n = weight
                taps = ((1, 0), (0, -1), (2, 1)) if middle else ((2, 0), (1, -1), (0, -2))
                for m in range(4):
                    if middle:
                        vec.tensor_scalar(dst[:, m, :], src[:, m, :], col(name, c + n + m), None, ALU.mult)
                    else:
                        vec.tensor_scalar(dst[:, m, :], src[:, m, :], col(name, c + 2 * n + m), col("ffn_conv_b", c + m),
                                          ALU.mult, ALU.add)
                for tap, shift in taps[1:]:
                    dve.drain()
                    for m in range(4):
                        a, b = (slice(-shift, T), slice(0, T + shift)) if shift < 0 else (slice(0, T - shift), slice(shift, T))
                        mm = vec.scalar_tensor_tensor(dst[:, m, a], src[:, m, b], col(name, c + tap * n + m), dst[:, m, a],
                                                      ALU.mult, ALU.add)
                return mm

            def conv_qk(first):
                def group(i, g):
                    wait_act()
                    ran(conv3(buf_b, buf_a, ("conv_qk", 16), first + 4 * g, True))
                    act_at.add()
                return group

            run("ctx_k", conv_qk(8))
            def decays():
                for d in range(2):
                    vec.tensor_copy(rows[:, d, :], gate_tmp[32 * d:32 * d + 4, 0, :])
                    vec.tensor_copy(rows[:, 12 + d, :], gate_tmp[64 + 32 * d:68 + 32 * d, 0, :])
                dve.drain()
                vec.tensor_tensor_scan(rows[:, 2, :], log_f[:, 0:T], log_f[:, 0:T], 0.0, ALU.add, ALU.bypass)
                vec.tensor_tensor_scan(rows[:, 3, ::-1], log_f[:, T:2 * T][:, ::-1], log_f[:, T:2 * T][:, ::-1], 0.0,
                                       ALU.add, ALU.bypass)
                dve.drain()
                vec.tensor_tensor(rows[:, 4:6, :], rows[:, 0:2, :], rows[:, 2:4, :], ALU.subtract)
                dve.drain()

            log_f = rows[:, 12:14, :].rearrange("p a b -> p (a b)")

            def ctx_rows():
                decays()
                vec.tensor_reduce(small[:, 0:2], rows[:, 4:6, :], AX, ALU.max)
                dve.drain()
                vec.tensor_scalar(small[:, 0:2], small[:, 0:2], 0.0, None, ALU.max)
                dve.drain()
                for d in range(2):
                    end = T - 1 if d == 0 else 0
                    vec.tensor_tensor(small[:, 2 + d:3 + d], rows[:, 2 + d, end:end + 1], small[:, d:d + 1], ALU.add)
                    mm = vec.tensor_scalar(rows[:, 6 + d, :], rows[:, 4 + d, :], small[:, d:d + 1], None, ALU.subtract)
                steps.done(mm)

            run("ctx_v", none(), between=ctx_rows)
            steps.wait(pe=3)
            vec.tensor_copy(columns[:, 0:4, :].rearrange("p a b -> p (a b)"), msc[:, 0, 0:16])
            vec.memset(va[:, :, :, MLSTM_D:VA], 1.0)
            dve.drain()
            dve.wait_ge(act_done, ACT_DONE["ctx_v"])
            for r in range(8):
                d, h = divmod(r, 4)
                buf = flat(buf_b) if r % 2 == 0 else flat(buf_c)
                if r >= 2:
                    steps.wait(pe=4 + r - 2)
                for tt in range(2):
                    mm = vec.tensor_scalar(buf[:, tt * VA:(tt + 1) * VA], va[:, tt, h, :], columns[:, 2 * d + tt, h:h + 1],
                                           None, ALU.mult)
                steps.done(mm)
            steps.end("ctx_gates")
            dve.wait_ge(x_in, 16)
            dve.wait_ge(unit_used, used(STAGE["ctx_v"]))
            pair(a_hi, a_lo, modulate(x, 0, 0), "lat_pair")

            run("lat_k", conv_qk(8))

            def lat_rows():
                decays()
                vec.tensor_tensor_scan(rows[:, 14, :], rows[:, 4, :], rows[:, 4, :], small[:, 2:3], ALU.max, ALU.bypass)
                vec.tensor_tensor_scan(rows[:, 15, ::-1], rows[:, 5, ::-1], rows[:, 5, ::-1], small[:, 3:4], ALU.max, ALU.bypass)
                vec.tensor_copy(rows[:, 12:14, :], rows[:, 4:6, :])
                dve.drain()
                for d in range(2):
                    vec.tensor_scalar(rows[:, 6 + d, :], rows[:, 14 + d, :], small[:, 2 + d:3 + d], -1.0, ALU.subtract, ALU.mult)
                steps.done(vec.scalar_tensor_tensor(rows[:, 0:2, :], rows[:, 2:4, :], -1.0, rows[:, 14:16, :], ALU.mult,
                                                    ALU.subtract))

            run("lat_v", none(), between=lat_rows)
            run("lat_q", conv_qk(0))
            dve.wait_ge(rows_turned, 4)
            make_mod(1)
            steps.wait(pe=1)
            steps.done(vec.tensor_copy(columns[:, 0:12, :].rearrange("p a b -> p (a b)"), msc[:, 0, 0:48]))
            steps.end("lat_gates")
            dve.wait_ge(mask_in, 32)
            num = flat(buf_a)
            for r in range(8):
                d, h = divmod(r, 4)
                steps.wait(pe=2 * r + 1)
                dve.drain()
                steps.done(vec.tensor_tensor(buf_a[:, 0:2, :], mask[:, d, :, :],
                                             msc[:, 1, 0:T].unsqueeze(1).to_broadcast([P, 2, T]), ALU.subtract))
                steps.wait(act=r + 1)
                steps.done(vec.scalar_tensor_tensor(buf_c[:, 0:2, :].rearrange("p a b -> p (a b)"), msc[:, 0, :],
                                                    MLSTM_D ** -0.5, buf_b[:, 0:2, :].rearrange("p a b -> p (a b)"),
                                                    ALU.mult, ALU.mult))
                steps.wait(pe=2 * r + 2)
                for tt in range(2):
                    vec.tensor_scalar(num[:, tt * VA:(tt + 1) * VA], acc[:, 2 + tt, 0:VA],
                                      columns[:, 2 * d + tt, h:h + 1], None, ALU.mult)
                dve.drain()
                for tt in range(2):
                    vec.tensor_tensor(num[:, tt * VA:(tt + 1) * VA], num[:, tt * VA:(tt + 1) * VA], acc[:, tt, 0:VA],
                                      ALU.add)
                dve.drain()
                den = num[:, 0:2 * VA].rearrange("p (a b) -> p a b", a=2)[:, :, MLSTM_D]
                vec.scalar_tensor_tensor(tiny[:, 0:2], den, -1.0, den, ALU.mult, ALU.max)
                dve.drain()
                vec.tensor_tensor(tiny[:, 0:2], tiny[:, 0:2], columns[:, 4 + 2 * d:6 + 2 * d, h], ALU.max)
                dve.drain()
                vec.reciprocal(tiny[:, 2:4], tiny[:, 0:2])
                dve.drain()
                vec.tensor_scalar(tiny[:, 2:4], tiny[:, 2:4], 0.5, None, ALU.mult)
                dve.drain()
                for tt in range(2):
                    out = h_tok[:, tt, h * MLSTM_D:(h + 1) * MLSTM_D]
                    n = num[:, tt * VA:tt * VA + MLSTM_D]
                    if d == 0:
                        mm = vec.tensor_scalar(out, n, tiny[:, 2 + tt:3 + tt], None, ALU.mult)
                    else:
                        mm = vec.scalar_tensor_tensor(out, n, tiny[:, 2 + tt:3 + tt], out, ALU.mult, ALU.add)
                steps.done(mm)
            steps.end("mlstm")

            def output_gate(i, g):
                wait_act()
                part = h_tok[:, :, g * NCOL:(g + 1) * NCOL]
                ran(vec.scalar_tensor_tensor(part, buf_a[:].rearrange("p (a b) t -> p a (b t)", a=2), 1.0, part,
                                             ALU.add, ALU.mult))

            run("lat_o", output_gate)
            dve.drain()
            run("pool_u", none())
            for n in range(8):
                vec.bn_stats(stats[:, n, :], h_tok[:, n // 4, (n % 4) * MLSTM_D:(n % 4 + 1) * MLSTM_D])
            dve.drain()
            for n in range(8):
                mm = vec.bn_aggr(moments[:, n, :], stats[:, n, :])
            steps.done(mm)
            steps.wait(act=1)
            vec.reciprocal(tiny[:, 8:16], tiny[:, 0:8])
            dve.drain()
            for n in range(8):
                part = h_tok[:, n // 4, (n % 4) * MLSTM_D:(n % 4 + 1) * MLSTM_D]
                mm = vec.tensor_scalar(part, part, moments[:, n, 0:1], tiny[:, 8 + n:9 + n], ALU.subtract, ALU.mult)
            steps.done(mm)
            steps.end("mh_norm")
            steps.end("pool")

            def gate_to_pair(factor, hi, lo, chunk=0):
                def group(i, g):
                    wait_act()
                    at_ = i * (8 * T) + g * (4 * T)
                    ran(vec.tensor_tensor(flat(buf_b), flat(buf_a), flat(factor)[:, bass.ds(at_, 4 * T)], ALU.mult))
                    wait_act()
                    at_ = chunk * T + i * (8 * T) + g * (4 * T)
                    vec.tensor_tensor(flat(lo)[:, bass.ds(at_, 4 * T)], flat(buf_b),
                                      flat(hi)[:, bass.ds(at_, 4 * T)].bitcast(F32), ALU.subtract).then_inc(pair_ready, 1)
                return group

            dve.wait_ge(act_step, AFTER["pool"]["act"])
            run("mlstm_z", gate_to_pair(h_feat, b_hi, b_lo))
            run("pool_z", gate_to_pair(pool_y, b_hi, b_lo, chunk=8))

            def residual(scale, with_mean=False):
                def group(i, g):
                    wait_act()
                    part = flat(x)[:, bass.ds(i * (8 * T) + g * (4 * T), 4 * T)]
                    ran(vec.scalar_tensor_tensor(part, part, scale, flat(buf_a), ALU.mult, ALU.add))
                    at_ = i * (2 * T) + g * T
                    if with_mean:
                        dve.drain()
                        vec.tensor_reduce(flat(buf_c)[:, bass.ds(at_, T)], part.rearrange("p (c t) -> p t c", t=T), AX, ALU.add)
                    wait_act()
                    ran(vec.tensor_reduce(flat(buf_b)[:, bass.ds(at_, T)], buf_a[:].rearrange("p c t -> p t c"), AX, ALU.add))
                return group

            def layer_norm(name):
                steps.wait(pe=1)
                vec.tensor_scalar(mean[:], msc[:, 1, 0:T], 1.0 / D, None, ALU.mult)
                dve.drain()
                vec.tensor_tensor(rstd[:], mean[:], mean[:], ALU.mult)
                dve.drain()
                steps.done(vec.scalar_tensor_tensor(spare[:], msc[:, 0, 0:T], 1.0 / D, rstd[:], ALU.mult, ALU.subtract))
                steps.wait(act=1)
                vec.reciprocal(rstd[:], rstd[:])
                steps.end(name)

            def normalised(c, n):
                part = x[:, c:c + n, :]
                vec.tensor_tensor(part, part, bcast(mean, n), ALU.subtract)
                dve.drain()
                mm = vec.tensor_tensor(part, part, bcast(rstd, n), ALU.mult)
                dve.drain()
                return mm

            lng = prm[:, COL["post_ln_g"]:COL["post_ln_g"] + 16]
            lnb = prm[:, COL["post_ln_b"]:COL["post_ln_b"] + 16]
            vec.tensor_tensor(both_affine[:, 0, :], lng, mod[:, 64:80, 0], ALU.mult)
            vec.tensor_tensor(both_affine[:, 1, :], lnb, mod[:, 64:80, 0], ALU.mult)
            dve.drain()
            vec.tensor_tensor(both_affine[:, 1, :], both_affine[:, 1, :], mod[:, 48:64, 0], ALU.add)
            dve.drain()

            def affine(out, c):
                return vec.tensor_scalar(out, x[:, c, :], both_affine[:, 0, c:c + 1], both_affine[:, 1, c:c + 1],
                                         ALU.mult, ALU.add)

            run("even_out", residual(ALPHA, with_mean=True))
            layer_norm("ln0")
            pair(a_hi, a_lo, affine, "sgu_pair", before=normalised)

            run("sgu_v", none())
            dve.wait_ge(act_done, ACT_DONE["sgu_v"])
            for n in range(8):
                vec.bn_stats(stats[:, n, :], sgu_tok[:, n // 4, (n % 4) * NCOL:(n % 4 + 1) * NCOL])
            dve.drain()
            for tt in range(2):
                mm = vec.bn_aggr(moments[:, tt, :], stats[:, 4 * tt:4 * tt + 4, :].rearrange("p a b -> p (a b)"))
            steps.done(mm)
            steps.wait(act=2)
            vec.reciprocal(tiny[:, 2:4], tiny[:, 0:2])
            dve.drain()
            for tt in range(2):
                mm = vec.tensor_scalar(sgu_tok[:, tt, :], sgu_tok[:, tt, :], moments[:, tt, 0:1], tiny[:, 2 + tt:3 + tt],
                                       ALU.subtract, ALU.mult)
            steps.done(mm)
            for q in range(4):
                dve.drain()
                for c in range(4):
                    h = (4 * q + c) // 2
                    vec.scalar_tensor_tensor(buf_a[:, c, 0:P], row_sum[:, h, :], col("sgu_ln_b", 4 * q + c), b_sp[:, h, :],
                                             ALU.mult, ALU.add)
                dve.drain()
                steps.wait(pe=2 + q)
                for c in range(4):
                    mm = vec.scalar_tensor_tensor(
                        sgu_s[:, 4 * q + c, :].rearrange("p (n t) -> p n t", n=2),
                        msc[:, 2 + c // 2, (c % 2) * T:(c % 2 + 1) * T].rearrange("p (n t) -> p n t", n=2),
                        col("sgu_ln_g", 4 * q + c), buf_a[:, c, 0:P].unsqueeze(1).to_broadcast([P, 2, P]),
                        ALU.mult, ALU.add)
                steps.done(mm)
            steps.end("sgu_mix")
            dve.drain()

            def times_slab(i, g):
                wait_act()
                part = flat(sgu_s)[:, bass.ds(i * (8 * T) + g * (4 * T), 4 * T)]
                ran(vec.tensor_tensor(part, part, flat(buf_a), ALU.mult))

            run("sgu_u", times_slab)
            dve.drain()
            run("sgu_z", gate_to_pair(sgu_s, b_hi, b_lo))
            run("odd_out", residual(ALPHA, with_mean=True))
            layer_norm("ln1")
            dve.drain()

            def quarter_sums(q):
                steps.wait(act=q + 1)
                buf = buf_a if q % 2 == 0 else buf_c
                steps.done(vec.tensor_reduce(buf_b[:, q, :], buf[:].rearrange("p c t -> p t c"), AX, ALU.add))

            for q in range(4):
                steps.done(normalised(4 * q, 4))
                if q:
                    quarter_sums(q - 1)
            quarter_sums(3)
            reciprocal_of_root(5)
            steps.end("mix_norm")
            pair(a_hi, a_lo, rms_of(x, "norm_mix"), "mix_pair")

            dve.wait_ge(ret_in, 16)
            pos, ang = angle[:, 0, :], angle[:, 1, :]
            vec.tensor_copy(pos, ang_i[:])
            dve.drain()
            vec.tensor_scalar(ang, pos, col("inv_freq", 0), None, ALU.mult)
            dve.drain()
            vec.tensor_scalar(pos, ang, 1.0 / (2 * np.pi), None, ALU.mult)
            dve.drain()
            for magic in (ROUND, -ROUND):
                vec.tensor_scalar(pos, pos, magic, None, ALU.add)
                dve.drain()
            for part in TWO_PI_PARTS:
                vec.scalar_tensor_tensor(ang, pos, -part, ang, ALU.mult, ALU.add)
                dve.drain()
            steps.done(vec.tensor_scalar(ang, ang, PI_BELOW, -PI_BELOW, ALU.min, ALU.max))
            steps.wait(act=1)
            cos, sin = angle[:, 4, :], angle[:, 2, :]
            vec.tensor_tensor(cos, angle[:, 3, :], angle[:, 3, :], ALU.mult)
            dve.drain()
            steps.done(vec.tensor_scalar(cos, cos, -2.0, 1.0, ALU.mult, ALU.add))
            dve.drain()
            steps.end("angles")

            def rotated(slab):
                def group(i, g):
                    wait_act()
                    part = slab[:, 4 * g:4 * g + 4, :]
                    vec.tensor_tensor(part, acc_f(g).rearrange("p (c t) -> p c t", t=T), cos.unsqueeze(1).to_broadcast([P, 4, T]),
                                      ALU.mult).then_inc(acc_free, 1)
                    vec.tensor_tensor(buf_b[:], buf_a[:], sin.unsqueeze(1).to_broadcast([P, 4, T]), ALU.mult)
                    dve.drain()
                    ran(vec.tensor_tensor(part, part, buf_b[:], ALU.add))
                return group

            run("ret_q", rotated(qf))
            run("ret_k", rotated(kf))
            run("ret_v", none())
            dve.wait_ge(ret_in, 32)
            for h in range(RET_H):
                buf = buf_b if h % 2 == 0 else buf_c
                steps.wait(pe=1 if h == 0 else 2 * h)
                if h >= 2:
                    steps.wait(pe=2 * (h - 2) + 3)
                vec.scalar_tensor_tensor(buf[:, 0, :], msc[:, h % 2, 0:T], RET_QK ** -0.5, decay[:, h, :], ALU.mult, ALU.mult)
                steps.done(vec.scalar_tensor_tensor(buf[:, 1, P:T], msc[:, h % 2, T + P:2 * T], RET_QK ** -0.5,
                                                    decay[:, h, 0:P], ALU.mult, ALU.mult))
            for n in range(16):
                h, tt = divmod(n, 2)
                steps.wait(act=1 + h)
                vec.bn_stats(stats[:, n, :], v_ret[:, tt, h * RET_V:(h + 1) * RET_V])
            dve.drain()
            for n in range(16):
                mm = vec.bn_aggr(moments[:, n, :], stats[:, n, :])
            steps.done(mm)
            steps.wait(act=9)
            vec.reciprocal(lam_tmp[:], tiny[:, 0:16])
            dve.drain()
            for n in range(16):
                h, tt = divmod(n, 2)
                part = v_ret[:, tt, h * RET_V:(h + 1) * RET_V]
                mm = vec.tensor_scalar(part, part, moments[:, n, 0:1], lam_tmp[:, n:n + 1], ALU.subtract, ALU.mult)
            steps.done(mm)
            steps.end("retention")
            dve.wait_ge(act_step, AFTER["retention"]["act"])
            run("ret_g", gate_to_pair(ret_feat, b_hi, b_lo))
            run("ret_proj", none())

            def merge_first(i, g):
                wait_act()
                part = flat(merged)[:, bass.ds(i * (8 * T) + g * (4 * T), 4 * T)]
                ran(vec.scalar_tensor_tensor(part, flat(buf_a), 1.0, part, ALU.add, ALU.mult))

            run("merge_a", merge_first)
            dve.drain()

            def conv4(i, g):
                wait_act()

                def weight(tap, m):
                    return prm[:, bass.ds(i * 8 + (COL["rnn_conv_w"] + 16 * tap + 4 * g + m), 1)]

                def part(m, start):
                    return flat(xr)[:, bass.ds(i * (8 * T) + ((4 * g + m) * T + start), T - start)]

                for m in range(4):
                    vec.tensor_scalar(part(m, 0), buf_a[:, m, :], weight(3, m),
                                      prm[:, bass.ds(i * 8 + (COL["rnn_conv_b"] + 4 * g + m), 1)], ALU.mult, ALU.add)
                for shift in (1, 2, 3):
                    dve.drain()
                    for m in range(4):
                        mm = vec.scalar_tensor_tensor(part(m, shift), buf_a[:, m, 0:T - shift], weight(3 - shift, m),
                                                      part(m, shift), ALU.mult, ALU.add)
                ran(mm)

            run("rnn_x", conv4)
            dve.drain()
            for c in range(DC):
                steps.wait(act=2 * c + 2)
                vec.scalar_tensor_tensor(xr[:, c, :], buf_b[:, c % 2, :], 1.0, xr[:, c, :], ALU.add, ALU.mult)
                vec.tensor_scalar(mean[:], buf_c[:, c % 2, :], 1.0, None, ALU.add)
                dve.drain()
                vec.reciprocal(spare[:], mean[:])
                dve.drain()
                steps.done(vec.tensor_tensor(ratio[:, c, :], buf_c[:, c % 2, :], spare[:], ALU.mult))
            dve.drain()
            for q in range(4):
                steps.wait(act=33 + q)
                for c in range(4 * q, 4 * q + 4):
                    vec.scalar_tensor_tensor(xr[:, c, :], xr[:, c, :], 0.5, ratio[:, c, :], ALU.mult, ALU.mult)
                dve.drain()
                for c in range(4 * q, 4 * q + 4):
                    vec.tensor_tensor_scan(xr[:, c, :], rec_a[:, c, :], xr[:, c, :], 0.0, ALU.mult, ALU.add)
            dve.drain()
            steps.end("rglru")
            run("rnn_y", gate_to_pair(xr, b_hi, b_lo))
            run("merge_b", none())

            def merge_second(i, g):
                wait_act()
                at_ = i * (8 * T) + g * (4 * T)
                vec.scalar_tensor_tensor(flat(buf_b), flat(sig_b)[:, bass.ds(at_, 4 * T)], 1.0, flat(buf_a), ALU.add, ALU.mult)
                dve.drain()
                ran(vec.tensor_tensor(flat(buf_b), flat(buf_b), flat(merged)[:, bass.ds(at_, 4 * T)], ALU.add))
                wait_act()
                vec.scalar_tensor_tensor(flat(a_lo)[:, bass.ds(at_, 4 * T)], flat(buf_b), 0.5,
                                         flat(a_hi)[:, bass.ds(at_, 4 * T)].bitcast(F32), ALU.mult,
                                         ALU.subtract).then_inc(pair_ready, 1)

            run("rnn_proj", merge_second)
            run("mix_out", residual(1.0))
            reciprocal_of_root(1)
            steps.end("xa_norm")
            pair(a_hi, a_lo, rms_of(x, "norm_xa"), "xa_pair")

            run("xa_q", none())
            for h in range(XA_H):
                steps.wait(pe=3 * h + 1)
                vec.tensor_reduce(soft[:, 0:2], msc[:, 0, :].rearrange("p (a b) -> p a b", a=2), AX, ALU.max)
                dve.drain()
                steps.done(vec.tensor_scalar(soft[:, 2:4], soft[:, 0:2], -(XA_D ** -0.5), None, ALU.mult))
                steps.wait(act=3 * h + 1)
                vec.reciprocal(soft[:, 6:8], soft[:, 4:6])
                dve.drain()
                for tt in range(2):
                    mm = vec.tensor_scalar(prob[:, tt, :], prob[:, tt, :], soft[:, 6 + tt:7 + tt], None, ALU.mult)
                steps.done(mm)
                steps.wait(act=3 * h + 3)
                vec.tensor_tensor(b_lo[:, 4 * h:4 * h + 4, :].rearrange("p a b -> p (a b)"),
                                  msc[:, 2:4, :].rearrange("p a b -> p (a b)"),
                                  b_hi[:, 4 * h:4 * h + 4, :].bitcast(F32).rearrange("p a b -> p (a b)"),
                                  ALU.subtract).then_inc(pair_ready, 1)
            steps.end("attention")
            run("xa_o", residual(1.0))
            reciprocal_of_root(1)
            steps.end("ffn_norm")
            pair(a_hi, a_lo, rms_of(x, "norm_ffn"), "ffn_pair")

            def gate_and_value(i, g):
                wait_act()
                dst = buf_b if g == 0 else buf_c

                for shift in (1, 2):
                    if shift == 2:
                        dve.drain()
                    for m in range(4):
                        weight = prm[:, bass.ds(i * 4 + (COL["ffn_conv_w"] + 2 * FC * (2 - shift) + FC * g + m), 1)]
                        first = (m % 2) * T
                        mm = vec.scalar_tensor_tensor(dst[:, m, shift:T],
                                                      acc[:, 2 * g + m // 2, first:first + T - shift], weight,
                                                      dst[:, m, shift:T], ALU.mult, ALU.add)
                mm.then_inc(acc_free, 1)
                if g == 0:
                    dve.drain()
                    ran(dve.drain())
                    wait_act()
                    return
                dve.drain()
                ran(vec.tensor_tensor(flat(buf_c), flat(buf_c), flat(buf_b), ALU.mult))
                wait_act()
                vec.tensor_tensor(flat(h_lo)[:, bass.ds(i * (4 * T), 4 * T)], flat(buf_c),
                                  flat(h_hi)[:, bass.ds(i * (4 * T), 4 * T)].bitcast(F32),
                                  ALU.subtract).then_inc(pair_ready, 1)

            run("ffn_up", gate_and_value)
            run("ffn_down", residual(1.0))
            reciprocal_of_root(1)
            for c in range(DC):
                mm = vec.scalar_tensor_tensor(y_out[:, c, :], x[:, c, :], col("final_norm", c), rstd[:], ALU.mult, ALU.mult)
            steps.done(mm)
            steps.end("final")


def units(w):
    k, n = w.shape
    w = w.reshape(k // (KU * P), KU, P, n // NCOL, NCOL).transpose(3, 0, 2, 1, 4)
    return np.ascontiguousarray(w).reshape(-1, P, UNIT)


def chunks(a):
    return np.ascontiguousarray(a.reshape(a.shape[0], -1, P).transpose(2, 1, 0))


def columns_of(v):
    return v.reshape(-1, P).T


def spread_heads(a):
    out = np.zeros((a.shape[0], 4, 32), a.dtype)
    out[:, :, :4] = a.reshape(a.shape[0], 4, 4)
    return out.reshape(a.shape[0], P)


def constants():
    s, q = np.arange(T)[:, None], np.arange(T)[None, :]
    seen = np.stack([s <= q, s >= q])
    mask = np.where(seen, 0.0, -1e30).astype(np.float32)
    mask = mask.reshape(2, 2, P, T).transpose(2, 0, 1, 3)
    pool = np.zeros((P, POOL_G, P))
    for g, w in enumerate(POOL_WINDOWS):
        for row in range(P // GRID_W):
            for pos in range(GRID_W):
                lo, hi = max(pos - w // 2, 0), min(pos + (w - 1 - w // 2), GRID_W - 1)
                pool[row * GRID_W + lo:row * GRID_W + hi + 1, g, row * GRID_W + pos] = 1.0 / (hi - lo + 1)
                pool[row * GRID_W + pos, g, row * GRID_W + pos] -= 1.0
    log_gamma = np.log1p(-(2.0 ** (-5.0 - np.arange(RET_H))))
    rel = np.arange(T)[None, None, :] - np.arange(P)[:, None, None]
    decay = np.where(rel >= 0, np.exp(log_gamma[None, :, None] * np.maximum(rel, 0)), 0.0)
    pick = np.zeros((4, 4, P), np.float32)
    for h in range(4):
        pick[h, h] = 1.0
    half = RET_QK // 2
    freq = np.float32(10000.0) ** (-np.arange(half, dtype=np.float32) * np.float32(2.0) / np.float32(RET_QK))
    return {
        "ident": np.eye(P, dtype=np.float32), "ones": np.ones((P, P), np.float32), "pick": pick,
        "mask": np.ascontiguousarray(mask), "pool_mat": pool.astype(np.float32), "decay": decay.astype(np.float32),
        "inv_freq": np.tile(freq.astype(np.float32), 2),
        "rot_sign": np.repeat(np.float32([-1.0, 1.0]), half),
    }


def lay_out(i):
    const = constants()
    bias = spread_heads(np.concatenate([i["b_igate"][0].reshape(1, -1), i["b_fgate"][0].reshape(1, -1)], axis=1)).T
    parts = {
        "ada_b": i["ada_b"], "post_ln_g": i["post_ln_g"], "post_ln_b": i["post_ln_b"], "conv_qk": i["conv_qk"],
        "mh_norm_g": i["mh_norm_g"], "pool_scale": i["pool_scale"], "sgu_ln_g": i["sgu_ln_g"],
        "sgu_ln_b": i["sgu_ln_b"], "norm_mix": i["norm_mix_w_2"], "ret_gn": i["ret_gn_w_2"],
        "rnn_conv_w": i["rnn_conv_w_2"], "rnn_conv_b": i["rnn_conv_b_2"], "rg_b_a": i["rg_b_a_2"],
        "rg_b_x": i["rg_b_x_2"], "rg_lambda": i["rg_lambda_2"], "norm_xa": i["norm_xa_w_2"],
        "norm_mem": i["norm_mem_w_2"], "norm_ffn": i["norm_ffn_w_2"], "ffn_conv_w": i["ffn_conv_w_2"],
        "ffn_conv_b": i["ffn_conv_b_2"], "final_norm": i["final_norm_w_2"], "inv_freq": const.pop("inv_freq"),
        "rot_sign": const.pop("rot_sign"),
    }
    params = [bias if name == "gate_bias" else columns_of(parts[name]) for name, _ in PARAM_COLUMNS]
    out = dict(const)
    out["params"] = np.ascontiguousarray(np.concatenate(params, axis=1))
    assert out["params"].shape == (P, N_PARAM)
    out["x"], out["ctx"], out["mem"] = chunks(i["x"][0]), chunks(i["ctx"][0]), chunks(i["mem_2"][0])
    out["cond"] = np.ascontiguousarray(np.stack([i["c"][0].reshape(DC, P).T, i["c_ctx"].reshape(DC, P).T], axis=2))
    out["positions"] = np.ascontiguousarray(i["positions_2"].reshape(T))

    out["w_xa_k"], out["w_xa_v"] = units(i["xa_w_k_2"][0]), units(i["xa_w_v_2"][0])
    out["w_ada"] = np.concatenate([units(i["ada_w"][0]), units(i["ada_w"][1])])

    w = i["w_in_even"][0]
    n_m = MLSTM_H * MLSTM_D
    for k, name in enumerate(("w_q", "w_k", "w_v", "w_o", "w_mlstm_z")):
        out[name] = units(w[:, k * n_m:(k + 1) * n_m])
    gate = spread_heads(w[:, 5 * n_m:5 * n_m + 16])
    out["w_gate"] = np.ascontiguousarray(gate.reshape(GATE_UNITS, UNIT // P, P, P).transpose(0, 2, 1, 3)).reshape(-1, P, UNIT)
    out["w_pool_u"] = units(w[:, 5 * n_m + 16:6 * n_m + 16])
    out["w_pool_z"] = units(w[:, 6 * n_m + 16:])
    out["pool_w"] = np.ascontiguousarray(i["pool_w"][0].reshape(POOL_G, 2, P, 256).transpose(2, 0, 1, 3)).reshape(P, 8, 256)
    out["w_even_out"] = units(i["w_out_even"][0])
    w = i["w_in_odd"][0]
    out["w_sgu_u"], out["w_sgu_v"], out["w_sgu_z"] = units(w[:, :D]), units(w[:, D:2 * D]), units(w[:, 2 * D:])
    out["w_sp"] = np.ascontiguousarray(i["w_sp"][0].transpose(2, 0, 1))
    out["b_sp"] = np.ascontiguousarray(np.broadcast_to(i["b_sp"][0][None], (P, SGU_H, SGU_CHUNK)))
    out["w_odd_out"] = units(i["w_out_odd"][0])
    w = i["w_in_2"][0]
    first = 0
    for name, width in (("w_ret_q", 1024), ("w_ret_k", 1024), ("w_ret_v", D), ("w_ret_g", D), ("w_rnn_x", D),
                        ("w_rnn_y", D), ("w_merge_a", D), ("w_merge_b", D)):
        out[name] = units(w[:, first:first + width])
        first += width
    out["rg_w"] = np.ascontiguousarray(np.stack([i["rg_w_a_2"][0], i["rg_w_x_2"][0]]).transpose(2, 0, 1, 3))
    out["w_ret_proj"], out["w_rnn_proj"] = units(i["w_proj_ret_2"][0]), units(i["w_proj_rnn_2"][0])
    out["w_mix_out"] = units(i["w_mix_out_2"][0])
    out["w_xa_q"], out["w_xa_o"] = units(i["xa_w_q_2"][0]), units(i["xa_w_o_2"][0])
    up = i["ffn_w_up_2"][0].reshape(D, 2, FF // NCOL, NCOL).transpose(0, 2, 1, 3).reshape(D, 2 * FF)
    out["w_ffn_up"] = units(up)
    out["w_ffn_down"] = units(i["ffn_w_down_2"][0])
    return out


def kernel(**inputs):
    import concourse.bacc as bacc
    from concourse.bass_utils import run_bass_kernel_spmd

    laid = lay_out({k: np.asarray(v) for k, v in inputs.items()})
    nc = bacc.Bacc("TRN2", target_bir_lowering=False, num_devices=1)
    t = {}
    for name, a in laid.items():
        t[name] = nc.dram_tensor(f"in_{name}", a.shape, mybir.dt.from_np(a.dtype), kind="ExternalInput").ap()
    t["out"] = nc.dram_tensor("out_y", (P, DC, T), F32, kind="ExternalOutput").ap()
    t["mem_k"] = nc.dram_tensor("mem_k", (P, DC * T), F32).ap()
    t["mem_v"] = nc.dram_tensor("mem_v", (P, 2 * D), F32).ap()
    build(nc, t)
    r = run_bass_kernel_spmd(nc, [{f"in_{k}": v for k, v in laid.items()}], core_ids=[0])
    y = r.results[0]["out_y"]
    return np.ascontiguousarray(y.transpose(2, 1, 0)).reshape(1, T, D)
```

```python
from contextlib import ExitStack

import numpy as np

import concourse.bass as bass
import concourse.mybir as mybir

F32 = mybir.dt.float32
F32R = mybir.dt.float32r
I32 = mybir.dt.int32
ALU = mybir.AluOpType
ACT = mybir.ActivationFunctionType
AX = mybir.AxisListType.X

P = 128
T = 256
D = 2048
DC = D // P
NCOL = 512
KU = 2
UNIT = KU * NCOL
RING = 4
MLSTM_H, MLSTM_D = 4, 256
POOL_G = 4
POOL_WINDOWS = (2, 4, 8, 16)
GRID_W = 64
SGU_H, SGU_CHUNK = 8, 128
RET_H, RET_QK, RET_V = 8, 128, 256
XA_H, XA_D = 4, 512
FF = 5632
FC = FF // P
ALPHA = float((2.0 * 2) ** 0.25)
LN_EPS, GN_EPS, RMS_EPS = 1e-5, 1e-5, 1e-6
GATE_UNITS = DC * P // UNIT
VA = MLSTM_D + 1
ROUND = 1.5 * 2 ** 23
TWO_PI_PARTS = [6.28125, 0.0019350051879882812, 3.0199159795074593e-07]
PI_BELOW = 3.1415925
SERIES = (17, 15, 13, 11, 9, 7, 5, 3)

PARAM_COLUMNS = [
    ("ada_b", 96), ("post_ln_g", 32), ("post_ln_b", 32), ("conv_qk", 48), ("mh_norm_g", 8), ("pool_scale", 8),
    ("sgu_ln_g", 16), ("sgu_ln_b", 16), ("norm_mix", 16), ("ret_gn", 16), ("rnn_conv_w", 64), ("rnn_conv_b", 16),
    ("rg_b_a", 16), ("rg_b_x", 16), ("rg_lambda", 16), ("norm_xa", 16), ("norm_mem", 16), ("norm_ffn", 16),
    ("ffn_conv_w", 3 * 2 * FC), ("ffn_conv_b", 2 * FC), ("final_norm", 16), ("gate_bias", 1), ("inv_freq", 1), ("rot_sign", 1),
]
COL = {}
_at = 0
for _name, _n in PARAM_COLUMNS:
    COL[_name] = _at
    _at += _n
N_PARAM = _at



class Stage:
    def __init__(self, name, weights, mode, iters, group_units=DC // KU, groups=2, ada=None, gate=False, act=1, dve=0, ready=0):
        self.name, self.weights, self.mode, self.iters = name, weights, mode, iters
        self.group_units, self.groups, self.ada, self.gate = group_units, groups, ada, gate
        self.act, self.dve, self.ready = act * groups, dve * groups, ready * groups
        self.n_w = groups * group_units
        self.kinds = [("w", *divmod(n, group_units), (n + 1) % group_units == 0) for n in range(self.n_w)]
        if ada is not None:
            mixed = []
            for n in range(self.n_w // 2):
                a = [("a", *divmod(3 * n + m, DC // KU), (3 * n + m + 1) % (DC // KU) == 0) for m in range(3)]
                mixed += [self.kinds[2 * n], a[0], self.kinds[2 * n + 1], a[1], a[2]]
            self.kinds = mixed
        if gate:
            at = self.kinds.index(("w", 1, 1, False))
            self.kinds[at:at] = [("x", 0, k, k == GATE_UNITS - 1) for k in range(GATE_UNITS)]
        self.n = len(self.kinds)
        self.total = self.n * iters
        assert iters == 1 or self.n % RING == 0


STAGES = [
    Stage("mem_k", "w_xa_k", "F", 2, ada=0),
    Stage("mem_v", "w_xa_v", "T", 2, ada=6),
    Stage("ctx_k", "w_k", "F", 1, ada=12, gate=True, act=2, dve=1),
    Stage("ctx_v", "w_v", "T", 1, ada=15),
    Stage("lat_k", "w_k", "F", 1, ada=18, gate=True, act=2, dve=1),
    Stage("lat_v", "w_v", "T", 1, ada=21),
    Stage("lat_q", "w_q", "F", 1, act=2, dve=1),
    Stage("lat_o", "w_o", "T", 1, act=1, dve=1),
    Stage("pool_u", "w_pool_u", "T", 1, act=1),
    Stage("mlstm_z", "w_mlstm_z", "F", 1, act=2, dve=1, ready=1),
    Stage("pool_z", "w_pool_z", "F", 1, act=2, dve=1, ready=1),
    Stage("even_out", "w_even_out", "F", 2, act=2, dve=2),
    Stage("sgu_v", "w_sgu_v", "T", 2, act=1),
    Stage("sgu_u", "w_sgu_u", "F", 1, groups=4, act=1, dve=1),
    Stage("sgu_z", "w_sgu_z", "F", 2, act=2, dve=1, ready=1),
    Stage("odd_out", "w_odd_out", "F", 2, act=2, dve=2),
    Stage("ret_q", "w_ret_q", "F", 1, act=1, dve=1),
    Stage("ret_k", "w_ret_k", "F", 1, act=1, dve=1),
    Stage("ret_v", "w_ret_v", "T", 2, act=1),
    Stage("rnn_x", "w_rnn_x", "F", 1, groups=4, act=1, dve=1),
    Stage("ret_g", "w_ret_g", "F", 2, act=2, dve=1, ready=1),
    Stage("ret_proj", "w_ret_proj", "F", 2, act=1),
    Stage("merge_a", "w_merge_a", "F", 1, groups=4, act=1, dve=1),
    Stage("rnn_y", "w_rnn_y", "F", 2, act=2, dve=1, ready=1),
    Stage("merge_b", "w_merge_b", "F", 2, act=1),
    Stage("rnn_proj", "w_rnn_proj", "F", 2, act=2, dve=1, ready=1),
    Stage("mix_out", "w_mix_out", "F", 2, act=2, dve=2),
    Stage("xa_q", "w_xa_q", "F", 2, act=1),
    Stage("xa_o", "w_xa_o", "F", 2, act=2, dve=2),
    Stage("ffn_up", "w_ffn_up", "F", 11, act=2, dve=1, ready=0.5),
    Stage("ffn_down", "w_ffn_down", "F", 2, group_units=FC // KU, act=2, dve=2),
]
_u = _g = 0
ACT_DONE, DVE_DONE = {}, {}
_a = _d = 0
for _s in STAGES:
    _s.u0, _s.g0 = _u, _g
    _s.ready = int(_s.ready)
    _u += _s.total
    _g += _s.groups * _s.iters
    _a += _s.act * _s.iters
    _d += _s.dve * _s.iters
    ACT_DONE[_s.name], DVE_DONE[_s.name] = _a, _d
STAGE = {_s.name: _s for _s in STAGES}
LAST = STAGES[-1]


SECTIONS = [
    ("mem_norm", 1, 5, 4), ("cond", 0, 2, 2), ("mem_pair", 0, 8, 8), ("lam", 0, 1, 1), ("mod", 1, 0, 1),
    ("ctx_pair", 0, 8, 8), ("ctx_gates", 11, 12, 11), ("lat_pair", 0, 8, 8), ("lat_gates", 1, 2, 4),
    ("mlstm", 16, 8, 24), ("mh_norm", 2, 3, 2), ("pool", 4, 4, 0), ("ln0", 1, 1, 1), ("sgu_pair", 0, 8, 8),
    ("sgu_mix", 5, 2, 6), ("ln1", 1, 1, 1), ("mix_norm", 1, 5, 8), ("mix_pair", 0, 8, 8), ("angles", 0, 1, 2), ("retention", 20, 13, 10),
    ("rglru", 16, 36, 16), ("xa_norm", 1, 1, 0), ("xa_pair", 0, 8, 8), ("attention", 12, 12, 8),
    ("ffn_norm", 1, 1, 0), ("ffn_pair", 0, 8, 8), ("final", 1, 1, 1),
]
BEFORE, AFTER = {}, {}
_c = dict(pe=0, act=0, dve=0)
for _name, *_n in SECTIONS:
    BEFORE[_name] = dict(_c)
    _c = {k: _c[k] + n for k, n in zip(("pe", "act", "dve"), _n)}
    AFTER[_name] = dict(_c)
class MlstmStep:
    scores = staticmethod(lambda r: r + 1 if r < 2 else 2 * r)
    results = staticmethod(lambda r: 2 * r + 3 if r < 7 else 16)
    masked = staticmethod(lambda r: r + 1 if r < 2 else 3 * r)
    weighted = staticmethod(lambda r: 3 if r == 0 else 3 * r + 2 if r < 7 else 23)
    read = staticmethod(lambda r: 3 * r + 4 if r < 7 else 24)


class XaStep:
    exponentials = staticmethod(lambda h: 1 if h == 0 else 3 * h)
    hi = staticmethod(lambda h: 3 * h + 4 if h < XA_H - 1 else 3 * h + 3)
    logits = staticmethod(lambda h: 1 if h == 0 else 3 * h - 1)
    turned = staticmethod(lambda h: 3 * h + 3 if h < XA_H - 1 else 3 * h + 2)
    result = staticmethod(lambda h: 3 * h + 4 if h < XA_H - 1 else 3 * h + 3)


MIX_AT = (6, 9, 14, 18)
TURN_AT = (10, 13, 16, 19)
RG_CHUNK_AT = {6 + 3 * c // 2: c for c in range(DC)}


def rg_act_step(c, part):
    return 2 * c + part + max(0, (c - 2) // 4)


def rg_root_step(q):
    return rg_act_step(4 * q + 5, 2) + 1 if q < 3 else rg_act_step(DC - 1, 2) + 1


PAIR = dict(mem=8, ctx=16, lat=24, even_out=28, sgu=36, odd_out=40, mix=48, ret_proj=52, rnn_proj=56, mix_out=60,
            xa=68, xa_o=72, ffn=80, ffn_down=91)


class Steps:

    def __init__(self, eng, own, sems):
        self.eng, self.own, self.sems, self.at, self.n = eng, own, sems, 0, 0

    def wait(self, **need):
        for k, n in need.items():
            self.eng.wait_ge(self.sems[k], BEFORE[SECTIONS[self.at][0]][k] + n)

    def done(self, instruction):
        instruction.then_inc(self.sems[self.own], 1)
        self.n += 1

    def end(self, name):
        assert SECTIONS[self.at][0] == name, (name, SECTIONS[self.at])
        before, after = BEFORE[name][self.own], AFTER[name][self.own]
        assert self.n == after - before, (name, self.own, self.n, after - before)
        self.n = 0
        self.at += 1


class Count:

    def __init__(self):
        self.v, self.i, self.step = 0, None, 0

    def add(self, n=1):
        self.v += n
        return self.at()

    def at(self):
        return self.v if self.i is None else self.i * self.step + self.v


def rounds(eng, n, *counts):
    before = [c.v for c, _ in counts]
    if n == 1:
        yield 0
    else:
        with eng.Fori(0, n) as i:
            for c, step in counts:
                c.i, c.step = i, step
            yield i
    for (c, step), b in zip(counts, before):
        assert c.v - b == step, (c.v - b, step)
        c.v, c.i = b + step * n, None


def build(nc, t):
    ctx = ExitStack()
    with ctx:
        at = [-(-nc.sbuf_base // 64) * 64]

        def place(name, shape, dt, offset):
            return nc.alloc_sbuf_tensor_at(name, shape, dt, offset=offset)

        def sb(name, shape, dt=F32):
            size = -(-int(np.prod(shape[1:])) * 4 // 32) * 32
            at[0] += size
            return place(name, shape, dt, at[0] - size)

        SLAB = DC * T * 4
        raw = sb("raw", [P, RING, KU, NCOL])
        w_hi = sb("w_hi", [P, RING, KU, NCOL], F32R)
        w_lo = sb("w_lo", [P, RING, KU, NCOL], F32R)
        a_hi = sb("a_hi", [P, DC, T], F32R)
        a_lo = sb("a_lo", [P, DC, T], F32R)
        x = sb("x", [P, DC, T])
        work = at[0]
        at[0] += 88 * 1024

        def wk(name, shape, offset, dt=F32):
            assert offset + int(np.prod(shape[1:])) * 4 <= 88 * 1024, name
            return place(name, shape, dt, work + offset)

        K = 1024
        mem = wk("mem", [P, DC, T], 0)
        mod_rows = wk("mod_rows", [4, 48 * P], 16 * K)
        cond_pair = wk("cond_pair", [P, DC, P], 80 * K, F32R)
        kv_stage = wk("kv_stage", [P, 2, 2 * NCOL], 72 * K)
        cond = wk("cond", [P, DC, 2], 30 * K)
        cond_silu = wk("cond_silu", [P, DC, 2], 30 * K + 128)
        square = wk("square", [P, DC, T], 32 * K)
        ctx_x = wk("ctx_x", [P, DC, T], 0)
        rows = wk("rows", [4, 16, T], 0)
        mod_rows2 = wk("mod_rows2", [4, 2, 3 * NCOL], 18 * K)
        gate_tmp = wk("gate_tmp", [P, 5, T], 40 * K - 128)
        columns = wk("columns", [P, 16, 4], 16 * K)
        small = wk("small", [4, 4], 17 * K)
        b_hi = wk("b_hi", [P, DC, T], 0, F32R)
        b_lo = wk("b_lo", [P, DC, T], 16 * K, F32R)
        kf = wk("kf", [P, 8, T], 32 * K - 128)
        qf = wk("qf", [P, 8, T], 40 * K - 128)
        va = wk("va", [P, 2, MLSTM_H, VA], 48 * K - 128)
        h_feat = wk("h_feat", [P, 8, T], 48 * K)
        state_at = 48 * K - 128 + 2 * MLSTM_H * VA * 4
        state = wk("state", [P, 8, 2, VA], state_at)
        h_tok_at = state_at + 16 * VA * 4
        h_tok = wk("h_tok", [P, 2, 4 * MLSTM_D], h_tok_at)
        k_tok = wk("k_tok", [P, 2, 4 * MLSTM_D], h_tok_at)
        mask_at = h_tok_at + 8 * K
        mask = wk("mask", [P, 2, 2, T], mask_at)
        pool_mat = wk("pool_mat", [P, POOL_G, P], mask_at + 4 * K)
        pool_tok = wk("pool_tok", [P, 2, 1024], 32 * K)
        pool_feat = wk("pool_feat", [P, 8, T], 40 * K)
        pool_y = wk("pool_y", [P, 8, T], 32 * K)
        pool_w = wk("pool_w", [P, 8, T], 57 * K)
        sgu_tok = wk("sgu_tok", [P, 2, D], 32 * K)
        sgu_s = wk("sgu_s", [P, DC, T], 48 * K)
        w_sp = wk("w_sp", [P, SGU_H, P], 64 * K)
        b_sp = wk("b_sp", [P, SGU_H, P], 68 * K)
        row_sum = wk("row_sum", [P, SGU_H, P], 72 * K)
        v_ret = wk("v_ret", [P, 2, D], 48 * K)
        ret_feat = wk("ret_feat", [P, DC, T], 64 * K)
        decay = wk("decay", [P, RET_H, T], 80 * K)
        angle = wk("angle", [P, 5, T], 0)
        ang_i = wk("ang_i", [P, T], 87 * K, I32)
        merged = wk("merged", [P, DC, T], 64 * K)
        xr = wk("xr", [P, DC, T], 32 * K)
        rec_a = wk("rec_a", [P, DC, T], 48 * K)
        rg_w = wk("rg_w", [P, 2, DC, P], 0)
        ratio = wk("ratio", [P, DC, T], 16 * K)
        sig_b = wk("sig_b", [P, DC, T], 32 * K)
        xa_qf = wk("xa_qf", [P, DC, T], 32 * K)
        xa_kf = wk("xa_kf", [P, DC, T], 48 * K)
        xa_vt = wk("xa_vt", [P, 2, D], 64 * K)
        prob = wk("prob", [P, 2, T], 80 * K)
        prob_t = wk("prob_t", [P, 2, T], 82 * K)
        soft = wk("soft", [P, 16], 84 * K)
        h_hi = wk("h_hi", [P, FC, T], 0, F32R)
        h_lo = wk("h_lo", [P, FC, T], 44 * K, F32R)
        y_out = wk("y_out", [P, DC, T], 0)

        prm = sb("prm", [P, N_PARAM])
        ident = sb("ident", [P, P])
        ones = sb("ones", [P, P])
        pick = sb("pick", [4, 4, P])
        mod = sb("mod", [P, 96, 2])
        buf_a = sb("buf_a", [P, 4, T])
        buf_b = sb("buf_b", [P, 4, T])
        buf_c = sb("buf_c", [P, 4, T])
        mean = sb("mean", [P, T])
        num = place("num", [P, 2 * VA], F32, at[0] - T * 4)
        rstd = sb("rstd", [P, T])
        spare = sb("spare", [P, T])
        stats = sb("stats", [P, 16, 6])
        moments = sb("moments", [P, 16, 2])
        tiny = sb("tiny", [P, 24])
        lam = sb("lam", [P, 4, 16])
        lam_tmp = sb("lam_tmp", [P, 16])
        both_affine = sb("both_affine", [P, 2, 16])
        assert at[0] <= nc.sbuf_usable_end, (at[0], nc.sbuf_usable_end)

        acc = ctx.enter_context(nc.psum_tensor("acc", [P, 4, NCOL], F32))
        msc = ctx.enter_context(nc.psum_tensor("msc", [P, 4, NCOL], F32))

        def flat(tile):
            return tile[:].rearrange("p a b -> p (a b)")

        def col(name, c):
            return prm[:, bass.ds(COL[name] + c, 1)]

        def acc_f(g):
            return acc[:, 2 * (g % 2):2 * (g % 2) + 2, :].rearrange("p a b -> p (a b)")

        def sem(name):
            return ctx.enter_context(nc.semaphore(name))

        raw_landed = [sem(f"raw_landed{i}") for i in range(RING)]
        hi_done, lo_done, unit_used = sem("hi_done"), sem("lo_done"), sem("unit_used")
        acc_free, ada_free = sem("acc_free"), sem("ada_free")
        act_done, dve_done, pair_ready = sem("act_done"), sem("dve_done"), sem("pair_ready")
        consts_in, x_in, cond_in = sem("consts_in"), sem("x_in"), sem("cond_in")
        mem_in = [sem(f"mem_in{q}") for q in range(4)]
        ctx_in, pool_in, sgu_in = sem("ctx_in"), sem("pool_in"), sem("sgu_in")
        ret_in, rg_in, xa_in, mask_in = sem("ret_in"), sem("rg_in"), sem("xa_in"), sem("mask_in")
        kv_stored = [sem("kv_stored0"), sem("kv_stored1")]
        y_stored = sem("y_stored")
        pe_step, act_step, dve_step = sem("pe_step"), sem("act_step"), sem("dve_step")
        step_sems = dict(pe=pe_step, act=act_step, dve=dve_step)
        eps_set = sem("eps_set")
        rows_turned = sem("rows_turned")
        gate_rows = sem("gate_rows")

        block = ctx.enter_context(nc.Block())

        def used(stage):
            return RING + stage.u0 + stage.total

        @block.sync
        def _(sp):
            for q in range(4):
                nc.sync.dma_start(mem[:, 4 * q:4 * q + 4, :], t["mem"][:, 4 * q:4 * q + 4, :]).then_inc(mem_in[q], 16)
            nc.sync.dma_start(prm[:], t["params"]).then_inc(consts_in, 16)
            nc.sync.dma_start(ident[:], t["ident"]).then_inc(consts_in, 16)
            nc.sync.dma_start(ones[:], t["ones"]).then_inc(consts_in, 16)
            nc.sync.dma_start(pick[:], t["pick"]).then_inc(consts_in, 16)
            nc.sync.dma_start(cond[:], t["cond"]).then_inc(cond_in, 16)
            nc.sync.dma_start(x[:], t["x"]).then_inc(x_in, 16)

            def load(stage):
                for i in rounds(sp, stage.iters):
                    for j, (kind, g, k, _) in enumerate(stage.kinds):
                        u = stage.u0 + j
                        if stage.name == "merge_a" and j == 2 * RING:
                            sp.wait_ge(unit_used, used(STAGE["ret_proj"]))
                            nc.sync.dma_start(rg_w[:], t["rg_w"]).then_inc(rg_in, 16)
                        sp.wait_ge(lo_done, i * stage.n + (u + 1))
                        if kind == "w":
                            src, at_ = t[stage.weights], i * stage.n_w + (g * stage.group_units + k)
                        elif kind == "a":
                            src, at_ = t["w_ada"], i * (3 * DC // KU) + ((stage.ada + g) * (DC // KU) + k)
                        else:
                            src, at_ = t["w_gate"], k
                        nc.sync.dma_start(raw[:, u % RING].rearrange("p a b -> p (a b)"),
                                          src[bass.ds(at_, 1), :, :].rearrange("a p n -> p (a n)")
                                          ).then_inc(raw_landed[u % RING], 16)

            for stage in STAGES:
                if stage.name == "mem_v":
                    sp.wait_ge(pair_ready, PAIR["mem"])
                    nc.sync.dma_start(ctx_x[:], t["ctx"]).then_inc(ctx_in, 16)
                if stage.name == "lat_o":
                    sp.wait_ge(unit_used, used(STAGE["lat_v"]))
                    nc.sync.dma_start(mask[:], t["mask"]).then_inc(mask_in, 16)
                    nc.sync.dma_start(pool_mat[:], t["pool_mat"]).then_inc(mask_in, 16)
                    nc.sync.dma_start(ang_i[:], t["positions"].partition_broadcast(P)).then_inc(ret_in, 16)
                if stage.name == "pool_u":
                    sp.wait_ge(pe_step, AFTER["mlstm"]["pe"])
                    nc.sync.dma_start(pool_w[:], t["pool_w"]).then_inc(pool_in, 16)
                if stage.name == "sgu_v":
                    sp.wait_ge(pe_step, AFTER["pool"]["pe"])
                    nc.sync.dma_start(w_sp[:], t["w_sp"]).then_inc(sgu_in, 16)
                    nc.sync.dma_start(b_sp[:], t["b_sp"]).then_inc(sgu_in, 16)
                if stage.name == "ret_k":
                    sp.wait_ge(dve_step, AFTER["angles"]["dve"])
                    nc.sync.dma_start(decay[:], t["decay"]).then_inc(ret_in, 16)
                if stage.name == "xa_q":
                    sp.wait_ge(pair_ready, PAIR["mix_out"])
                    sp.wait_ge(kv_stored[0], 16 * 5)
                    sp.wait_ge(kv_stored[1], 16 * 5)
                    nc.sync.dma_start(flat(xa_kf), t["mem_k"]).then_inc(xa_in, 16)
                    nc.sync.dma_start(flat(xa_vt), t["mem_v"]).then_inc(xa_in, 16)
                load(stage)
            sp.wait_ge(dve_step, AFTER["final"]["dve"])
            nc.sync.dma_start(t["out"], y_out[:]).then_inc(y_stored, 16)
            sp.wait_ge(y_stored, 16)

        @block.tensor
        def _(pe):
            steps = Steps(pe, "pe", step_sems)
            pe.sem_inc(unit_used, RING)
            pe.sem_inc(acc_free, 2)
            pe.sem_inc(ada_free, 3)

            def run(name, hi, lo, ready, batch=0, between=None, side=None):
                stage = STAGE[name]
                for i in rounds(pe, stage.iters):
                    if not batch:
                        pe.wait_ge(pair_ready, ready)
                    for j, (kind, g, k, ends) in enumerate(stage.kinds):
                        u = stage.u0 + j
                        slot = u % RING
                        first, last = k == 0, ends
                        if side:
                            side(j)
                        if kind == "a":
                            if first:
                                pe.wait_ge(ada_free, i * 3 + (stage.ada + g + 1))
                                if stage.gate and g == 2:
                                    steps.wait(dve=1)
                            pe.wait_ge(lo_done, i * stage.n + (u + 1 + RING))
                            for c in range(KU):
                                kc = KU * k + c
                                pe.matmul(msc[:, g, :], cond_pair[:, kc, :], w_hi[:, slot, c, :],
                                          start=(first and c == 0), stop=False)
                                mm = pe.matmul(msc[:, g, :], cond_pair[:, kc, :], w_lo[:, slot, c, :],
                                               start=False, stop=(last and c == KU - 1))
                            mm.then_inc(unit_used, 1)
                            continue
                        if kind == "x":
                            if first:
                                pe.wait_ge(ada_free, stage.ada + 3)
                            pe.wait_ge(lo_done, u + 1 + RING)
                            w_h = w_hi[:, slot].rearrange("p a b -> p (a b)")
                            w_l = w_lo[:, slot].rearrange("p a b -> p (a b)")
                            for c in range(UNIT // P):
                                kc = UNIT // P * k + c
                                cols = slice(c * P, (c + 1) * P)
                                pe.matmul(msc[:, 2, 0:T], w_h[:, cols], hi[:, kc, :], start=(kc == 0), stop=False)
                                pe.matmul(msc[:, 2, 0:T], w_h[:, cols], lo[:, kc, :], start=False, stop=False)
                                mm = pe.matmul(msc[:, 2, 0:T], w_l[:, cols], hi[:, kc, :], start=False, stop=(kc == DC - 1))
                            mm.then_inc(unit_used, 1)
                            continue
                        if first and g == 1 and between:
                            between()
                        if first:
                            pe.wait_ge(acc_free, i * 2 + (stage.g0 + g + 1))
                        if batch and g == 0 and KU * k % batch == 0:
                            pe.wait_ge(pair_ready, ready + KU * k // batch + 1)
                        pe.wait_ge(lo_done, i * stage.n + (u + 1 + RING))
                        for c in range(KU):
                            kc = KU * k + c
                            begin, end = first and c == 0, last and c == KU - 1
                            if stage.mode == "F":
                                for m in range(4):
                                    out = acc[:, 2 * (g % 2) + m // 2, (m % 2) * T:(m % 2 + 1) * T]
                                    wh = w_hi[:, slot, c, m * P:(m + 1) * P]
                                    wl = w_lo[:, slot, c, m * P:(m + 1) * P]
                                    pe.matmul(out, wh, hi[:, kc, :], start=(begin and m % 2 == 0), stop=False,
                                              skip_group_check=True)
                                    pe.matmul(out, wh, lo[:, kc, :], start=False, stop=False,
                                              skip_group_check=True)
                                    mm = pe.matmul(out, wl, hi[:, kc, :], start=False, stop=end,
                                                   skip_group_check=True)
                            else:
                                for tt in range(2):
                                    out = acc[:, 2 * (g % 2) + tt, :]
                                    xh = hi[:, kc, tt * P:(tt + 1) * P]
                                    xl = lo[:, kc, tt * P:(tt + 1) * P]
                                    pe.matmul(out, xh, w_hi[:, slot, c, :], start=begin, stop=False)
                                    pe.matmul(out, xl, w_hi[:, slot, c, :], start=False, stop=False)
                                    mm = pe.matmul(out, xh, w_lo[:, slot, c, :], start=False, stop=end)
                        mm.then_inc(unit_used, 1)

            def column_sums(steps_of=(1, 2, 3, 4)):
                for q in range(4):
                    steps.wait(dve=steps_of[q])
                    mm = pe.matmul(msc[:, 0, 0:T], ones[:], buf_b[:, q, :], start=(q == 0), stop=(q == 3))
                steps.done(mm)

            def sums_of(stage, with_mean=False):
                for q in range(4):
                    pe.wait_ge(dve_done, DVE_DONE[stage] - 2 * (3 - q))
                    if with_mean:
                        pe.matmul(msc[:, 1, 0:T], ones[:], buf_c[:, q, :], start=(q == 0), stop=(q == 3))
                    mm = pe.matmul(msc[:, 0, 0:T], ones[:], buf_b[:, q, :], start=(q == 0), stop=(q == 3))
                steps.done(mm)

            def two_chunks(bank, c, tt):
                return msc[:, bank + c // 2, (c % 2) * T + tt * P:(c % 2) * T + (tt + 1) * P]

            pe.wait_ge(consts_in, 64)
            column_sums()
            steps.end("mem_norm")
            steps.wait(dve=2)
            steps.end("cond")
            steps.end("mem_pair")
            steps.end("lam")
            run("mem_k", a_hi, a_lo, 0, batch=2)
            run("mem_v", a_hi, a_lo, PAIR["mem"])
            pe.wait_ge(ada_free, 3 + 12)
            for c in range(48):
                mm = pe.transpose(msc[:, 3, 4 * c:4 * c + 4], mod_rows[:, c * P:(c + 1) * P], ident[0:4, 0:4])
            steps.done(mm)
            steps.end("mod")
            steps.end("ctx_pair")

            def turn_rows(n):
                pe.wait_ge(ada_free, 3 + 12 + 3 * (n + 1))
                for c in range(12):
                    at_ = 4 * (48 + 12 * n + c)
                    mm = pe.transpose(msc[:, 3, at_:at_ + 4], mod_rows2[:, n % 2, c * P:(c + 1) * P], ident[0:4, 0:4])
                mm.then_inc(rows_turned, 1)

            def row_columns(first, n):
                for r in range(n):
                    for tt in range(2):
                        mm = pe.transpose(msc[:, 0, 8 * r + 4 * tt:8 * r + 4 * tt + 4],
                                          rows[:, first + r, tt * P:(tt + 1) * P], ident[0:4, 0:4])
                steps.done(mm)

            run("ctx_k", a_hi, a_lo, PAIR["mem"], batch=2)

            def in_ctx_v():
                turn_rows(0)

            run("ctx_v", a_hi, a_lo, PAIR["ctx"], between=in_ctx_v)
            pe.wait_ge(act_done, ACT_DONE["ctx_v"])
            for tt in range(2):
                for c in range(8):
                    mm = pe.transpose(acc[:, 2 * tt + c // 4, (c % 4) * P:(c % 4 + 1) * P],
                                      kf[:, c, tt * P:(tt + 1) * P], ident[:])
                steps.done(mm)
            turn_rows(1)
            steps.wait(act=4)
            row_columns(8, 2)
            for r in range(8):
                h = r % 4
                buf = flat(buf_b) if r % 2 == 0 else flat(buf_c)
                steps.wait(dve=4 + r)
                if r >= 2:
                    steps.wait(act=5 + r - 2)
                for kc in range(2):
                    for tt in range(2):
                        mm = pe.matmul(acc[:, 2 * (r % 2) + kc, 0:VA],
                                       k_tok[:, tt, h * MLSTM_D + kc * P:h * MLSTM_D + (kc + 1) * P],
                                       buf[:, tt * VA:(tt + 1) * VA], start=(tt == 0), stop=(tt == 1))
                steps.done(mm)
            steps.wait(act=12)
            steps.end("ctx_gates")
            steps.end("lat_pair")

            run("lat_k", a_hi, a_lo, PAIR["ctx"], batch=2)

            def in_lat_v():
                turn_rows(2)

            run("lat_v", a_hi, a_lo, PAIR["lat"], between=in_lat_v)
            run("lat_q", a_hi, a_lo, PAIR["lat"])
            turn_rows(3)
            steps.wait(act=2, dve=3)
            row_columns(8, 6)
            steps.wait(dve=4)
            steps.end("lat_gates")
            pe.wait_ge(act_done, ACT_DONE["lat_q"])

            def mlstm_scores(r):
                d, h = divmod(r, 4)
                if r >= 2:
                    steps.wait(dve=MlstmStep.weighted(r - 2))
                bank = 2 * (r % 2)
                for j in range(2):
                    for kc in range(2):
                        pe.matmul(msc[:, bank, j * T:(j + 1) * T], kf[:, 2 * h + kc, j * P:(j + 1) * P],
                                  qf[:, 2 * h + kc, :], start=(j == 0 and kc == 0), stop=(kc == 1),
                                  skip_group_check=True)
                steps.done(pe.matmul(msc[:, bank + 1, 0:T], pick[:, h, :], rows[:, 14 + d, :], start=True, stop=True))

            mlstm_scores(0)
            mlstm_scores(1)
            for r in range(8):
                h = r % 4
                if r >= 1:
                    steps.wait(dve=MlstmStep.read(r - 1))
                for tt in range(2):
                    for kc in range(2):
                        pe.matmul(acc[:, 2 + tt, 0:VA], qf[:, 2 * h + kc, tt * P:(tt + 1) * P],
                                  state[:, r, kc, :], start=(kc == 0), stop=(kc == 1))
                steps.wait(dve=MlstmStep.weighted(r))
                first = 2 * (r % 2)
                for tt in range(2):
                    for j in range(2):
                        mm = pe.matmul(acc[:, tt, 0:VA], buf_c[:, first + j, tt * P:(tt + 1) * P], va[:, j, h, :],
                                       start=(j == 0), stop=(j == 1))
                steps.done(mm)
                if r + 2 < 8:
                    mlstm_scores(r + 2)
            steps.wait(dve=24)
            steps.end("mlstm")
            run("lat_o", a_hi, a_lo, PAIR["lat"])

            def turn_mlstm(j):
                if j not in (6, 9):
                    return
                half = (j - 6) // 3
                if half == 0:
                    steps.wait(dve=2)
                else:
                    steps.wait(act=2)
                for c in range(4):
                    for tt in range(2):
                        mm = pe.transpose(two_chunks(2, c, tt),
                                          h_tok[:, tt, (4 * half + c) * P:(4 * half + c + 1) * P], ident[:])
                steps.done(mm)

            run("pool_u", a_hi, a_lo, PAIR["lat"], side=turn_mlstm)
            steps.end("mh_norm")

            def pooling(j):
                if j == 2:
                    pe.wait_ge(act_done, ACT_DONE["pool_u"])
                    pe.wait_ge(mask_in, 32)
                    pe.wait_ge(pool_in, 16)
                if j in (2, 4):
                    half = (j - 2) // 2
                    if half == 1:
                        steps.wait(act=1)
                    for c in range(4):
                        for tt in range(2):
                            mm = pe.matmul(two_chunks(0, c, tt),
                                           pool_tok[:, tt, (4 * half + c) * P:(4 * half + c + 1) * P],
                                           pool_mat[:, (4 * half + c) // 2, :], start=(c % 2 == 0 and tt == 0),
                                           stop=True, skip_group_check=True)
                    steps.done(mm)
                if j in (6, 8):
                    half = (j - 6) // 2
                    steps.wait(act=2 + half)
                    for c in range(4):
                        g = (4 * half + c) // 2
                        for kc in range(2):
                            mm = pe.matmul(msc[:, c // 2, (c % 2) * T:(c % 2 + 1) * T],
                                           pool_w[:, 2 * g + kc, (c % 2) * P:(c % 2 + 1) * P],
                                           pool_feat[:, 2 * g + kc, :], start=(c % 2 == 0 and kc == 0),
                                           stop=(kc == 1), skip_group_check=True)
                    steps.done(mm)

            run("mlstm_z", a_hi, a_lo, PAIR["lat"], side=pooling)
            steps.end("pool")
            run("pool_z", a_hi, a_lo, PAIR["lat"])
            run("even_out", b_hi, b_lo, PAIR["lat"], batch=4)
            sums_of("even_out", with_mean=True)
            steps.end("ln0")
            steps.end("sgu_pair")

            run("sgu_v", a_hi, a_lo, PAIR["even_out"], batch=2)
            pe.wait_ge(sgu_in, 32)
            for h in range(SGU_H):
                mm = pe.matmul(msc[:, h // 4, (h % 4) * P:(h % 4 + 1) * P], ones[:], w_sp[:, h, :],
                               start=(h % 4 == 0), stop=True, skip_group_check=True)
            steps.done(mm)

            def mix(j):
                if j not in MIX_AT:
                    return
                q = MIX_AT.index(j)
                steps.wait(dve=2 + q)
                for c in range(4):
                    for n in range(2):
                        mm = pe.matmul(two_chunks(2, c, n), sgu_tok[:, n, (4 * q + c) * P:(4 * q + c + 1) * P],
                                       w_sp[:, (4 * q + c) // 2, :], start=(c % 2 == 0 and n == 0), stop=True,
                                       skip_group_check=True)
                steps.done(mm)

            run("sgu_u", a_hi, a_lo, PAIR["sgu"], side=mix)
            steps.end("sgu_mix")
            run("sgu_z", a_hi, a_lo, PAIR["sgu"])
            run("odd_out", b_hi, b_lo, PAIR["sgu"], batch=4)
            sums_of("odd_out", with_mean=True)
            steps.end("ln1")

            column_sums((3, 5, 7, 8))
            steps.end("mix_norm")
            steps.end("mix_pair")
            steps.end("angles")
            run("ret_q", a_hi, a_lo, PAIR["odd_out"], batch=2)
            run("ret_k", a_hi, a_lo, PAIR["mix"])
            run("ret_v", a_hi, a_lo, PAIR["mix"])

            def inner(h):
                buf = buf_b if h % 2 == 0 else buf_c
                steps.wait(dve=1 + h)
                if h >= 2:
                    steps.wait(act=1 + h - 2)
                cols = slice(h * RET_V, (h + 1) * RET_V)
                pe.matmul(acc[:, 2 * (h % 2), 0:RET_V], buf[:, 0, 0:P], v_ret[:, 0, cols], start=True, stop=True)
                pe.matmul(acc[:, 2 * (h % 2) + 1, 0:RET_V], buf[:, 0, P:T], v_ret[:, 0, cols], start=True,
                          stop=False)
                steps.done(pe.matmul(acc[:, 2 * (h % 2) + 1, 0:RET_V], buf[:, 1, P:T], v_ret[:, 1, cols],
                                     start=False, stop=True))

            pe.wait_ge(act_done, ACT_DONE["ret_v"])
            pe.wait_ge(dve_done, DVE_DONE["ret_k"])
            for h in range(RET_H):
                if h >= 2:
                    steps.wait(dve=1 + h - 2)
                for j in range(2):
                    mm = pe.matmul(msc[:, h % 2, j * T:(j + 1) * T], kf[:, h, j * P:(j + 1) * P], qf[:, h, :],
                                   start=(j == 0), stop=True, skip_group_check=True)
                steps.done(mm)
                if h >= 1:
                    inner(h - 1)
            inner(RET_H - 1)
            steps.wait(act=8)

            def turn_heads(j):
                if j not in TURN_AT:
                    return
                q = TURN_AT.index(j)
                if q == 0:
                    steps.wait(dve=10)
                if q >= 2:
                    steps.wait(act=10 + q - 2)
                for c in range(4):
                    for tt in range(2):
                        mm = pe.transpose(two_chunks(2 * (q % 2), c, tt),
                                          v_ret[:, tt, (4 * q + c) * P:(4 * q + c + 1) * P], ident[:])
                steps.done(mm)

            run("rnn_x", a_hi, a_lo, PAIR["mix"], side=turn_heads)
            steps.end("retention")
            run("ret_g", a_hi, a_lo, PAIR["mix"])
            run("ret_proj", b_hi, b_lo, PAIR["mix"], batch=4)
            def rg_gates(j):
                c = RG_CHUNK_AT.get(j)
                if c is None:
                    return
                if c == 0:
                    pe.wait_ge(rg_in, 16)
                    pe.wait_ge(dve_done, DVE_DONE["rnn_x"])
                    pe.wait_ge(act_step, AFTER["retention"]["act"])
                if c >= 2:
                    steps.wait(act=rg_act_step(c - 2, 1))
                for a in range(2):
                    mm = pe.matmul(msc[:, c % 2, a * T:(a + 1) * T], rg_w[:, a, c, :], xr[:, c, :],
                                   start=(a == 0), stop=True, skip_group_check=True)
                steps.done(mm)

            run("merge_a", a_hi, a_lo, PAIR["mix"], side=rg_gates)
            steps.end("rglru")
            run("rnn_y", a_hi, a_lo, PAIR["mix"])
            run("merge_b", a_hi, a_lo, PAIR["mix"])
            run("rnn_proj", b_hi, b_lo, PAIR["rnn_proj"])
            run("mix_out", a_hi, a_lo, PAIR["rnn_proj"], batch=4)
            sums_of("mix_out")
            steps.end("xa_norm")
            steps.end("xa_pair")

            run("xa_q", a_hi, a_lo, PAIR["mix_out"], batch=2)
            pe.wait_ge(act_done, ACT_DONE["xa_q"])
            pe.wait_ge(xa_in, 32)

            def logits(h):
                for tt in range(2):
                    for kc in range(4):
                        mm = pe.matmul(msc[:, 0, tt * T:(tt + 1) * T], xa_qf[:, 4 * h + kc, tt * P:(tt + 1) * P],
                                       xa_kf[:, 4 * h + kc, :], start=(tt == 0 and kc == 0), stop=(kc == 3),
                                       skip_group_check=True)
                steps.done(mm)

            logits(0)
            for h in range(XA_H):
                if h + 1 < XA_H:
                    steps.wait(act=XaStep.exponentials(h))
                    logits(h + 1)
                steps.wait(dve=2 * h + 2)
                for j in range(2):
                    for tt in range(2):
                        mm = pe.transpose(msc[:, 1, j * T + tt * P:j * T + (tt + 1) * P],
                                          prob[:, tt, j * P:(j + 1) * P], ident[:])
                steps.done(mm)
                steps.wait(act=3 * h + 2)
                if h >= 1:
                    pe.wait_ge(pair_ready, PAIR["xa"] + h)
                for c in range(4):
                    for j in range(2):
                        mm = pe.matmul(msc[:, 2 + c // 2, (c % 2) * T:(c % 2 + 1) * T],
                                       xa_vt[:, j, h * XA_D + c * P:h * XA_D + (c + 1) * P], prob_t[:, j, :],
                                       start=(c % 2 == 0 and j == 0), stop=(j == 1), skip_group_check=True)
                steps.done(mm)
            steps.end("attention")
            run("xa_o", b_hi, b_lo, PAIR["xa"], batch=4)
            sums_of("xa_o")
            steps.end("ffn_norm")
            steps.end("ffn_pair")

            run("ffn_up", a_hi, a_lo, PAIR["xa_o"], batch=2)
            run("ffn_down", h_hi, h_lo, PAIR["ffn"], batch=4)
            sums_of("ffn_down")
            steps.end("final")

        def walk(stage, i, split, epilogues, last=False, side=None, window=None):
            rests = []
            first, stop = window or (0, stage.n)
            for j in range(first, stop):
                kind, g, _, ends = stage.kinds[j % stage.n]
                rest = epilogues[kind](i, g, i * stage.n + (stage.u0 + j + 1 + RING)) if ends else None
                if not (last and j + RING >= stage.n):
                    split(stage, i, j + RING)
                for r in rests:
                    r()
                rests = [rest] if rest else []
                if side:
                    side(j)
            for r in rests:
                r()

        def walk_stage(eng, stage, split, epilogues, side, *counts):
            if stage is LAST:
                for i in range(stage.iters):
                    walk(stage, i, split, epilogues, i == stage.iters - 1)
            elif stage.name == "ffn_up":
                walk(stage, 0, split, epilogues, window=(0, 1))
                for i in rounds(eng, stage.iters - 1, *counts):
                    walk(stage, i, split, epilogues, window=(1, stage.n + 1))
                walk(stage, stage.iters - 1, split, epilogues, window=(1, stage.n))
            else:
                for i in rounds(eng, stage.iters, *counts):
                    walk(stage, i, split, epilogues, side=side)

        @block.scalar
        def _(act):
            steps = Steps(act, "act", step_sems)
            done, dve = Count(), Count()

            def split(stage, i, j):
                u = stage.u0 + j
                slot = u % RING
                act.wait_ge(raw_landed[slot], i * (stage.n // RING * 16) + 16 * (u // RING + 1))
                act.wait_ge(unit_used, i * stage.n + (u + 1))
                nc.scalar.copy(w_hi[:, slot], raw[:, slot]).then_inc(hi_done, 1)

            def ran(instruction):
                instruction.then_inc(act_done, 1)
                done.add()

            def forget_exp(i, g, n_used):
                def rest():
                    steps.wait(dve=1)
                    steps.done(nc.scalar.activation(gate_tmp[64:P, 2, :], gate_tmp[64:P, 1, :], ACT.Exp, scale=-1.0))
                return rest

            def run(name, group, side=None):
                stage = STAGE[name]

                def rows_out(i, g, n_used):
                    if stage.ada >= 18 and g == 0:
                        act.wait_ge(rows_turned, stage.ada // 3 - 5)
                    act.wait_ge(unit_used, n_used)
                    if stage.ada < 12:
                        out = mod_rows[:, bass.ds(i * (3 * NCOL) + (stage.ada + g) * NCOL, NCOL)]
                    else:
                        out = mod_rows2[:, stage.ada // 3 % 2, g * NCOL:(g + 1) * NCOL]
                    nc.scalar.copy(out, msc[0:4, g, :]).then_inc(ada_free, 1)

                def finish(i, g, n_used):
                    act.wait_ge(unit_used, n_used)
                    if dve.v:
                        act.wait_ge(dve_done, dve.at())
                    return group(i, g)

                walk_stage(act, stage, split, {"w": finish, "a": rows_out, "x": forget_exp}, side,
                           (done, stage.act), (dve, stage.dve))

            both = flat(buf_a)

            def to_buffer(func, scale=1.0):
                def group(i, g):
                    nc.scalar.activation(both, acc_f(g), func, scale=scale).then_inc(acc_free, 1)
                    act.drain()
                    ran(act.nop())
                return group

            def to_slab(slab, func=ACT.Copy, scale=1.0):
                def group(i, g):
                    nc.scalar.activation(flat(slab)[:, bass.ds(i * (8 * T) + g * (4 * T), 4 * T)], acc_f(g), func,
                                         scale=scale).then_inc(acc_free, 1)
                    act.drain()
                    ran(act.nop())
                return group

            def to_tokens(slab):
                def group(i, g):
                    nc.scalar.copy(slab[:, :, bass.ds(i * (2 * NCOL) + g * NCOL, NCOL)],
                                   acc[:, 2 * g:2 * g + 2, :]).then_inc(acc_free, 1)
                    act.drain()
                    ran(act.nop())
                return group

            def gate_to_pair(func, hi, chunk=0, scale=1.0):
                def group(i, g):
                    to_buffer(func)(i, g)

                    def rest():
                        act.wait_ge(dve_done, dve.add())
                        ran(nc.scalar.activation(flat(hi)[:, bass.ds(chunk * T + i * (8 * T) + g * (4 * T), 4 * T)],
                                                 flat(buf_b), ACT.Copy, scale=scale))
                    return rest
                return group

            def with_dve(group, n=1):
                def wrapped(i, g):
                    group(i, g)
                    dve.add(n)
                return wrapped

            def rms(name):
                steps.wait(pe=1)
                steps.done(nc.scalar.activation(spare[:], msc[:, 0, 0:T], ACT.Sqrt, bias=tiny[:, 21:22],
                                                scale=1.0 / D))
                steps.end(name)

            def layer_norm(name):
                steps.wait(dve=1)
                steps.done(nc.scalar.activation(rstd[:], spare[:], ACT.Sqrt, bias=tiny[:, 20:21]))
                steps.end(name)

            def pair(hi, name, after=None):
                for q in range(8):
                    steps.wait(dve=q + 1)
                    steps.done(nc.scalar.copy(hi[:, 2 * q:2 * q + 2, :], buf_a[:, 2 * (q % 2):2 * (q % 2) + 2, :]))
                    if after:
                        after(2 * q)
                        after(2 * q + 1)
                steps.end(name)

            act.sem_inc(kv_stored[0], 16)
            act.sem_inc(kv_stored[1], 16)
            act.wait_ge(eps_set, 1)
            for q in range(4):
                act.wait_ge(mem_in[q], 16)
                steps.done(nc.scalar.activation(square[:, 4 * q:4 * q + 4, :].rearrange("p a b -> p (a b)"),
                                                mem[:, 4 * q:4 * q + 4, :].rearrange("p a b -> p (a b)"), ACT.Square))
            rms("mem_norm")
            act.wait_ge(cond_in, 16)
            steps.done(nc.scalar.activation(cond_silu[:], cond[:], ACT.Silu))
            act.drain()
            steps.wait(dve=1)
            steps.done(nc.scalar.copy(cond_pair[:, :, 0:4:2], cond_silu[:]))
            steps.end("cond")
            for j in range(RING):
                split(STAGES[0], 0, j)
            pair(a_hi, "mem_pair")
            act.wait_ge(consts_in, 64)
            steps.wait(dve=1)
            steps.done(nc.scalar.activation(lam[:, 1, :], lam[:, 0, :], ACT.Exp, scale=-1.0))
            steps.end("lam")

            stored = [Count(), Count()]
            for c in stored:
                c.v = 16

            def store(dst, tokens):
                def group(i, g):
                    act.wait_ge(kv_stored[g], i * 16 + stored[g].v)
                    nc.scalar.copy(kv_stage[:, g, :], acc_f(g)).then_inc(acc_free, 1)
                    act.drain()
                    if tokens:
                        out = dst.rearrange("p (t n) -> p t n", t=2)[:, :, bass.ds(i * (2 * NCOL) + g * NCOL, NCOL)]
                        src = kv_stage[:, g, :].rearrange("p (t n) -> p t n", t=2)
                    else:
                        out, src = dst[:, bass.ds(i * (8 * T) + g * (4 * T), 4 * T)], kv_stage[:, g, :]
                    nc.scalar.dma_start(out, src).then_inc(kv_stored[g], 16)
                    ran(act.nop())
                return group

            run("mem_k", store(t["mem_k"], False))
            for c in stored:
                c.v += 32
            run("mem_v", store(t["mem_v"], True))
            steps.end("mod")

            pair(a_hi, "ctx_pair")

            def conv_silu(dst):
                def group(i, g):
                    to_buffer(ACT.Copy)(i, g)

                    def rest():
                        act.wait_ge(dve_done, dve.add())
                        ran(nc.scalar.activation(dst[:, 4 * g:4 * g + 4, :].rearrange("p a b -> p (a b)"), flat(buf_b),
                                                 ACT.Silu))
                    return rest
                return group

            def values(i, g):
                for tt in range(2):
                    mm = nc.scalar.copy(va[:, tt, 2 * g:2 * g + 2, 0:MLSTM_D],
                                        acc[:, 2 * g + tt, :].rearrange("p (h n) -> p h n", h=2))
                mm.then_inc(acc_free, 1)
                act.drain()
                ran(act.nop())

            run("ctx_k", conv_silu(kf))
            run("ctx_v", values)
            act.wait_ge(kv_stored[0], 16 * 5)
            act.wait_ge(kv_stored[1], 16 * 5)
            for tt in range(2):
                steps.wait(pe=1 + tt)
                steps.done(nc.scalar.copy(k_tok[:, tt, :], acc_f(tt)))
            steps.wait(dve=3)
            steps.done(nc.scalar.activation(rows[:, 8:10, :], rows[:, 6:8, :], ACT.Exp))
            for r in range(8):
                steps.wait(pe=4 + r)
                steps.done(nc.scalar.activation(state[:, r, :, :], acc[:, 2 * (r % 2):2 * (r % 2) + 2, 0:VA], ACT.Copy,
                                                scale=MLSTM_D ** -0.5))
            steps.end("ctx_gates")
            pair(a_hi, "lat_pair")

            run("lat_k", conv_silu(kf))
            run("lat_v", values)
            steps.wait(dve=3)
            nc.scalar.activation(rows[:, 8:10, :], rows[:, 6:8, :], ACT.Exp)
            steps.done(nc.scalar.activation(rows[:, 10:12, :], rows[:, 0:2, :], ACT.Exp))
            run("lat_q", conv_silu(qf))
            steps.end("lat_gates")
            for r in range(8):
                d, h = divmod(r, 4)
                steps.wait(dve=MlstmStep.masked(r))
                first = 2 * (r % 2)
                for j in range(2):
                    mm = nc.scalar.activation(buf_b[:, first + j, :], buf_a[:, first + j, :], ACT.Exp,
                                              bias=columns[:, (4 + d) * 2 + j, h:h + 1])
                steps.done(mm)
            steps.end("mlstm")
            act.wait_ge(dve_step, AFTER["mlstm"]["dve"])
            run("lat_o", with_dve(to_buffer(ACT.Tanh, 0.5)))

            def mlstm_out(j):
                if j == 1:
                    steps.wait(dve=1)
                    steps.done(nc.scalar.activation(tiny[:, 0:8], moments[:, 0:8, 1], ACT.Sqrt, bias=tiny[:, 20:21]))
                if j in (6, 9):
                    half = (j - 6) // 3
                    steps.wait(pe=1 + half)
                    for c in range(4):
                        mm = nc.scalar.activation(h_feat[:, 4 * half + c, :],
                                                  msc[:, 2 + c // 2, (c % 2) * T:(c % 2 + 1) * T], ACT.Copy,
                                                  scale=col("mh_norm_g", 4 * half + c))
                    steps.done(mm)

            run("pool_u", to_tokens(pool_tok), side=mlstm_out)
            steps.end("mh_norm")

            def pooling(j):
                if j in (2, 4):
                    half = (j - 2) // 2
                    steps.wait(pe=1 + half)
                    steps.done(nc.scalar.copy(pool_feat[:, 4 * half:4 * half + 4, :].rearrange("p a b -> p (a b)"),
                                              msc[:, 0:2, :].rearrange("p a b -> p (a b)")))
                if j in (6, 8):
                    half = (j - 6) // 2
                    steps.wait(pe=3 + half)
                    for c in range(4):
                        mm = nc.scalar.activation(pool_y[:, 4 * half + c, :],
                                                  msc[:, c // 2, (c % 2) * T:(c % 2 + 1) * T], ACT.Copy,
                                                  scale=col("pool_scale", 4 * half + c))
                    steps.done(mm)

            run("mlstm_z", gate_to_pair(ACT.Silu, b_hi), side=pooling)
            steps.end("pool")
            run("pool_z", gate_to_pair(ACT.Silu, b_hi, chunk=8))

            def modulated(layer):
                def group(i, g):
                    for m in range(4):
                        mm = nc.scalar.activation(buf_a[:, m, :], acc[:, 2 * g + m // 2, (m % 2) * T:(m % 2 + 1) * T],
                                                  ACT.Copy,
                                                  scale=mod[:, bass.ds(i * 8 + (48 * layer + 32 + 4 * g + m), 1), 0])
                    mm.then_inc(acc_free, 1)
                    act.drain()
                    ran(act.nop())
                return group

            def with_squares(group):
                def wrapped(i, g):
                    group(i, g)

                    def rest():
                        act.wait_ge(dve_done, dve.add())
                        ran(nc.scalar.activation(both, flat(x)[:, bass.ds(i * (8 * T) + g * (4 * T), 4 * T)], ACT.Square))
                        dve.add()
                    return rest
                return wrapped

            def affine(layer, c):
                return nc.scalar.activation(x[:, c, :], x[:, c, :], ACT.Identity, bias=col("post_ln_b", 16 * layer + c),
                                            scale=col("post_ln_g", 16 * layer + c))

            run("even_out", with_squares(modulated(0)))
            layer_norm("ln0")
            pair(a_hi, "sgu_pair", after=lambda c: affine(0, c))

            run("sgu_v", to_tokens(sgu_tok))
            steps.wait(pe=1)
            steps.done(nc.scalar.copy(row_sum[:].rearrange("p a b -> p (a b)"),
                                      msc[:, 0:2, :].rearrange("p a b -> p (a b)")))

            def deviations(j):
                if j == 2:
                    steps.wait(dve=1)
                    steps.done(nc.scalar.activation(tiny[:, 0:2], moments[:, 0:2, 1], ACT.Sqrt, bias=tiny[:, 20:21]))

            run("sgu_u", with_dve(to_buffer(ACT.Copy)), side=deviations)
            steps.end("sgu_mix")
            run("sgu_z", gate_to_pair(ACT.Silu, b_hi))
            run("odd_out", with_squares(modulated(1)))
            layer_norm("ln1")
            for q in range(4):
                steps.wait(dve=(1, 2, 4, 6)[q])
                buf = buf_a if q % 2 == 0 else buf_c
                for m in range(4):
                    c = 4 * q + m
                    mm = nc.scalar.activation(buf[:, m, :], x[:, c, :], ACT.Square, bias=col("post_ln_b", 16 + c),
                                              scale=col("post_ln_g", 16 + c))
                steps.done(mm)
                act.drain()
                for m in range(4):
                    affine(1, 4 * q + m)
            rms("mix_norm")
            pair(a_hi, "mix_pair")

            steps.wait(dve=1)
            nc.scalar.activation(angle[:, 2, :], angle[:, 1, :], ACT.Sin, scale=col("rot_sign", 0))
            steps.done(nc.scalar.activation(angle[:, 3, :], angle[:, 1, :], ACT.Sin, scale=0.5))
            steps.end("angles")

            def halves(i, g):
                for a in range(2):
                    nc.scalar.copy(both[64 * a:64 * a + 64, :], acc_f(g)[64 - 64 * a:128 - 64 * a, :])
                act.drain()
                ran(act.nop())
                dve.add()

            run("ret_q", halves)
            run("ret_k", halves)
            run("ret_v", to_tokens(v_ret))
            for h in range(RET_H):
                steps.wait(pe=2 * h + 3 if h < RET_H - 1 else 2 * h + 2)
                steps.done(nc.scalar.copy(v_ret[:, :, h * RET_V:(h + 1) * RET_V],
                                          acc[:, 2 * (h % 2):2 * (h % 2) + 2, 0:RET_V]))

            def heads_out(j):
                if j == 4:
                    steps.wait(dve=9)
                    steps.done(nc.scalar.activation(tiny[:, 0:16], moments[:, 0:16, 1], ACT.Sqrt, bias=tiny[:, 20:21]))
                if j in TURN_AT:
                    q = TURN_AT.index(j)
                    steps.wait(pe=17 + q)
                    for c in range(4):
                        mm = nc.scalar.activation(ret_feat[:, 4 * q + c, :],
                                                  msc[:, 2 * (q % 2) + c // 2, (c % 2) * T:(c % 2 + 1) * T], ACT.Copy,
                                                  scale=col("ret_gn", 4 * q + c))
                    steps.done(mm)

            run("rnn_x", with_dve(to_buffer(ACT.Copy)), side=heads_out)
            steps.end("retention")
            run("ret_g", gate_to_pair(ACT.Silu, b_hi))
            run("ret_proj", to_slab(merged))

            def rg_root(q):
                steps.wait(dve=4 * q + 4)
                part = ratio[:, 4 * q:4 * q + 4, :].rearrange("p a b -> p (a b)")
                steps.done(nc.scalar.activation(part, part, ACT.Sqrt, scale=2.0))

            def rg_gates(j):
                c = RG_CHUNK_AT.get(j)
                if c is None:
                    return
                steps.wait(pe=c + 1)
                if c >= 2:
                    steps.wait(dve=c - 1)
                nc.scalar.activation(buf_b[:, c % 2, :], msc[:, c % 2, 0:T], ACT.Tanh, bias=lam[:, 1, c:c + 1], scale=0.5)
                steps.done(nc.scalar.activation(buf_b[:, 2 + c % 2, :], msc[:, c % 2, T:2 * T], ACT.Tanh,
                                                bias=lam[:, 2, c:c + 1], scale=0.5))
                act.drain()
                nc.scalar.activation(buf_c[:, c % 2, :], buf_b[:, c % 2, :], ACT.Tanh, bias=lam[:, 0, c:c + 1],
                                     scale=lam[:, 0, c:c + 1])
                steps.done(nc.scalar.activation(rec_a[:, c, :], buf_b[:, c % 2, :], ACT.Exp, bias=lam[:, 3, c:c + 1],
                                                scale=lam[:, 3, c:c + 1]))
                if c in (5, 9, 13):
                    rg_root((c - 5) // 4)

            run("merge_a", with_dve(to_buffer(ACT.Tanh, 0.5)), side=rg_gates)
            rg_root(3)
            steps.end("rglru")
            run("rnn_y", gate_to_pair(ACT.Gelu_apprx_tanh, b_hi))
            run("merge_b", to_slab(sig_b, ACT.Tanh, 0.5))
            run("rnn_proj", gate_to_pair(ACT.Copy, a_hi, scale=0.5))
            run("mix_out", with_squares(to_buffer(ACT.Copy)))
            rms("xa_norm")
            pair(a_hi, "xa_pair")

            run("xa_q", to_slab(xa_qf))

            def exponentials(h):
                steps.wait(dve=2 * h + 1)
                for tt in range(2):
                    mm = nc.scalar.activation(prob[:, tt, :], msc[:, 0, tt * T:(tt + 1) * T], ACT.Exp,
                                              bias=soft[:, 2 + tt:3 + tt], scale=XA_D ** -0.5,
                                              accum_out=soft[:, 4 + tt:5 + tt])
                steps.done(mm)

            exponentials(0)
            for h in range(XA_H):
                steps.wait(pe=XaStep.turned(h))
                steps.done(nc.scalar.copy(flat(prob_t), msc[:, 1, :]))
                if h + 1 < XA_H:
                    exponentials(h + 1)
                steps.wait(pe=XaStep.result(h))
                steps.done(nc.scalar.copy(b_hi[:, 4 * h:4 * h + 4, :].rearrange("p a b -> p (a b)"),
                                          msc[:, 2:4, :].rearrange("p a b -> p (a b)")))
            steps.end("attention")
            run("xa_o", with_squares(to_buffer(ACT.Copy)))
            rms("ffn_norm")
            pair(a_hi, "ffn_pair")

            def gate_and_value(i, g):
                dst = buf_b if g == 0 else buf_c
                for m in range(4):
                    at_ = FC * g + m
                    mm = nc.scalar.activation(dst[:, m, :], acc[:, 2 * g + m // 2, (m % 2) * T:(m % 2 + 1) * T],
                                              ACT.Identity, bias=prm[:, bass.ds(i * 4 + (COL["ffn_conv_b"] + at_), 1)],
                                              scale=prm[:, bass.ds(i * 4 + (COL["ffn_conv_w"] + 4 * FC + at_), 1)])
                ran(mm)

                def rest():
                    act.wait_ge(dve_done, dve.add())
                    if g == 0:
                        ran(nc.scalar.activation(flat(buf_b), flat(buf_b), ACT.Silu))
                    else:
                        ran(nc.scalar.copy(flat(h_hi)[:, bass.ds(i * (4 * T), 4 * T)], flat(buf_c)))
                return rest

            run("ffn_up", gate_and_value)
            run("ffn_down", with_squares(to_buffer(ACT.Copy)))
            rms("final")

        @block.gpsimd
        def _(pool):
            for n, section in enumerate(("ctx_gates", "lat_gates")):
                pool.wait_ge(dve_step, BEFORE[section]["dve"] + 2)
                z, e, inverse = gate_tmp[64:P, 0, :], gate_tmp[64:P, 2, :], gate_tmp[64:P, 3, :]
                ratio_, square_, total = gate_tmp[64:P, 1, :], gate_tmp[64:P, 3, :], gate_tmp[64:P, 4, :]
                nc.gpsimd.tensor_tensor(ratio_, inverse, e, ALU.mult)
                pool.drain()
                nc.gpsimd.tensor_tensor(square_, ratio_, ratio_, ALU.mult)
                pool.drain()
                nc.gpsimd.tensor_scalar(total, square_, 1.0 / SERIES[0], None, ALU.mult)
                for k in SERIES[1:]:
                    pool.drain()
                    nc.gpsimd.tensor_scalar(total, total, 1.0 / k, None, ALU.add)
                    pool.drain()
                    nc.gpsimd.tensor_tensor(total, total, square_, ALU.mult)
                pool.drain()
                nc.gpsimd.tensor_scalar(total, total, 2.0, 2.0, ALU.mult, ALU.add)
                pool.drain()
                nc.gpsimd.tensor_tensor(total, total, ratio_, ALU.mult)
                pool.drain()
                nc.gpsimd.tensor_tensor(z, z, total, ALU.subtract)
                pool.drain()
                for d in range(2):
                    nc.gpsimd.tensor_copy(rows[:, d, :], gate_tmp[32 * d:32 * d + 4, 0, :])
                    mm = nc.gpsimd.tensor_copy(rows[:, 12 + d, :], gate_tmp[64 + 32 * d:68 + 32 * d, 0, :])
                mm.then_inc(gate_rows, 1)

        @block.vector
        def _(dve):
            steps = Steps(dve, "dve", step_sems)
            done, act_at = Count(), Count()
            vec = nc.vector

            def split(stage, i, j):
                u = stage.u0 + j
                slot = u % RING
                dve.wait_ge(hi_done, i * stage.n + (u + 1))
                vec.tensor_tensor(w_lo[:, slot], raw[:, slot], w_hi[:, slot].bitcast(F32),
                                  ALU.subtract).then_inc(lo_done, 1)

            def ran(instruction):
                instruction.then_inc(dve_done, 1)
                done.add()

            def gates_out(i, g, n_used):
                return lambda: make_gates(n_used)

            def make_gates(n_used):
                dve.wait_ge(unit_used, n_used)
                vec.tensor_scalar(gate_tmp[:, 0, :], msc[:, 2, 0:T], col("gate_bias", 0), None, ALU.add)
                dve.drain()
                z = gate_tmp[64:P, 0, :]
                steps.done(vec.scalar_tensor_tensor(gate_tmp[64:P, 1, :], z, -1.0, z, ALU.mult, ALU.max))
                steps.wait(act=1)
                e = gate_tmp[64:P, 2, :]
                vec.tensor_scalar(gate_tmp[64:P, 1, :], e, 2.0, None, ALU.add)
                vec.tensor_scalar(z, z, 0.0, None, ALU.min)
                dve.drain()
                steps.done(vec.reciprocal(gate_tmp[64:P, 3, :], gate_tmp[64:P, 1, :]))

            def run(name, group, between=None, side=None):
                stage = STAGE[name]

                def finish(i, g, n_used):
                    rest = group(i, g)

                    def then():
                        if rest:
                            rest()
                        if g == 0 and between:
                            between()
                    return then

                walk_stage(dve, stage, split, {"w": finish, "a": lambda i, g, n: None, "x": gates_out}, side,
                           (done, stage.dve), (act_at, stage.act))

            def wait_act(n=1):
                dve.wait_ge(act_done, act_at.add(n))

            def none(n=1):
                def group(i, g):
                    act_at.add(n)
                return group

            def bcast(tile, n):
                return tile[:].unsqueeze(1).to_broadcast([P, n, T])

            def reciprocal_of_root(n):
                steps.wait(act=n)
                vec.reciprocal(rstd[:], spare[:])
                dve.drain()

            def pair(hi, lo, make, name, before=None):
                def low(q):
                    steps.wait(act=q + 1)
                    vec.tensor_tensor(lo[:, 2 * q:2 * q + 2, :], buf_a[:, 2 * (q % 2):2 * (q % 2) + 2, :],
                                      hi[:, 2 * q:2 * q + 2, :].bitcast(F32), ALU.subtract).then_inc(pair_ready, 1)

                for q in range(8):
                    dve.drain()
                    if before:
                        before(2 * q, 2)
                    for c in range(2):
                        mm = make(buf_a[:, 2 * (q % 2) + c, :], 2 * q + c)
                    steps.done(mm)
                    if q:
                        low(q - 1)
                low(7)
                steps.end(name)

            def rms_of(slab, weight):
                def make(out, c):
                    return vec.scalar_tensor_tensor(out, slab[:, c, :], col(weight, c), rstd[:], ALU.mult, ALU.mult)
                return make

            def modulate(slab, layer, which):
                def make(out, c):
                    return vec.tensor_scalar(out, slab[:, c, :], mod[:, 48 * layer + 16 + c, which:which + 1],
                                             mod[:, 48 * layer + c, which:which + 1], ALU.mult, ALU.add)
                return make

            def log1p(out, e, t1, t2):
                vec.tensor_scalar(t1, e, 2.0, None, ALU.add)
                dve.drain()
                vec.reciprocal(t1, t1)
                dve.drain()
                vec.tensor_tensor(t1, t1, e, ALU.mult)
                dve.drain()
                vec.tensor_tensor(t2, t1, t1, ALU.mult)
                dve.drain()
                vec.tensor_scalar(out, t2, 1.0 / SERIES[0], None, ALU.mult)
                for n in SERIES[1:]:
                    dve.drain()
                    vec.scalar_tensor_tensor(out, out, 1.0 / n, t2, ALU.add, ALU.mult)
                dve.drain()
                vec.scalar_tensor_tensor(out, out, 1.0, t1, ALU.add, ALU.mult)
                dve.drain()
                vec.tensor_scalar(out, out, 2.0, None, ALU.mult)
                dve.drain()

            dve.sem_inc(lo_done, RING)
            vec.memset(tiny[:, 20:21], LN_EPS)
            vec.memset(tiny[:, 21:22], RMS_EPS)
            dve.drain().then_inc(eps_set, 1)
            for q in range(4):
                steps.wait(act=q + 1)
                steps.done(vec.tensor_reduce(buf_b[:, q, :], square[:, 4 * q:4 * q + 4, :].rearrange("p c t -> p t c"),
                                             AX, ALU.add))
            for q in range(4):
                dve.wait_ge(mem_in[q], 16)
            reciprocal_of_root(5)
            steps.end("mem_norm")
            steps.done(vec.memset(cond_pair[:].bitcast(F32), 0.0))
            steps.wait(act=2)
            steps.done(vec.tensor_tensor(cond_pair[:, :, 1:4:2], cond_silu[:], cond_pair[:, :, 0:4:2].bitcast(F32),
                                         ALU.subtract))
            steps.end("cond")
            for j in range(RING):
                split(STAGES[0], 0, j)
            dve.wait_ge(consts_in, 64)
            pair(a_hi, a_lo, rms_of(mem, "norm_mem"), "mem_pair")
            lmb = prm[:, COL["rg_lambda"]:COL["rg_lambda"] + 16]
            steps.done(vec.scalar_tensor_tensor(lam[:, 0, :], lmb, -1.0, lmb, ALU.mult, ALU.max))
            steps.wait(act=1)
            log1p(lam[:, 2, :], lam[:, 1, :], lam[:, 0, :], lam[:, 3, :])
            vec.tensor_scalar(lam[:, 0, :], lmb, -1.0, 0.0, ALU.mult, ALU.max)
            dve.drain()
            vec.tensor_tensor(lam[:, 0, :], lam[:, 0, :], lam[:, 2, :], ALU.add)
            dve.drain()
            vec.tensor_scalar(lam[:, 3, :], lam[:, 0, :], -4.0, None, ALU.mult)
            dve.drain()
            vec.tensor_scalar(lam[:, 0, :], lam[:, 3, :], -1.0, None, ALU.mult)
            vec.tensor_scalar(lam[:, 1, :], prm[:, COL["rg_b_a"]:COL["rg_b_a"] + 16], 0.5, None, ALU.mult)
            vec.tensor_scalar(lam[:, 2, :], prm[:, COL["rg_b_x"]:COL["rg_b_x"] + 16], 0.5, None, ALU.mult)
            steps.end("lam")
            run("mem_k", none())
            run("mem_v", none())
            def make_mod(layer):
                part = mod[:, 48 * layer:48 * layer + 48, :]
                rows4 = msc[:, 3, 192 * layer:192 * layer + 192].rearrange("p (c n) -> p c n", n=4)
                vec.tensor_copy(part, rows4[:, :, 0:4:2])
                dve.drain()
                vec.tensor_tensor(part, part, rows4[:, :, 1:4:2], ALU.add)
                dve.drain()
                bias = prm[:, COL["ada_b"] + 48 * layer:COL["ada_b"] + 48 * layer + 48]
                vec.tensor_tensor(part, part, bias.unsqueeze(2).to_broadcast([P, 48, 2]), ALU.add)
                dve.drain()
                scale = mod[:, 48 * layer + 16:48 * layer + 32, :]
                vec.tensor_scalar(scale, scale, 1.0, None, ALU.add)
                dve.drain()

            steps.wait(pe=1)
            make_mod(0)
            steps.done(dve.drain())
            steps.end("mod")

            dve.wait_ge(ctx_in, 16)
            dve.wait_ge(unit_used, used(STAGE["mem_v"]))
            pair(a_hi, a_lo, modulate(ctx_x, 0, 1), "ctx_pair")

            def conv3(first):
                def weight(tap, m):
                    return col("conv_qk", 16 * tap + first + m)

                for m in range(4):
                    vec.tensor_scalar(buf_b[:, m, :], buf_a[:, m, :], weight(1, m), None, ALU.mult)
                dve.drain()
                for m in range(4):
                    vec.scalar_tensor_tensor(buf_b[:, m, 1:T], buf_a[:, m, 0:T - 1], weight(0, m), buf_b[:, m, 1:T],
                                             ALU.mult, ALU.add)
                dve.drain()
                for m in range(4):
                    mm = vec.scalar_tensor_tensor(buf_b[:, m, 0:T - 1], buf_a[:, m, 1:T], weight(2, m),
                                                  buf_b[:, m, 0:T - 1], ALU.mult, ALU.add)
                return mm

            def conv_qk(first):
                def group(i, g):
                    wait_act()
                    ran(conv3(first + 4 * g))
                    act_at.add()
                return group

            run("ctx_k", conv_qk(8))
            def decays():
                vec.tensor_tensor_scan(rows[:, 2, :], rows[:, 12, :], rows[:, 12, :], 0.0, ALU.add, ALU.bypass)
                vec.tensor_tensor_scan(rows[:, 3, ::-1], rows[:, 13, ::-1], rows[:, 13, ::-1], 0.0, ALU.add, ALU.bypass)
                dve.drain()
                vec.tensor_tensor(rows[:, 4:6, :], rows[:, 0:2, :], rows[:, 2:4, :], ALU.subtract)
                dve.drain()

            def ctx_rows():
                dve.wait_ge(gate_rows, 1)
                decays()
                vec.tensor_reduce(small[:, 0:2], rows[:, 4:6, :], AX, ALU.max)
                dve.drain()
                vec.tensor_scalar(small[:, 0:2], small[:, 0:2], 0.0, None, ALU.max)
                dve.drain()
                for d in range(2):
                    end = T - 1 if d == 0 else 0
                    vec.tensor_tensor(small[:, 2 + d:3 + d], rows[:, 2 + d, end:end + 1], small[:, d:d + 1], ALU.add)
                    mm = vec.tensor_scalar(rows[:, 6 + d, :], rows[:, 4 + d, :], small[:, d:d + 1], None, ALU.subtract)
                steps.done(mm)

            run("ctx_v", none(), between=ctx_rows)
            steps.wait(pe=3)
            vec.tensor_copy(columns[:, 0:4, :].rearrange("p a b -> p (a b)"), msc[:, 0, 0:16])
            vec.memset(va[:, :, :, MLSTM_D:VA], 1.0)
            dve.drain()
            dve.wait_ge(act_done, ACT_DONE["ctx_v"])
            for r in range(8):
                d, h = divmod(r, 4)
                buf = flat(buf_b) if r % 2 == 0 else flat(buf_c)
                if r >= 2:
                    steps.wait(pe=4 + r - 2)
                for tt in range(2):
                    mm = vec.tensor_scalar(buf[:, tt * VA:(tt + 1) * VA], va[:, tt, h, :], columns[:, 2 * d + tt, h:h + 1],
                                           None, ALU.mult)
                steps.done(mm)
            steps.end("ctx_gates")
            dve.wait_ge(x_in, 16)
            dve.wait_ge(unit_used, used(STAGE["ctx_v"]))
            pair(a_hi, a_lo, modulate(x, 0, 0), "lat_pair")

            run("lat_k", conv_qk(8))

            def lat_rows():
                dve.wait_ge(gate_rows, 2)
                decays()
                vec.tensor_tensor_scan(rows[:, 14, :], rows[:, 4, :], rows[:, 4, :], small[:, 2:3], ALU.max, ALU.bypass)
                vec.tensor_tensor_scan(rows[:, 15, ::-1], rows[:, 5, ::-1], rows[:, 5, ::-1], small[:, 3:4], ALU.max, ALU.bypass)
                vec.tensor_copy(rows[:, 12:14, :], rows[:, 4:6, :])
                dve.drain()
                for d in range(2):
                    vec.tensor_scalar(rows[:, 6 + d, :], rows[:, 14 + d, :], small[:, 2 + d:3 + d], -1.0, ALU.subtract, ALU.mult)
                steps.done(vec.scalar_tensor_tensor(rows[:, 0:2, :], rows[:, 2:4, :], -1.0, rows[:, 14:16, :], ALU.mult,
                                                    ALU.subtract))

            run("lat_v", none(), between=lat_rows)
            run("lat_q", conv_qk(0))
            dve.wait_ge(rows_turned, 4)
            make_mod(1)
            steps.wait(pe=1)
            steps.done(vec.tensor_copy(columns[:, 0:12, :].rearrange("p a b -> p (a b)"), msc[:, 0, 0:48]))
            steps.end("lat_gates")
            dve.wait_ge(mask_in, 32)

            def masked(r):
                steps.wait(pe=MlstmStep.scores(r))
                first = 2 * (r % 2)
                steps.done(vec.tensor_tensor(buf_a[:, first:first + 2, :], mask[:, r // 4, :, :],
                                             msc[:, first + 1, 0:T].unsqueeze(1).to_broadcast([P, 2, T]), ALU.subtract))

            def weighted(r):
                steps.wait(act=r + 1)
                first = 2 * (r % 2)
                steps.done(vec.scalar_tensor_tensor(buf_c[:, first:first + 2, :].rearrange("p a b -> p (a b)"),
                                                    msc[:, first, :], MLSTM_D ** -0.5,
                                                    buf_b[:, first:first + 2, :].rearrange("p a b -> p (a b)"),
                                                    ALU.mult, ALU.mult))

            masked(0)
            masked(1)
            weighted(0)
            for r in range(8):
                d, h = divmod(r, 4)
                steps.wait(pe=MlstmStep.results(r))
                for tt in range(2):
                    mm = vec.tensor_scalar(num[:, tt * VA:(tt + 1) * VA], acc[:, 2 + tt, 0:VA],
                                           columns[:, 2 * d + tt, h:h + 1], None, ALU.mult)
                if r < 7:
                    steps.done(mm)
                dve.drain()
                for tt in range(2):
                    mm = vec.tensor_tensor(num[:, tt * VA:(tt + 1) * VA], num[:, tt * VA:(tt + 1) * VA], acc[:, tt, 0:VA],
                                           ALU.add)
                if r == 7:
                    steps.done(mm)
                dve.drain()
                den = num[:, 0:2 * VA].rearrange("p (a b) -> p a b", a=2)[:, :, MLSTM_D]
                vec.scalar_tensor_tensor(tiny[:, 0:2], den, -1.0, den, ALU.mult, ALU.max)
                dve.drain()
                vec.tensor_tensor(tiny[:, 0:2], tiny[:, 0:2], columns[:, 4 + 2 * d:6 + 2 * d, h], ALU.max)
                dve.drain()
                vec.reciprocal(tiny[:, 2:4], tiny[:, 0:2])
                dve.drain()
                vec.tensor_scalar(tiny[:, 2:4], tiny[:, 2:4], 0.5, None, ALU.mult)
                dve.drain()
                for tt in range(2):
                    out = h_tok[:, tt, h * MLSTM_D:(h + 1) * MLSTM_D]
                    n = num[:, tt * VA:tt * VA + MLSTM_D]
                    if d == 0:
                        vec.tensor_scalar(out, n, tiny[:, 2 + tt:3 + tt], None, ALU.mult)
                    else:
                        vec.scalar_tensor_tensor(out, n, tiny[:, 2 + tt:3 + tt], out, ALU.mult, ALU.add)
                if r + 1 < 8:
                    weighted(r + 1)
                if r + 2 < 8:
                    masked(r + 2)
                dve.drain()
            steps.end("mlstm")

            def output_gate(i, g):
                wait_act()
                part = h_tok[:, :, g * NCOL:(g + 1) * NCOL]
                ran(vec.scalar_tensor_tensor(part, buf_a[:].rearrange("p (a b) t -> p a (b t)", a=2), 1.0, part,
                                             ALU.add, ALU.mult))

            run("lat_o", output_gate)
            dve.drain()

            def normalise_mlstm(j):
                if j == 0:
                    for n in range(8):
                        vec.bn_stats(stats[:, n, :], h_tok[:, n // 4, (n % 4) * MLSTM_D:(n % 4 + 1) * MLSTM_D])
                    dve.drain()
                    for n in range(8):
                        mm = vec.bn_aggr(moments[:, n, :], stats[:, n, :])
                    steps.done(mm)
                if j == 2:
                    steps.wait(act=1)
                    vec.reciprocal(tiny[:, 8:16], tiny[:, 0:8])
                    dve.drain()
                    for n in range(8):
                        part = h_tok[:, n // 4, (n % 4) * MLSTM_D:(n % 4 + 1) * MLSTM_D]
                        mm = vec.tensor_scalar(part, part, moments[:, n, 0:1], tiny[:, 8 + n:9 + n], ALU.subtract, ALU.mult)
                    steps.done(mm)

            run("pool_u", none(), side=normalise_mlstm)
            steps.end("mh_norm")

            def gate_to_pair(factor, hi, lo, chunk=0):
                def group(i, g):
                    wait_act()
                    at_ = i * (8 * T) + g * (4 * T)
                    ran(vec.tensor_tensor(flat(buf_b), flat(buf_a), flat(factor)[:, bass.ds(at_, 4 * T)], ALU.mult))

                    def rest():
                        wait_act()
                        at_ = chunk * T + i * (8 * T) + g * (4 * T)
                        vec.tensor_tensor(flat(lo)[:, bass.ds(at_, 4 * T)], flat(buf_b),
                                          flat(hi)[:, bass.ds(at_, 4 * T)].bitcast(F32),
                                          ALU.subtract).then_inc(pair_ready, 1)
                    return rest
                return group

            dve.wait_ge(act_step, AFTER["mh_norm"]["act"])
            run("mlstm_z", gate_to_pair(h_feat, b_hi, b_lo))
            steps.end("pool")
            dve.wait_ge(act_step, AFTER["pool"]["act"])
            run("pool_z", gate_to_pair(pool_y, b_hi, b_lo, chunk=8))

            def residual(scale, with_mean=False):
                def group(i, g):
                    wait_act()
                    part = flat(x)[:, bass.ds(i * (8 * T) + g * (4 * T), 4 * T)]
                    ran(vec.scalar_tensor_tensor(part, part, scale, flat(buf_a), ALU.mult, ALU.add))

                    def rest():
                        at_ = i * (2 * T) + g * T
                        if with_mean:
                            dve.drain()
                            vec.tensor_reduce(flat(buf_c)[:, bass.ds(at_, T)], part.rearrange("p (c t) -> p t c", t=T), AX,
                                              ALU.add)
                        wait_act()
                        ran(vec.tensor_reduce(flat(buf_b)[:, bass.ds(at_, T)], buf_a[:].rearrange("p c t -> p t c"), AX,
                                              ALU.add))
                    return rest
                return group

            def layer_norm(name):
                steps.wait(pe=1)
                vec.tensor_scalar(mean[:], msc[:, 1, 0:T], 1.0 / D, None, ALU.mult)
                dve.drain()
                vec.tensor_tensor(rstd[:], mean[:], mean[:], ALU.mult)
                dve.drain()
                steps.done(vec.scalar_tensor_tensor(spare[:], msc[:, 0, 0:T], 1.0 / D, rstd[:], ALU.mult, ALU.subtract))
                steps.wait(act=1)
                vec.reciprocal(rstd[:], rstd[:])
                steps.end(name)

            def normalised(c, n):
                part = x[:, c:c + n, :]
                vec.tensor_tensor(part, part, bcast(mean, n), ALU.subtract)
                dve.drain()
                mm = vec.tensor_tensor(part, part, bcast(rstd, n), ALU.mult)
                dve.drain()
                return mm

            lng = prm[:, COL["post_ln_g"]:COL["post_ln_g"] + 16]
            lnb = prm[:, COL["post_ln_b"]:COL["post_ln_b"] + 16]
            vec.tensor_tensor(both_affine[:, 0, :], lng, mod[:, 64:80, 0], ALU.mult)
            vec.tensor_tensor(both_affine[:, 1, :], lnb, mod[:, 64:80, 0], ALU.mult)
            dve.drain()
            vec.tensor_tensor(both_affine[:, 1, :], both_affine[:, 1, :], mod[:, 48:64, 0], ALU.add)
            dve.drain()

            def affine(out, c):
                return vec.tensor_scalar(out, x[:, c, :], both_affine[:, 0, c:c + 1], both_affine[:, 1, c:c + 1],
                                         ALU.mult, ALU.add)

            run("even_out", residual(ALPHA, with_mean=True))
            layer_norm("ln0")
            pair(a_hi, a_lo, affine, "sgu_pair", before=normalised)

            run("sgu_v", none())
            dve.wait_ge(act_done, ACT_DONE["sgu_v"])

            def normalise_and_mix(j):
                if j in (0, 1):
                    for n in range(4 * j, 4 * j + 4):
                        vec.bn_stats(stats[:, n, :], sgu_tok[:, n // 4, (n % 4) * NCOL:(n % 4 + 1) * NCOL])
                if j == 1:
                    dve.drain()
                    for tt in range(2):
                        mm = vec.bn_aggr(moments[:, tt, :], stats[:, 4 * tt:4 * tt + 4, :].rearrange("p a b -> p (a b)"))
                    steps.done(mm)
                if j == 3:
                    steps.wait(act=2)
                    vec.reciprocal(tiny[:, 2:4], tiny[:, 0:2])
                    dve.drain()
                if j in (3, 4):
                    tt = j - 3
                    mm = vec.tensor_scalar(sgu_tok[:, tt, :], sgu_tok[:, tt, :], moments[:, tt, 0:1], tiny[:, 2 + tt:3 + tt],
                                           ALU.subtract, ALU.mult)
                if j == 4:
                    steps.done(mm)
                if j in MIX_AT:
                    q = MIX_AT.index(j)
                    for c in range(4):
                        h = (4 * q + c) // 2
                        vec.scalar_tensor_tensor(buf_c[:, c, 0:P], row_sum[:, h, :], col("sgu_ln_b", 4 * q + c),
                                                 b_sp[:, h, :], ALU.mult, ALU.add)
                    dve.drain()
                    steps.wait(pe=2 + q)
                    for c in range(4):
                        mm = vec.scalar_tensor_tensor(
                            sgu_s[:, 4 * q + c, :].rearrange("p (n t) -> p n t", n=2),
                            msc[:, 2 + c // 2, (c % 2) * T:(c % 2 + 1) * T].rearrange("p (n t) -> p n t", n=2),
                            col("sgu_ln_g", 4 * q + c), buf_c[:, c, 0:P].unsqueeze(1).to_broadcast([P, 2, P]),
                            ALU.mult, ALU.add)
                    steps.done(mm)
                    dve.drain()

            def times_slab(i, g):
                wait_act()
                part = flat(sgu_s)[:, bass.ds(i * (8 * T) + g * (4 * T), 4 * T)]
                ran(vec.tensor_tensor(part, part, flat(buf_a), ALU.mult))

            run("sgu_u", times_slab, side=normalise_and_mix)
            steps.end("sgu_mix")
            dve.drain()
            run("sgu_z", gate_to_pair(sgu_s, b_hi, b_lo))
            run("odd_out", residual(ALPHA, with_mean=True))
            layer_norm("ln1")
            dve.drain()

            def quarter_sums(q):
                steps.wait(act=q + 1)
                buf = buf_a if q % 2 == 0 else buf_c
                steps.done(vec.tensor_reduce(buf_b[:, q, :], buf[:].rearrange("p c t -> p t c"), AX, ALU.add))

            for q in range(4):
                steps.done(normalised(4 * q, 4))
                if q:
                    quarter_sums(q - 1)
            quarter_sums(3)
            reciprocal_of_root(5)
            steps.end("mix_norm")
            pair(a_hi, a_lo, rms_of(x, "norm_mix"), "mix_pair")

            dve.wait_ge(ret_in, 16)
            pos, ang = angle[:, 0, :], angle[:, 1, :]
            vec.tensor_copy(pos, ang_i[:])
            dve.drain()
            vec.tensor_scalar(ang, pos, col("inv_freq", 0), None, ALU.mult)
            dve.drain()
            vec.tensor_scalar(pos, ang, 1.0 / (2 * np.pi), None, ALU.mult)
            dve.drain()
            for magic in (ROUND, -ROUND):
                vec.tensor_scalar(pos, pos, magic, None, ALU.add)
                dve.drain()
            for part in TWO_PI_PARTS:
                vec.scalar_tensor_tensor(ang, pos, -part, ang, ALU.mult, ALU.add)
                dve.drain()
            steps.done(vec.tensor_scalar(ang, ang, PI_BELOW, -PI_BELOW, ALU.min, ALU.max))
            steps.wait(act=1)
            cos, sin = angle[:, 4, :], angle[:, 2, :]
            vec.tensor_tensor(cos, angle[:, 3, :], angle[:, 3, :], ALU.mult)
            dve.drain()
            steps.done(vec.tensor_scalar(cos, cos, -2.0, 1.0, ALU.mult, ALU.add))
            dve.drain()
            steps.end("angles")

            def rotated(slab):
                def group(i, g):
                    wait_act()
                    part = slab[:, 4 * g:4 * g + 4, :]
                    vec.tensor_tensor(part, acc_f(g).rearrange("p (c t) -> p c t", t=T), cos.unsqueeze(1).to_broadcast([P, 4, T]),
                                      ALU.mult).then_inc(acc_free, 1)
                    vec.tensor_tensor(buf_b[:], buf_a[:], sin.unsqueeze(1).to_broadcast([P, 4, T]), ALU.mult)
                    dve.drain()
                    ran(vec.tensor_tensor(part, part, buf_b[:], ALU.add))
                return group

            run("ret_q", rotated(qf))
            run("ret_k", rotated(kf))
            run("ret_v", none())
            dve.wait_ge(ret_in, 32)
            for h in range(RET_H):
                buf = buf_b if h % 2 == 0 else buf_c
                steps.wait(pe=1 if h == 0 else 2 * h)
                if h >= 2:
                    steps.wait(pe=2 * (h - 2) + 3)
                vec.scalar_tensor_tensor(buf[:, 0, :], msc[:, h % 2, 0:T], RET_QK ** -0.5, decay[:, h, :], ALU.mult, ALU.mult)
                steps.done(vec.scalar_tensor_tensor(buf[:, 1, P:T], msc[:, h % 2, T + P:2 * T], RET_QK ** -0.5,
                                                    decay[:, h, 0:P], ALU.mult, ALU.mult))

            def normalise_heads(j):
                if j < 4:
                    for n in range(4 * j, 4 * j + 4):
                        h, tt = divmod(n, 2)
                        steps.wait(act=1 + h)
                        vec.bn_stats(stats[:, n, :], v_ret[:, tt, h * RET_V:(h + 1) * RET_V])
                if j == 3:
                    dve.drain()
                    for n in range(16):
                        mm = vec.bn_aggr(moments[:, n, :], stats[:, n, :])
                    steps.done(mm)
                if j == 5:
                    steps.wait(act=9)
                    vec.reciprocal(lam_tmp[:], tiny[:, 0:16])
                    dve.drain()
                if 5 <= j < 9:
                    for n in range(4 * (j - 5), 4 * (j - 5) + 4):
                        h, tt = divmod(n, 2)
                        part = v_ret[:, tt, h * RET_V:(h + 1) * RET_V]
                        mm = vec.tensor_scalar(part, part, moments[:, n, 0:1], lam_tmp[:, n:n + 1], ALU.subtract, ALU.mult)
                if j == 8:
                    steps.done(mm)

            def conv4(i, g):
                wait_act()

                def weight(tap, m):
                    return prm[:, bass.ds(i * 8 + (COL["rnn_conv_w"] + 16 * tap + 4 * g + m), 1)]

                def part(m, start):
                    return flat(xr)[:, bass.ds(i * (8 * T) + ((4 * g + m) * T + start), T - start)]

                for m in range(4):
                    vec.tensor_scalar(part(m, 0), buf_a[:, m, :], weight(3, m),
                                      prm[:, bass.ds(i * 8 + (COL["rnn_conv_b"] + 4 * g + m), 1)], ALU.mult, ALU.add)
                for shift in (1, 2, 3):
                    dve.drain()
                    for m in range(4):
                        mm = vec.scalar_tensor_tensor(part(m, shift), buf_a[:, m, 0:T - shift], weight(3 - shift, m),
                                                      part(m, shift), ALU.mult, ALU.add)
                ran(mm)

            run("rnn_x", conv4, side=normalise_heads)
            dve.drain()
            steps.end("retention")
            dve.wait_ge(act_step, AFTER["retention"]["act"])
            run("ret_g", gate_to_pair(ret_feat, b_hi, b_lo))
            run("ret_proj", none())

            def merge_first(i, g):
                wait_act()
                part = flat(merged)[:, bass.ds(i * (8 * T) + g * (4 * T), 4 * T)]
                ran(vec.scalar_tensor_tensor(part, flat(buf_a), 1.0, part, ALU.add, ALU.mult))


            def rg_chunk(c):
                steps.wait(act=rg_act_step(c, 2))
                vec.scalar_tensor_tensor(xr[:, c, :], buf_b[:, 2 + c % 2, :], 1.0, xr[:, c, :], ALU.add, ALU.mult)
                vec.tensor_scalar(mean[:], buf_c[:, c % 2, :], 1.0, None, ALU.add)
                dve.drain()
                vec.reciprocal(spare[:], mean[:])
                dve.drain()
                steps.done(vec.tensor_tensor(ratio[:, c, :], buf_c[:, c % 2, :], spare[:], ALU.mult))

            def rg_scan(q):
                steps.wait(act=rg_root_step(q))
                dve.drain()
                for c in range(4 * q, 4 * q + 4):
                    vec.scalar_tensor_tensor(xr[:, c, :], xr[:, c, :], 0.5, ratio[:, c, :], ALU.mult, ALU.mult)
                dve.drain()
                for c in range(4 * q, 4 * q + 4):
                    vec.tensor_tensor_scan(xr[:, c, :], rec_a[:, c, :], xr[:, c, :], 0.0, ALU.mult, ALU.add)

            def recurrence(j):
                c = RG_CHUNK_AT.get(j)
                if c:
                    rg_chunk(c - 1)
                if c in (7, 11, 15):
                    rg_scan((c - 7) // 4)
                if j == max(RG_CHUNK_AT) + 2:
                    rg_chunk(DC - 1)

            run("merge_a", merge_first, side=recurrence)
            rg_scan(3)
            dve.drain()
            steps.end("rglru")
            run("rnn_y", gate_to_pair(xr, b_hi, b_lo))
            run("merge_b", none())

            def merge_second(i, g):
                wait_act()
                at_ = i * (8 * T) + g * (4 * T)
                vec.scalar_tensor_tensor(flat(buf_b), flat(sig_b)[:, bass.ds(at_, 4 * T)], 1.0, flat(buf_a), ALU.add, ALU.mult)
                dve.drain()
                ran(vec.tensor_tensor(flat(buf_b), flat(buf_b), flat(merged)[:, bass.ds(at_, 4 * T)], ALU.add))

                def rest():
                    wait_act()
                    vec.scalar_tensor_tensor(flat(a_lo)[:, bass.ds(at_, 4 * T)], flat(buf_b), 0.5,
                                             flat(a_hi)[:, bass.ds(at_, 4 * T)].bitcast(F32), ALU.mult,
                                             ALU.subtract).then_inc(pair_ready, 1)
                return rest

            run("rnn_proj", merge_second)
            run("mix_out", residual(1.0))
            reciprocal_of_root(1)
            steps.end("xa_norm")
            pair(a_hi, a_lo, rms_of(x, "norm_xa"), "xa_pair")

            run("xa_q", none())

            def maxima(h):
                steps.wait(pe=XaStep.logits(h))
                vec.tensor_reduce(soft[:, 0:2], msc[:, 0, :].rearrange("p (a b) -> p a b", a=2), AX, ALU.max)
                dve.drain()
                steps.done(vec.tensor_scalar(soft[:, 2:4], soft[:, 0:2], -(XA_D ** -0.5), None, ALU.mult))

            maxima(0)
            for h in range(XA_H):
                steps.wait(act=XaStep.exponentials(h))
                vec.reciprocal(soft[:, 6:8], soft[:, 4:6])
                dve.drain()
                for tt in range(2):
                    mm = vec.tensor_scalar(prob[:, tt, :], prob[:, tt, :], soft[:, 6 + tt:7 + tt], None, ALU.mult)
                steps.done(mm)
                if h + 1 < XA_H:
                    maxima(h + 1)
                steps.wait(act=XaStep.hi(h))
                vec.tensor_tensor(b_lo[:, 4 * h:4 * h + 4, :].rearrange("p a b -> p (a b)"),
                                  msc[:, 2:4, :].rearrange("p a b -> p (a b)"),
                                  b_hi[:, 4 * h:4 * h + 4, :].bitcast(F32).rearrange("p a b -> p (a b)"),
                                  ALU.subtract).then_inc(pair_ready, 1)
            steps.end("attention")
            run("xa_o", residual(1.0))
            reciprocal_of_root(1)
            steps.end("ffn_norm")
            pair(a_hi, a_lo, rms_of(x, "norm_ffn"), "ffn_pair")

            def gate_and_value(i, g):
                wait_act()
                dst = buf_b if g == 0 else buf_c

                for shift in (1, 2):
                    if shift == 2:
                        dve.drain()
                    for m in range(4):
                        weight = prm[:, bass.ds(i * 4 + (COL["ffn_conv_w"] + 2 * FC * (2 - shift) + FC * g + m), 1)]
                        first = (m % 2) * T
                        mm = vec.scalar_tensor_tensor(dst[:, m, shift:T],
                                                      acc[:, 2 * g + m // 2, first:first + T - shift], weight,
                                                      dst[:, m, shift:T], ALU.mult, ALU.add)
                mm.then_inc(acc_free, 1)
                dve.drain()
                if g == 0:
                    ran(dve.drain())
                    return wait_act
                ran(vec.tensor_tensor(flat(buf_c), flat(buf_c), flat(buf_b), ALU.mult))

                def rest():
                    wait_act()
                    vec.tensor_tensor(flat(h_lo)[:, bass.ds(i * (4 * T), 4 * T)], flat(buf_c),
                                      flat(h_hi)[:, bass.ds(i * (4 * T), 4 * T)].bitcast(F32),
                                      ALU.subtract).then_inc(pair_ready, 1)
                return rest

            run("ffn_up", gate_and_value)
            run("ffn_down", residual(1.0))
            reciprocal_of_root(1)
            for c in range(DC):
                mm = vec.scalar_tensor_tensor(y_out[:, c, :], x[:, c, :], col("final_norm", c), rstd[:], ALU.mult, ALU.mult)
            steps.done(mm)
            steps.end("final")


def units(w):
    k, n = w.shape
    w = w.reshape(k // (KU * P), KU, P, n // NCOL, NCOL).transpose(3, 0, 2, 1, 4)
    return np.ascontiguousarray(w).reshape(-1, P, UNIT)


def chunks(a):
    return np.ascontiguousarray(a.reshape(a.shape[0], -1, P).transpose(2, 1, 0))


def columns_of(v):
    return v.reshape(-1, P).T


def spread_heads(a):
    out = np.zeros((a.shape[0], 4, 32), a.dtype)
    out[:, :, :4] = a.reshape(a.shape[0], 4, 4)
    return out.reshape(a.shape[0], P)


def constants():
    s, q = np.arange(T)[:, None], np.arange(T)[None, :]
    seen = np.stack([s <= q, s >= q])
    mask = np.where(seen, 0.0, -1e30).astype(np.float32)
    mask = mask.reshape(2, 2, P, T).transpose(2, 0, 1, 3)
    pool = np.zeros((P, POOL_G, P))
    for g, w in enumerate(POOL_WINDOWS):
        for row in range(P // GRID_W):
            for pos in range(GRID_W):
                lo, hi = max(pos - w // 2, 0), min(pos + (w - 1 - w // 2), GRID_W - 1)
                pool[row * GRID_W + lo:row * GRID_W + hi + 1, g, row * GRID_W + pos] = 1.0 / (hi - lo + 1)
                pool[row * GRID_W + pos, g, row * GRID_W + pos] -= 1.0
    log_gamma = np.log1p(-(2.0 ** (-5.0 - np.arange(RET_H))))
    rel = np.arange(T)[None, None, :] - np.arange(P)[:, None, None]
    decay = np.where(rel >= 0, np.exp(log_gamma[None, :, None] * np.maximum(rel, 0)), 0.0)
    pick = np.zeros((4, 4, P), np.float32)
    for h in range(4):
        pick[h, h] = 1.0
    half = RET_QK // 2
    freq = np.float32(10000.0) ** (-np.arange(half, dtype=np.float32) * np.float32(2.0) / np.float32(RET_QK))
    return {
        "ident": np.eye(P, dtype=np.float32), "ones": np.ones((P, P), np.float32), "pick": pick,
        "mask": np.ascontiguousarray(mask), "pool_mat": pool.astype(np.float32), "decay": decay.astype(np.float32),
        "inv_freq": np.tile(freq.astype(np.float32), 2),
        "rot_sign": np.repeat(np.float32([-1.0, 1.0]), half),
    }


def lay_out(i):
    const = constants()
    bias = spread_heads(np.concatenate([i["b_igate"][0].reshape(1, -1), i["b_fgate"][0].reshape(1, -1)], axis=1)).T
    parts = {
        "ada_b": i["ada_b"], "post_ln_g": i["post_ln_g"], "post_ln_b": i["post_ln_b"], "conv_qk": i["conv_qk"],
        "mh_norm_g": i["mh_norm_g"], "pool_scale": i["pool_scale"], "sgu_ln_g": i["sgu_ln_g"],
        "sgu_ln_b": i["sgu_ln_b"], "norm_mix": i["norm_mix_w_2"], "ret_gn": i["ret_gn_w_2"],
        "rnn_conv_w": i["rnn_conv_w_2"], "rnn_conv_b": i["rnn_conv_b_2"], "rg_b_a": i["rg_b_a_2"],
        "rg_b_x": i["rg_b_x_2"], "rg_lambda": i["rg_lambda_2"], "norm_xa": i["norm_xa_w_2"],
        "norm_mem": i["norm_mem_w_2"], "norm_ffn": i["norm_ffn_w_2"], "ffn_conv_w": i["ffn_conv_w_2"],
        "ffn_conv_b": i["ffn_conv_b_2"], "final_norm": i["final_norm_w_2"], "inv_freq": const.pop("inv_freq"),
        "rot_sign": const.pop("rot_sign"),
    }
    params = [bias if name == "gate_bias" else columns_of(parts[name]) for name, _ in PARAM_COLUMNS]
    out = dict(const)
    out["params"] = np.ascontiguousarray(np.concatenate(params, axis=1))
    assert out["params"].shape == (P, N_PARAM)
    out["x"], out["ctx"], out["mem"] = chunks(i["x"][0]), chunks(i["ctx"][0]), chunks(i["mem_2"][0])
    out["cond"] = np.ascontiguousarray(np.stack([i["c"][0].reshape(DC, P).T, i["c_ctx"].reshape(DC, P).T], axis=2))
    out["positions"] = np.ascontiguousarray(i["positions_2"].reshape(T))

    out["w_xa_k"], out["w_xa_v"] = units(i["xa_w_k_2"][0]), units(i["xa_w_v_2"][0])
    out["w_ada"] = np.concatenate([units(i["ada_w"][0]), units(i["ada_w"][1])])

    w = i["w_in_even"][0]
    n_m = MLSTM_H * MLSTM_D
    for k, name in enumerate(("w_q", "w_k", "w_v", "w_o", "w_mlstm_z")):
        out[name] = units(w[:, k * n_m:(k + 1) * n_m])
    gate = spread_heads(w[:, 5 * n_m:5 * n_m + 16])
    out["w_gate"] = np.ascontiguousarray(gate.reshape(GATE_UNITS, UNIT // P, P, P).transpose(0, 2, 1, 3)).reshape(-1, P, UNIT)
    out["w_pool_u"] = units(w[:, 5 * n_m + 16:6 * n_m + 16])
    out["w_pool_z"] = units(w[:, 6 * n_m + 16:])
    out["pool_w"] = np.ascontiguousarray(i["pool_w"][0].reshape(POOL_G, 2, P, 256).transpose(2, 0, 1, 3)).reshape(P, 8, 256)
    out["w_even_out"] = units(i["w_out_even"][0])
    w = i["w_in_odd"][0]
    out["w_sgu_u"], out["w_sgu_v"], out["w_sgu_z"] = units(w[:, :D]), units(w[:, D:2 * D]), units(w[:, 2 * D:])
    out["w_sp"] = np.ascontiguousarray(i["w_sp"][0].transpose(2, 0, 1))
    out["b_sp"] = np.ascontiguousarray(np.broadcast_to(i["b_sp"][0][None], (P, SGU_H, SGU_CHUNK)))
    out["w_odd_out"] = units(i["w_out_odd"][0])
    w = i["w_in_2"][0]
    first = 0
    for name, width in (("w_ret_q", 1024), ("w_ret_k", 1024), ("w_ret_v", D), ("w_ret_g", D), ("w_rnn_x", D),
                        ("w_rnn_y", D), ("w_merge_a", D), ("w_merge_b", D)):
        out[name] = units(w[:, first:first + width])
        first += width
    out["rg_w"] = np.ascontiguousarray(np.stack([i["rg_w_a_2"][0], i["rg_w_x_2"][0]]).transpose(2, 0, 1, 3))
    out["w_ret_proj"], out["w_rnn_proj"] = units(i["w_proj_ret_2"][0]), units(i["w_proj_rnn_2"][0])
    out["w_mix_out"] = units(i["w_mix_out_2"][0])
    out["w_xa_q"], out["w_xa_o"] = units(i["xa_w_q_2"][0]), units(i["xa_w_o_2"][0])
    up = i["ffn_w_up_2"][0].reshape(D, 2, FF // NCOL, NCOL).transpose(0, 2, 1, 3).reshape(D, 2 * FF)
    out["w_ffn_up"] = units(up)
    out["w_ffn_down"] = units(i["ffn_w_down_2"][0])
    return out


def kernel(**inputs):
    import concourse.bacc as bacc
    from concourse.bass_utils import run_bass_kernel_spmd

    laid = lay_out({k: np.asarray(v) for k, v in inputs.items()})
    nc = bacc.Bacc("TRN2", target_bir_lowering=False, num_devices=1)
    t = {}
    for name, a in laid.items():
        t[name] = nc.dram_tensor(f"in_{name}", a.shape, mybir.dt.from_np(a.dtype), kind="ExternalInput").ap()
    t["out"] = nc.dram_tensor("out_y", (P, DC, T), F32, kind="ExternalOutput").ap()
    t["mem_k"] = nc.dram_tensor("mem_k", (P, DC * T), F32).ap()
    t["mem_v"] = nc.dram_tensor("mem_v", (P, 2 * D), F32).ap()
    build(nc, t)
    r = run_bass_kernel_spmd(nc, [{f"in_{k}": v for k, v in laid.items()}], core_ids=[0])
    y = r.results[0]["out_y"]
    return np.ascontiguousarray(y.transpose(2, 1, 0)).reshape(1, T, D)
```
